# Optimizing a Trainium2 kernel written in Bass

```python
import jax, jax.numpy as jnp
from jax import lax
import numpy as np

D_MODEL = 1024
BATCH = 1
SEQ = 512
DEPTH = 2

CHUNK = 64
EPS = 1e-6
D_RNN = 1536
RNN_BLOCKS = 16
BLOCK_W = D_RNN // RNN_BLOCKS
CONV_WIDTH = 4
LRU_C = 8.0
HEAD_DIM = 64
N_Q_HEADS = D_MODEL // HEAD_DIM
N_KV_HEADS = 2
GROUP = N_Q_HEADS // N_KV_HEADS
WINDOW = 128
WINDOW_CHUNKS = WINDOW // CHUNK
KEYS_PER_BLOCK = WINDOW_CHUNKS * CHUNK
NEG_INF = -1e30
D_FF = ((8 * D_MODEL // 3 + 255) // 256) * 256

kernel_name = "yoco_rglru_swa_sink_alibi_sandwich"

def rmsnorm(x, g):
    xf = x.astype(jnp.float32)
    y = xf * lax.rsqrt(jnp.mean(xf * xf, axis=-1, keepdims=True) + EPS)
    return (y * g.astype(jnp.float32)).astype(x.dtype)

def swiglu(h, w_gu, w_down):
    u = h @ w_gu
    return (jax.nn.silu(u[..., :D_FF]) * u[..., D_FF:]) @ w_down

def rglru_mixer(h, w_in, conv_w, conv_b, w_rg, b_rg, w_ig, b_ig, lam, w_out):
    B, S, _ = h.shape
    u = h @ w_in
    gate_br, x_br = u[..., :D_RNN], u[..., D_RNN:]
    xp = jnp.pad(x_br, ((0, 0), (CONV_WIDTH - 1, 0), (0, 0)))
    xc = conv_b + xp[:, 0:S, :] * conv_w[0]
    for k in range(1, CONV_WIDTH):
        xc = xc + xp[:, k:k + S, :] * conv_w[k]
    xb = xc.reshape(B, S, RNN_BLOCKS, BLOCK_W)
    r = jax.nn.sigmoid(jnp.einsum('bsnc,ncd->bsnd', xb, w_rg) + b_rg).reshape(B, S, D_RNN)
    i = jax.nn.sigmoid(jnp.einsum('bsnc,ncd->bsnd', xb, w_ig) + b_ig).reshape(B, S, D_RNN)
    log_a = -LRU_C * r.astype(jnp.float32) * jax.nn.softplus(-lam.astype(jnp.float32))
    a = jnp.exp(log_a)
    b = jnp.sqrt(-jnp.expm1(2.0 * log_a)) * (i * xc).astype(jnp.float32)

    def step(carry, ab):
        at, bt = ab
        carry = at * carry + bt
        return carry, carry

    _, hs = lax.scan(step, jnp.zeros((B, D_RNN), jnp.float32),
                     (jnp.swapaxes(a, 0, 1), jnp.swapaxes(b, 0, 1)))
    y = jnp.swapaxes(hs, 0, 1).astype(h.dtype) * jax.nn.gelu(gate_br)
    return y @ w_out

def window_blocks(t, nc):
    tp = jnp.pad(t, ((0, 0), (WINDOW_CHUNKS - 1, 0), (0, 0), (0, 0), (0, 0)))
    return jnp.concatenate([tp[:, j:j + nc] for j in range(WINDOW_CHUNKS)], axis=2)

def swa_sink_attention(hn, w_q, sinks, w_o, k, v):
    B, S, _ = hn.shape
    nc = S // CHUNK
    q = (hn @ w_q).reshape(B, nc, CHUNK, N_KV_HEADS, GROUP, HEAD_DIM)
    kw = window_blocks(k.reshape(B, nc, CHUNK, N_KV_HEADS, HEAD_DIM), nc)
    vw = window_blocks(v.reshape(B, nc, CHUNK, N_KV_HEADS, HEAD_DIM), nc)
    s = jnp.einsum('bcqkgd,bcwkd->bckgqw', q, kw).astype(jnp.float32) * (HEAD_DIM ** -0.5)
    rel = (jnp.arange(CHUNK)[:, None] - jnp.arange(KEYS_PER_BLOCK)[None, :]
           + (WINDOW_CHUNKS - 1) * CHUNK)
    dist = jnp.abs(rel).astype(jnp.float32)
    slopes = jnp.exp2(-8.0 * jnp.arange(1, N_Q_HEADS + 1, dtype=jnp.float32) / N_Q_HEADS)
    alibi = -slopes.reshape(N_KV_HEADS, GROUP)[:, :, None, None] * dist
    key_chunk = (jnp.arange(nc)[:, None] - (WINDOW_CHUNKS - 1)
                 + (jnp.arange(KEYS_PER_BLOCK) // CHUNK)[None, :])
    valid = (key_chunk >= 0)[None, :, None, None, None, :]
    s = jnp.where(valid, s + alibi[None, None], NEG_INF)
    sink = sinks.astype(jnp.float32).reshape(N_KV_HEADS, GROUP)[None, None, :, :, None, None]
    m = jnp.maximum(jnp.max(s, axis=-1, keepdims=True), sink)
    p = jnp.exp(s - m)
    p = p / (jnp.sum(p, axis=-1, keepdims=True) + jnp.exp(sink - m))
    o = jnp.einsum('bckgqw,bcwkd->bcqkgd', p.astype(vw.dtype), vw)
    return o.reshape(B, S, N_Q_HEADS * HEAD_DIM) @ w_o

def setup_inputs(seed: int = 0) -> dict:
    key = jax.random.key(seed)
    ks = jax.random.split(key, 24)
    n_a = DEPTH // 2
    n_b = DEPTH - n_a
    f32 = jnp.float32
    nrm = lambda k, shape, fan: jax.random.normal(k, shape, f32) * fan ** -0.5
    gain = lambda k, shape: 1.0 + 0.05 * jax.random.normal(k, shape, f32)
    a0 = jax.random.uniform(ks[9], (n_a, D_RNN), f32, 0.9, 0.999)
    sig = a0 ** (1.0 / LRU_C)
    return {
        "x": jax.random.normal(ks[0], (BATCH, SEQ, D_MODEL), f32),
        "a_w_in": nrm(ks[1], (n_a, D_MODEL, 2 * D_RNN), D_MODEL),
        "a_conv_w": nrm(ks[2], (n_a, CONV_WIDTH, D_RNN), CONV_WIDTH),
        "a_conv_b": 0.01 * jax.random.normal(ks[3], (n_a, D_RNN), f32),
        "a_w_rg": nrm(ks[4], (n_a, RNN_BLOCKS, BLOCK_W, BLOCK_W), BLOCK_W),
        "a_b_rg": 0.01 * jax.random.normal(ks[5], (n_a, RNN_BLOCKS, BLOCK_W), f32),
        "a_w_ig": nrm(ks[6], (n_a, RNN_BLOCKS, BLOCK_W, BLOCK_W), BLOCK_W),
        "a_b_ig": 0.01 * jax.random.normal(ks[7], (n_a, RNN_BLOCKS, BLOCK_W), f32),
        "a_lam": jnp.log(sig / (1.0 - sig)),
        "a_w_out": nrm(ks[8], (n_a, D_RNN, D_MODEL), D_RNN),
        "kv_norm": gain(ks[10], (D_MODEL,)),
        "w_kv": nrm(ks[11], (D_MODEL, 2 * N_KV_HEADS * HEAD_DIM), D_MODEL),
        "b_w_q": nrm(ks[12], (n_b, D_MODEL, N_Q_HEADS * HEAD_DIM), D_MODEL),
        "b_sinks": jax.random.normal(ks[13], (n_b, N_Q_HEADS), f32),
        "b_w_o": nrm(ks[14], (n_b, N_Q_HEADS * HEAD_DIM, D_MODEL), N_Q_HEADS * HEAD_DIM),
        "ffn_w_gu": nrm(ks[15], (DEPTH, D_MODEL, 2 * D_FF), D_MODEL),
        "ffn_w_down": nrm(ks[16], (DEPTH, D_FF, D_MODEL), D_FF),
        "mix_pre": gain(ks[17], (DEPTH, D_MODEL)),
        "mix_post": gain(ks[18], (DEPTH, D_MODEL)),
        "ffn_pre": gain(ks[19], (DEPTH, D_MODEL)),
        "ffn_post": gain(ks[20], (DEPTH, D_MODEL)),
    }

def reference(x, a_w_in, a_conv_w, a_conv_b, a_w_rg, a_b_rg, a_w_ig, a_b_ig, a_lam, a_w_out,
              kv_norm, w_kv, b_w_q, b_sinks, b_w_o, ffn_w_gu, ffn_w_down,
              mix_pre, mix_post, ffn_pre, ffn_post):
    B, S, _ = x.shape
    n_a = DEPTH // 2
    h = x
    k = v = None
    for l in range(DEPTH):
        hn = rmsnorm(h, mix_pre[l])
        if l < n_a:
            mix = rglru_mixer(hn, a_w_in[l], a_conv_w[l], a_conv_b[l], a_w_rg[l], a_b_rg[l],
                              a_w_ig[l], a_b_ig[l], a_lam[l], a_w_out[l])
        else:
            if l == n_a:
                kv = rmsnorm(h, kv_norm) @ w_kv
                k = kv[..., :N_KV_HEADS * HEAD_DIM].reshape(B, S, N_KV_HEADS, HEAD_DIM)
                v = kv[..., N_KV_HEADS * HEAD_DIM:].reshape(B, S, N_KV_HEADS, HEAD_DIM)
            j = l - n_a
            mix = swa_sink_attention(hn, b_w_q[j], b_sinks[j], b_w_o[j], k, v)
        h = h + rmsnorm(mix, mix_post[l])
        f = swiglu(rmsnorm(h, ffn_pre[l]), ffn_w_gu[l], ffn_w_down[l])
        h = h + rmsnorm(f, ffn_post[l])
    return h


_drawn_inputs = setup_inputs


def setup_inputs(seed=0):
    import zlib

    import numpy as np

    out = dict(_drawn_inputs(seed))
    spreads = {}
    factors = {'a_b_rg': 23.658, 'a_b_ig': 8.0}
    for name, (base, spread) in spreads.items():
        noise = np.random.default_rng([zlib.crc32(name.encode()), seed]).standard_normal(out[name].shape)
        drawn = base * np.exp(spread * noise) if base else spread * noise
        out[name] = __import__('jax').numpy.asarray(drawn.astype(out[name].dtype))
    for name, factor in factors.items():
        out[name] = (out[name] * factor).astype(out[name].dtype)
    return out
```

```python
import concourse.bass as bass
from concourse import mybir
from contextlib import ExitStack

F32 = mybir.dt.float32
F32R = mybir.dt.float32r
I32 = mybir.dt.int32
ALU = mybir.AluOpType
ACT = mybir.ActivationFunctionType
AX = mybir.AxisListType

P = 128
D, S, R, FF = 1024, 512, 1536, 2816
DC, RC, FC = D // P, R // P, FF // P
TC = S // P
BW = 96
HD, HEADS, CHUNK = 64, 16, 64
EPS = 1e-6
MASKED = 1e33
W_COLS = 1024
CREDIT = 8

T_IN = 0
T_OUT = T_IN + 32
T_GU = [T_OUT + 16, 0]
T_DN = [T_GU[0] + 44, 0]
T_KV = T_DN[0] + 32
T_Q = T_KV + 4
T_O = T_Q + 8
T_GU[1] = T_O + 8
T_DN[1] = T_GU[1] + 44
DN_K = [6, 5, 6, 5]
DN_AT = [0, 6, 11, 17]
RI_AT = [0, 256, 640 - 128]
RI_PAIRS = [[0, 1], [0, 1, 2], [1, 2]]
RI_COLS = 896
IN_RAW = [0, 1, 2, 3, None, None, 0, 1]

PREP = {"mix": 0, "ffn0": 1, "kv": 2, "q": 3, "ffn1": 4}
SQS = {"mix": 0, "ffn0": 1, "kv": 2, "ffn1": 3}
RES = {"ffn0": 0, "kv": 1, "ffn1": 2, "out": 3}
BLOCK_NORM = {"post_mix0": 0, "post_ffn0": 1, "post_mix1": 2, "post_ffn1": 3}
NORM = {"mix": 0, "post_mix0": 1, "ffn0": 2, "post_ffn0": 3, "kv": 4, "post_mix1": 5, "ffn1": 6, "post_ffn1": 7}
OUTS = {"mix0": 0, "ffn0": 1, "mix1": 2, "ffn1": 3}

G_MIX_PRE, G_MIX_POST, G_FFN_PRE, G_FFN_POST, G_KV, G_ROWS = 0, 16, 32, 48, 64, 72
R_CONV_W, R_CONV_B, R_BRG, R_BIG, R_LAM, R_ROWS = 0, 48, 60, 72, 84, 96


class Count:

    def __init__(self, sem):
        self.sem, self.n, self.shift = sem, 0, 0

    def inc(self, ins):
        ins.then_inc(self.sem, 1)
        self.n += 1
        return self.n + self.shift


def repeat(eng, times, count, per_turn, body):
    if times <= 0:
        return
    start = count.n
    with eng.Fori(0, times) as i:
        count.shift = i * per_turn
        body(i)
        assert count.n - start == per_turn, (count.n - start, per_turn)
    count.n, count.shift = start + times * per_turn, 0


def trunk(nc, x, a_w_in, a_conv_w, a_conv_b, a_w_rg, a_b_rg, a_w_ig, a_b_ig, a_lam, a_w_out,
          kv_norm, w_kv, b_w_q, b_sinks, b_w_o, ffn_w_gu, ffn_w_down,
          mix_pre, mix_post, ffn_pre, ffn_post, out):
    at = {"top": (nc.sbuf_base + 63) // 64 * 64}

    def sb(name, shape, dt=F32, offset=None):
        n = 4
        for d in shape[1:]:
            n *= d
        if offset is None:
            offset = at["top"]
            at["top"] += (n + 31) // 32 * 32
        at[name] = offset
        return nc.alloc_sbuf_tensor_at(name, shape, dt, offset=offset)

    h = sb("h", [P, DC, S])
    x_hi = sb("x_hi", [P, DC, S], F32R)
    x_lo = sb("x_lo", [P, DC, S], F32R)
    mix = sb("mix", [P, DC, S], F32, at["x_hi"])
    raw = sb("raw", [P, 4, W_COLS])
    w_hi = sb("w_hi", [P, 4, W_COLS], F32R)
    w_lo = sb("w_lo", [P, 4, W_COLS], F32R)
    ident = sb("ident", [P, P])
    ones = sb("ones", [P, P])
    eps = sb("eps", [P, 1])
    g_rows = sb("g_rows", [P, P])
    r_rows = sb("r_rows", [P, P])
    gains = sb("gains", [P, G_ROWS])
    rnn = sb("rnn", [P, R_ROWS])
    half_b = sb("half_b", [P, 2 * RC])
    sp2 = sb("sp2", [P, RC])
    sp_t = sb("sp_t", [P, 4, RC])
    dist_i = sb("dist_i", [P, 3 * CHUNK], I32)
    dist = sb("dist", [P, 3 * CHUNK])
    slopes = sb("slopes", [P, HEADS])
    sinks_in = sb("sinks_in", [P, HEADS])
    sinks = sb("sinks", [P, DC, TC, 2])
    rstd = sb("rstd", [P, S])
    scratch = sb("scratch", [P, 4, S])
    std, sq, sq_sum = scratch[:, 0, :], scratch[:, 1:3, :], scratch[:, 3, :]
    U = at["top"]

    y_hi = sb("y_hi", [P, RC, S], F32R)
    y_lo = sb("y_lo", [P, RC, S], F32R)
    x_tok = sb("x_tok", [P, TC, D], F32, at["y_lo"])
    ri_raw = sb("ri_raw", [P, 2, RI_COLS])
    xp = sb("xp", [P, S + 4])
    xc = sb("xc", [P, 3, S])
    xc_hi = sb("xc_hi", [P, 3, S], F32R)
    xc_lo = sb("xc_lo", [P, 3, S], F32R)
    gate = sb("gate", [P, 3, S])
    t_i = sb("t_i", [P, 3, S])
    t_u = sb("t_u", [P, 3, S])
    root = scratch[:, 0:3, :]
    decay = sb("decay", [P, S])
    state = scratch[:, 3, :]
    end_a = at["top"]

    at["top"] = U
    hid_hi = sb("hid_hi", [P, FC, S], F32R)
    hid_lo = sb("hid_lo", [P, FC, S], F32R)
    end_f = at["top"]

    at["top"] = U
    o_hi = sb("o_hi", [P, DC, S], F32R)
    o_lo = sb("o_lo", [P, DC, S], F32R)
    xkv_hi = sb("xkv_hi", [P, DC, S], F32R, at["o_hi"])
    xkv_lo = sb("xkv_lo", [P, DC, S], F32R, at["o_lo"])
    q = sb("q", [P, DC, S])
    q_hi = sb("q_hi", [P, S], F32R)
    q_lo = sb("q_lo", [P, S], F32R)
    kv = sb("kv", [P, 2, S])
    k_hi = sb("k_hi", [P, S], F32R)
    k_lo = sb("k_lo", [P, S], F32R)
    v_hi = sb("v_hi", [P, TC, P], F32R)
    v_lo = sb("v_lo", [P, TC, P], F32R)
    va_hi = sb("va_hi", [P, TC, P], F32R)
    va_lo = sb("va_lo", [P, TC, P], F32R)
    s_sb = sb("s_sb", [P, 2, TC, 2, 3 * CHUNK])
    p_hi = sb("p_hi", [P, 2, 4 * P], F32R)
    p_lo = sb("p_lo", [P, 2, 4 * P], F32R)
    sm = sb("sm", [P, 2, 6, 2 * TC])
    end_b = at["top"]
    o_tok = sb("o_tok", [P, DC, S], F32, U)
    assert max(end_a, end_f, end_b) <= nc.sbuf_usable_end, (end_a, end_f, end_b, nc.sbuf_usable_end)

    win_v = a_w_in[0].rearrange("(k p) (g m c) -> p k g m c", p=P, g=2, c=P)
    wout_v = a_w_out[0].rearrange("(k p) n -> p k n", p=P)
    gu_v = [ffn_w_gu[f].rearrange("(k p) (u n) -> p k u n", p=P, u=2) for f in range(2)]
    dn_v = [ffn_w_down[f].rearrange("(k p) n -> p k n", p=P) for f in range(2)]
    kv_v = w_kv.rearrange("(k p) (u n) -> p k u n", p=P, u=2)
    q_v = b_w_q[0].rearrange("(k p) (g n) -> p k g n", p=P, g=2)
    o_v = b_w_o[0].rearrange("(g c d) n -> g d c n", g=2, d=HD)
    rg_v = [w[0].rearrange("(g b) c d -> c b g d", b=4) for w in (a_w_rg, a_w_ig)]
    ri_parts = [(0, 0, 96, 0, 0), (1, 0, 32, 0, 96), (1, 32, 64, 1, 0), (2, 0, 64, 1, 64), (2, 64, 32, 2, 0),
                (3, 0, 96, 2, 32)]

    with ExitStack() as ctx:
        banks = [ctx.enter_context(nc.psum_tensor(f"bank{b}", [P, S], F32)) for b in range(6)]
        o_ps = ctx.enter_context(nc.psum_tensor("o_ps", [P, TC, 2, P], F32))
        stat = o_ps[:, 2:4, :, :].rearrange("p j g n -> p (j g n)")

        def sem(name):
            return ctx.enter_context(nc.semaphore(name))

        x_landed = [sem(f"x_landed{c}") for c in range(TC)]
        params_landed = sem("params_landed")
        raw_landed = [sem(f"raw_landed{s}") for s in range(4)]
        ri_landed = [sem(f"ri_landed{s}") for s in range(2)]
        out_stored = sem("out_stored")
        consts_ready = sem("consts_ready")
        zero_ready = sem("zero_ready")
        pool_steps = sem("pool_steps")
        params_ready = sem("params_ready")
        rows_ready = sem("rows_ready")
        lam_exp = sem("lam_exp")
        lam_abs = sem("lam_abs")
        w_hi_ready = sem("w_hi_ready")
        w_lo_ready = sem("w_lo_ready")
        tiles_done = sem("tiles_done")
        xt_ready = sem("xt_ready")
        h_copied = sem("h_copied")
        sq_ready = sem("sq_ready")
        sq_used = sem("sq_used")
        stat_ready = sem("stat_ready")
        std_ready = sem("std_ready")
        rstd_ready = sem("rstd_ready")
        h_ready = sem("h_ready")
        xhi_ready = sem("xhi_ready")
        x_ready = sem("x_ready")
        xp_ready = sem("xp_ready")
        tap_ready = sem("tap_ready")
        conv_ready = sem("conv_ready")
        xchi_ready = sem("xchi_ready")
        xc_ready = sem("xc_ready")
        ri_free = sem("ri_free")
        act_steps = sem("act_steps")
        roots_ready = sem("roots_ready")
        gate_ready = sem("gate_ready")
        gelu_ready = sem("gelu_ready")
        y_ready = sem("y_ready")
        yhi_ready = sem("yhi_ready")
        ylo_ready = sem("ylo_ready")
        gu_free = sem("gu_free")
        g_ready = sem("g_ready")
        silu_ready = sem("silu_ready")
        hid_ready = sem("hid_ready")
        hidhi_ready = sem("hidhi_ready")
        hidlo_ready = sem("hidlo_ready")
        mix_free = sem("mix_free")
        sum_ready = sem("sum_ready")
        dve_steps = sem("dve_steps")
        kv_read = sem("kv_read")
        khi_ready = sem("khi_ready")
        v_turned = sem("v_turned")
        vhi_ready = sem("vhi_ready")
        v_ready = sem("v_ready")
        q_free = sem("q_free")
        qhi_ready = sem("qhi_ready")
        qlo_ready = sem("qlo_ready")
        s_ready = sem("s_ready")
        s_free = sem("s_free")
        max_ready = sem("max_ready")
        p_exp = sem("p_exp")
        p_ready = sem("p_ready")
        pt_ready = sem("pt_ready")
        phi_ready = sem("phi_ready")
        plo_ready = sem("plo_ready")
        o_ready = sem("o_ready")
        ohi_ready = sem("ohi_ready")
        olo_ready = sem("olo_ready")
        ot_ready = sem("ot_ready")
        otok_ready = sem("otok_ready")

        block = ctx.enter_context(nc.Block())

        @block.sync
        def _(sp):
            uses = [0, 0, 0, 0]

            def load(t, slot, lag, src, cols, part=(0, P)):
                sp.lower_ap_dma(src)
                sp.wait_ge(w_lo_ready, CREDIT + t - lag + 1)
                dst = raw[part[0]:part[1], slot, 0:cols]
                return sp.dma_start(dst.rearrange("p (k n) -> p k n", n=P), src)

            for c in range(TC):
                sp.dma_start(x_tok[:, c, :], x[0, c * P:(c + 1) * P, :]).then_inc(x_landed[c], 16)
            for row, v in ((G_MIX_PRE, mix_pre), (G_MIX_POST, mix_post), (G_FFN_PRE, ffn_pre), (G_FFN_POST, ffn_post)):
                sp.dma_start(g_rows[row:row + 16, :], v.rearrange("l (c p) -> (l c) p", p=P)).then_inc(params_landed, 16)
            sp.dma_start(g_rows[G_KV:G_ROWS, :], kv_norm.rearrange("(c p) -> c p", p=P)).then_inc(params_landed, 16)
            sp.dma_start(r_rows[0:48, :], a_conv_w[0].rearrange("w (c p) -> (w c) p", p=P)).then_inc(params_landed, 16)
            for row, v in ((R_CONV_B, a_conv_b[0]), (R_BRG, a_b_rg[0].rearrange("n c -> (n c)")),
                           (R_BIG, a_b_ig[0].rearrange("n c -> (n c)")), (R_LAM, a_lam[0])):
                sp.dma_start(r_rows[row:row + 12, :], v.rearrange("(c p) -> c p", p=P)).then_inc(params_landed, 16)
            sp.dma_start(sinks_in[:, :], b_sinks[0:1, :].broadcast_to([P, HEADS])).then_inc(params_landed, 16)
            sp.wait_ge(zero_ready, 1)

            def group(g):
                t = T_IN + 8 * g
                lags = [2, 2, 6, 8 - 0, None, None, 6, 6]
                for p in range(8):
                    if IN_RAW[p] is None:
                        blocks = [rg_v[p - 4][r0:r0 + n, b, bass.ds(g, 1), :].rearrange("c o d -> c (o d)")
                                  for b, r0, n, k, p0 in ri_parts]
                        sp.lower_ap_dma(blocks[0])
                        sp.wait_ge(w_lo_ready, CREDIT + t + p - 8 + 1)
                        for (b, r0, n, k, p0), src in zip(ri_parts, blocks):
                            lo = RI_AT[k] + BW * b
                            sp.dma_start(ri_raw[p0:p0 + n, p - 4, lo:lo + BW], src).then_inc(ri_landed[p - 4], 16)
                    else:
                        half, m = (1, 3 * g + p) if p < 3 else (0, 3 * g + (0, 0, 0, 0, 0, 0, 1, 2)[p])
                        src = win_v[:, :, half, bass.ds(m, 1), :].rearrange("p k o c -> p k (o c)")
                        load(t + p, IN_RAW[p], lags[p], src, W_COLS).then_inc(raw_landed[IN_RAW[p]], 16)

            with sp.Fori(0, 4) as g:
                group(g)

            with sp.Fori(0, 4) as i:
                for s in range(4):
                    m, half = 2 * i + s // 2, s % 2
                    load(T_OUT + 4 * i + s, s, 2 if s < 2 else 4, wout_v[:, 6 * half:6 * half + 6, bass.ds(P * m, P)],
                         6 * P).then_inc(raw_landed[s], 16)

            def ffn(f):
                with sp.Fori(0, FC // 2) as i:
                    for s in range(4):
                        m, up = 2 * i + s // 2, s % 2
                        load(T_GU[f] + 4 * i + s, s, 4, gu_v[f][:, :, up, bass.ds(P * m, P)],
                             W_COLS).then_inc(raw_landed[s], 16)
                with sp.Fori(0, DC) as m:
                    for s in range(4):
                        load(T_DN[f] + 4 * m + s, s, 4, dn_v[f][:, DN_AT[s]:DN_AT[s] + DN_K[s], bass.ds(P * m, P)],
                             DN_K[s] * P).then_inc(raw_landed[s], 16)

            ffn(0)
            for s in range(4):
                load(T_KV + s, s, 4, kv_v[:, 4 * (s // 2):4 * (s // 2) + 4, s % 2, :], 4 * P).then_inc(raw_landed[s], 16)
            with sp.Fori(0, 2) as i:
                for s in range(4):
                    m = 4 * i + s
                    halves = [q_v[:, :, g, bass.ds(HD * m, HD)] for g in range(2)]
                    sp.lower_ap_dma(halves[0])
                    sp.wait_ge(w_lo_ready, CREDIT + T_Q + m - 4 + 1)
                    for g in range(2):
                        sp.dma_start(raw[:, s, :].rearrange("p (k n) -> p k n", n=P)[:, :, HD * g:HD * g + HD],
                                     halves[g]).then_inc(raw_landed[s], 16)
            with sp.Fori(0, 2) as i:
                for s in range(4):
                    m = 4 * i + s
                    halves = [o_v[g, :, :, bass.ds(P * m, P)] for g in range(2)]
                    sp.lower_ap_dma(halves[0])
                    sp.wait_ge(w_lo_ready, CREDIT + T_O + m - 4 + 1)
                    for g in range(2):
                        sp.dma_start(raw[HD * g:HD * g + HD, s, :].rearrange("p (k n) -> p k n", n=P),
                                     halves[g]).then_inc(raw_landed[s], 16)
            ffn(1)
            for k in range(DC):
                sp.wait_ge(otok_ready, k + 1)
                sp.dma_start(out[0].rearrange("(c p) n -> p c n", p=P)[:, :, k * P:(k + 1) * P],
                             o_tok[:, k, :].rearrange("p (c n) -> p c n", n=P)).then_inc(out_stored, 16)
            sp.wait_ge(out_stored, 16 * DC)

        @block.gpsimd
        def _(pool):
            steps = Count(pool_steps)

            def then(ins):
                pool.wait_ge(pool_steps, steps.inc(ins))

            nc.gpsimd.memset(ri_raw[:, :, :], 0.0).then_inc(zero_ready, 1)
            then(nc.gpsimd.memset(ident[:, :], 0.0))
            then(nc.gpsimd.affine_select(out=ident[:, :], in_=ident[:, :], compare_op=ALU.not_equal, fill=1.0, base=0,
                                         pattern=[[-1, P]], channel_multiplier=1))
            nc.gpsimd.memset(ones[:, :], 1.0)
            nc.gpsimd.memset(eps[:, :], EPS)
            for n in range(HEADS):
                nc.gpsimd.memset(slopes[:, n:n + 1], -(2.0 ** (-8.0 * (n + 1) / HEADS)))
            nc.gpsimd.memset(xp[:, 0:4], 0.0)
            nc.gpsimd.iota(dist_i[:, :], pattern=[[-1, 3 * CHUNK]], base=CHUNK, channel_multiplier=1)\
                .then_inc(consts_ready, 1)

        @block.scalar
        def _(act):
            steps = Count(act_steps)
            landed = [0, 0, 0, 0]

            def split_hi(t, slot, raw_slot, count, cols):
                act.wait_ge(raw_landed[raw_slot], 16 * count)
                act.wait_ge(tiles_done, CREDIT + t - 4 + 1)
                nc.scalar.copy(w_hi[:, slot, 0:cols], raw[:, raw_slot, 0:cols]).then_inc(w_hi_ready, 1)

            def split_ri(t, g, slot, which):
                act.wait_ge(ri_landed[which], 96 * (g + 1))
                act.wait_ge(tiles_done, CREDIT + t - 4 + 1)
                nc.scalar.copy(w_hi[:, slot, 0:RI_COLS], ri_raw[:, which, :]).then_inc(w_hi_ready, 1)

            def prep(k, stage, gain_col, dst_hi, squares=True):
                nc.scalar.mul(dst_hi[:, k, :], h[:, k, :], gains[:, gain_col + k:gain_col + k + 1]).then_inc(xhi_ready, 1)
                if squares:
                    n = DC * SQS[stage] + k
                    if n >= 2:
                        act.wait_ge(sq_used, n - 1)
                    nc.scalar.activation(sq[:, k % 2, :], h[:, k, :], ACT.Square).then_inc(sq_ready, 1)

            def root_of_mean(norm):
                if norm in SQS:
                    act.wait_ge(sq_used, DC * (SQS[norm] + 1))
                else:
                    act.wait_ge(stat_ready, BLOCK_NORM[norm] + 1)
                nc.scalar.activation(std, stat, ACT.Sqrt, bias=eps[:, 0:1], scale=1.0 / D).then_inc(std_ready, 1)

            act.sem_inc(ri_free, 3)
            act.sem_inc(mix_free, 2)

            act.wait_ge(lam_abs, 1)
            nc.scalar.activation(sp_t[:, 1, :], sp_t[:, 0, :], ACT.Exp, scale=-1.0).then_inc(lam_exp, 1)

            act.wait_ge(params_ready, 1)
            for k in range(DC):
                act.wait_ge(xt_ready, k + 1)
                nc.scalar.copy(h[:, k, :], banks[4 + k % 2][:, :]).then_inc(h_copied, 1)
                act.wait_ge(h_copied, k + 1)
                nc.scalar.mul(x_hi[:, k, :], h[:, k, :], gains[:, G_MIX_PRE + k:G_MIX_PRE + k + 1]).then_inc(xhi_ready, 1)
                if k >= 2:
                    act.wait_ge(sq_used, k - 1)
                nc.scalar.activation(sq[:, k % 2, :], h[:, k, :], ACT.Square).then_inc(sq_ready, 1)
                if k == 0:
                    for s in range(3):
                        split_hi(s, s, s, 1, W_COLS)
            root_of_mean("mix")

            def group(g, last=False):
                t = T_IN + 8 * g
                fills = [(0, 2 * g + 1), (1, 2 * g + 1), (2, g + 1), (3, g + 1), None, None, (0, 2 * g + 2), (1, 2 * g + 2)]

                def ahead(p):
                    p += 3
                    if p in (4, 5):
                        split_ri(t + p, g, p % 4, p - 4)
                    elif p < 8:
                        split_hi(t + p, p % 4, *fills[p], W_COLS)
                    elif not last:
                        split_hi(t + p, p % 4, p - 8, (2 * g + 3) if p < 10 else g + 2, W_COLS)
                    else:
                        split_hi(t + p, p % 4, p - 8, 9 if p < 10 else 5, 6 * P)

                for p in range(3):
                    ahead(p)
                    c = 3 * g + p
                    act.wait_ge(xp_ready, c + 1)
                    nc.scalar.activation(xc[:, p, :], xp[:, 1:S + 1], ACT.Identity, bias=rnn[:, bass.ds(R_CONV_B + c, 1)],
                                         scale=rnn[:, bass.ds(R_CONV_W + c, 1)]).then_inc(tap_ready, 1)
                    act.wait_ge(conv_ready, c + 1)
                    nc.scalar.copy(xc_hi[:, p, :], xc[:, p, :]).then_inc(xchi_ready, 1)

                def gelu(j):
                    act.wait_ge(gate_ready, 3 + 3 * g + j + 1)
                    nc.scalar.activation(gate[:, j, :], gate[:, j, :], ACT.Gelu_apprx_tanh).then_inc(gelu_ready, 1)

                ahead(3)
                gelu(0)
                ahead(4)
                act.wait_ge(tiles_done, CREDIT + t + 4 + 1)
                for j in range(3):
                    ins = nc.scalar.activation(t_u[:, j, :], banks[3 + j][:, :], ACT.Tanh,
                                               bias=half_b[:, bass.ds(3 * g + j, 1)], scale=0.5)
                    ins.then_inc(ri_free, 1)
                ahead(5)
                act.wait_ge(tiles_done, CREDIT + t + 5 + 1)
                for j in range(3):
                    nc.scalar.activation(t_i[:, j, :], banks[3 + j][:, :], ACT.Tanh,
                                         bias=half_b[:, bass.ds(RC + 3 * g + j, 1)], scale=0.5).then_inc(ri_free, 1)
                act.wait_ge(ri_free, 3 + 6 * g + 6)
                for j in range(3):
                    steps_at = steps.inc(nc.scalar.activation(
                        t_u[:, j, :], t_u[:, j, :], ACT.Tanh, bias=sp2[:, bass.ds(3 * g + j, 1)],
                        scale=sp2[:, bass.ds(3 * g + j, 1)]))
                act.wait_ge(act_steps, steps_at)
                nc.scalar.activation(root, t_u[:, :, :], ACT.Sqrt).then_inc(roots_ready, 1)
                ahead(6)
                gelu(1)

                def y_high(j):
                    c = 3 * g + j
                    act.wait_ge(y_ready, c + 1)
                    nc.scalar.copy(y_hi[:, bass.ds(c, 1), :].rearrange("p o n -> p (o n)"), gate[:, j, :])\
                        .then_inc(yhi_ready, 1)

                y_high(0)
                ahead(7)
                gelu(2)
                y_high(1)
                y_high(2)

            repeat(act, 3, steps, 3, group)
            group(3, last=True)

            def out_chunk(stage, m, par, gain_col, t):
                n = DC * OUTS[stage] + m
                act.wait_ge(tiles_done, CREDIT + t + 1)
                nc.scalar.mul(mix[:, bass.ds(m, 1), :].rearrange("p o n -> p (o n)"), banks[4 + par][:, :],
                              gains[:, bass.ds(gain_col + m, 1)])
                act.wait_ge(sum_ready, n + 1)
                nc.scalar.activation(sq[:, 0, :], banks[4 + par][:, :], ACT.Square).then_inc(mix_free, 1)

            def w_out(i, last=False):
                for s in range(4):
                    if s == 0:
                        split_hi(T_OUT + 4 * i + 3, 3, 3, 5 + i, 6 * P)
                    elif not last:
                        split_hi(T_OUT + 4 * i + 3 + s, s - 1, s - 1, (9 if s < 3 else 5) + i + 1, 6 * P)
                    else:
                        split_hi(T_OUT + 4 * i + 3 + s, s - 1, s - 1, (9 if s < 3 else 5) + i + 1, W_COLS)
                    if s % 2:
                        out_chunk("mix0", 2 * i + s // 2, s // 2, G_MIX_POST, T_OUT + 4 * i + s)

            repeat(act, 3, steps, 0, w_out)
            w_out(3, last=True)
            base = [8 + 4, 8 + 4, 4 + 4, 4 + 4]

            def residual(stage, norm, gain_col, dst_hi=None):
                root_of_mean(norm)
                for k in range(DC):
                    if stage == "out":
                        continue
                    act.wait_ge(h_ready, DC * RES[stage] + k + 1)
                    prep(k, stage, gain_col, dst_hi)

            def ffn(f, base):
                residual(f"ffn{f}", f"post_mix{f}", G_FFN_PRE + DC * f, x_hi)
                root_of_mean(f"ffn{f}")

                def pairs(i, last=False):
                    for a in range(2):
                        n = FC * f + 2 * i + a
                        for s in (2 * a, 2 * a + 1):
                            slot = (s + 3) % 4
                            cols = DN_K[slot] * P if last and s > 0 else W_COLS
                            split_hi(T_GU[f] + 4 * i + s + 3, slot, slot, base[slot] + i + (2 if s > 0 else 1), cols)
                        act.wait_ge(g_ready, n + 1)
                        nc.scalar.activation(scratch[:, a, :], scratch[:, a, :], ACT.Silu).then_inc(silu_ready, 1)
                        act.wait_ge(hid_ready, n + 1)
                        nc.scalar.copy(hid_hi[:, bass.ds(2 * i + a, 1), :].rearrange("p o n -> p (o n)"),
                                       scratch[:, 2 + a, :]).then_inc(hidhi_ready, 1)

                repeat(act, FC // 2 - 1, steps, 0, pairs)
                pairs(FC // 2 - 1, last=True)
                b2 = [n + FC // 2 for n in base]

                def down(m, par, last=False):
                    for s in range(4):
                        slot = (s + 3) % 4
                        cols = DN_K[slot] * P
                        if last and s > 0:
                            cols = 4 * P if f == 0 else 0
                        if cols:
                            split_hi(T_DN[f] + 4 * m + s + 3, slot, slot, b2[slot] + m + (2 if s > 0 else 1), cols)
                    out_chunk(f"ffn{f}", m, par, G_FFN_POST + DC * f, T_DN[f] + 4 * m + 3)

                def two(i, last=False):
                    down(2 * i, 0)
                    down(2 * i + 1, 1, last)

                repeat(act, DC // 2 - 1, steps, 0, two)
                two(DC // 2 - 1, last=True)
                return [n + DC for n in b2]

            base = ffn(0, base)

            split_hi(T_KV + 3, 3, 3, base[3] + 1, 4 * P)
            residual("kv", "post_ffn0", G_KV, xkv_hi)
            root_of_mean("kv")
            for s in range(2):
                split_hi(T_Q + s, s, s, base[s] + 3, W_COLS)
            base = [n + 1 for n in base]
            for k in range(DC):
                nc.scalar.mul(x_hi[:, k, :], h[:, k, :], gains[:, G_MIX_PRE + DC + k:G_MIX_PRE + DC + k + 1])\
                    .then_inc(xhi_ready, 1)
            act.wait_ge(kv_read, 1)
            nc.scalar.copy(k_hi[:, :], kv[:, 0, :]).then_inc(khi_ready, 1)
            act.wait_ge(v_turned, 1)
            nc.scalar.copy(v_hi[:, :, :], banks[3][:, :].rearrange("p (j n) -> p j n", n=P)).then_inc(vhi_ready, 1)
            nc.scalar.copy(va_hi[0:HD, 1:TC, :], banks[2][0:HD, P:S].rearrange("p (j n) -> p j n", n=P))\
                .then_inc(vhi_ready, 1)

            def q_tiles(i, last=False):
                for s in range(4):
                    slot = (s + 2) % 4
                    t = T_Q + 4 * i + s + 2
                    split_hi(t, slot, slot, base[slot] + 2 * i + (4 if s >= 2 else 2), W_COLS)

            repeat(act, 1, steps, 0, q_tiles)
            q_tiles(1, last=True)
            base = [n + 4 for n in base]

            def softmax(m, b):
                act.wait_ge(max_ready, m + 1)
                for j in range(TC):
                    c0 = CHUNK if j == 0 else 0
                    for g in range(2):
                        nc.scalar.activation(s_sb[:, b, j, g, c0:], s_sb[:, b, j, g, c0:], ACT.Exp,
                                             bias=sm[:, b, 1, 2 * j + g:2 * j + g + 1],
                                             accum_out=sm[:, b, 3, 2 * j + g:2 * j + g + 1])
                nc.scalar.activation(sm[:, b, 4, :], sm[:, b, 2, :], ACT.Exp).then_inc(p_exp, 1)

            def q_high(m):
                if not isinstance(m, int) or m > 0:
                    act.wait_ge(s_ready, TC * m)
                nc.scalar.copy(q_hi[:, :], q[:, bass.ds(m, 1), :].rearrange("p o n -> p (o n)")).then_inc(qhi_ready, 1)

            def turned(m, b):
                for j in range(TC):
                    n = TC * m + j
                    act.wait_ge(pt_ready, n + 1)
                    if j > 0:
                        nc.scalar.copy(p_hi[0:HD, j % 2, 2 * P:], banks[4 + j % 2][0:HD, 2 * P:])
                    nc.scalar.copy(p_hi[:, j % 2, 0:2 * P], banks[4 + j % 2][:, 0:2 * P]).then_inc(phi_ready, 1)
                act.wait_ge(o_ready, m + 1)
                for g in range(2):
                    ins = nc.scalar.copy(
                        o_hi[HD * g:HD * g + HD, bass.ds(m, 1), :].rearrange("p o (j n) -> p (o j) n", n=P),
                        o_ps[HD * g:HD * g + HD, :, g, :])
                ins.then_inc(ohi_ready, 1)

            act.wait_ge(q_free, 2 + DC)
            q_high(0)

            def heads(i, last=False):
                for b in range(2):
                    m = 2 * i + b
                    softmax(m, b)
                    if not (last and b == 1):
                        q_high(m + 1)
                    turned(m, b)

            repeat(act, DC // 2 - 1, steps, 0, heads)
            heads(DC // 2 - 1, last=True)

            def w_o(i, last=False):
                for s in range(4):
                    slot = (s + 2) % 4
                    t = T_O + 4 * i + s + 2
                    if last and s >= 2:
                        split_hi(t, slot, slot, base[slot] + 4 + 1, W_COLS)
                    else:
                        split_hi(t, slot, slot, base[slot] + 2 * i + (4 if s >= 2 else 2), W_COLS)
                    out_chunk("mix1", 4 * i + s, s % 2, G_MIX_POST + DC, T_O + 4 * i + s)

            repeat(act, 1, steps, 0, w_o)
            w_o(1, last=True)
            base = [n + 4 for n in base]
            split_hi(T_GU[1] + 2, 2, 2, base[2] + 1, W_COLS)
            base = ffn(1, base)
            residual("out", "post_ffn1", None)
            for k in range(DC):
                act.wait_ge(ot_ready, k + 1)
                nc.scalar.copy(o_tok[:, k, :], banks[4 + k % 2][:, :]).then_inc(otok_ready, 1)

        @block.vector
        def _(dve):
            v = nc.vector
            steps = Count(dve_steps)

            def then(ins):
                dve.wait_ge(dve_steps, steps.inc(ins))

            def split_lo(t, slot, raw_slot, cols):
                dve.wait_ge(w_hi_ready, t + 1)
                v.tensor_tensor(w_lo[:, slot, 0:cols], raw[:, raw_slot, 0:cols], w_hi[:, slot, 0:cols].bitcast(F32),
                                ALU.subtract).then_inc(w_lo_ready, 1)

            def split_lo_ri(t, slot, which):
                dve.wait_ge(w_hi_ready, t + 1)
                v.tensor_tensor(w_lo[:, slot, 0:RI_COLS], ri_raw[:, which, :], w_hi[:, slot, 0:RI_COLS].bitcast(F32),
                                ALU.subtract).then_inc(w_lo_ready, 1)

            def input_lo(k, stage, gain_col, hi, lo):
                dve.wait_ge(xhi_ready, DC * PREP[stage] + k + 1)
                v.scalar_tensor_tensor(out=lo[:, k, :], in0=h[:, k, :], scalar=gains[:, gain_col + k:gain_col + k + 1],
                                       in1=hi[:, k, :].bitcast(F32), op0=ALU.mult, op1=ALU.subtract).then_inc(x_ready, 1)

            def reciprocal_of_root(norm):
                dve.wait_ge(std_ready, NORM[norm] + 1)
                v.reciprocal(rstd[:, :], std).then_inc(rstd_ready, 1)
                dve.wait_ge(rstd_ready, NORM[norm] + 1)

            dve.sem_inc(w_lo_ready, CREDIT)
            dve.sem_inc(gate_ready, 3)
            dve.sem_inc(gu_free, 2)
            dve.sem_inc(q_free, 2)
            dve.sem_inc(s_free, 2)
            dve.sem_inc(sum_ready, 1)

            dve.wait_ge(rows_ready, 2)
            v.tensor_copy(gains[:, :], banks[0][:, 0:G_ROWS])
            then(v.tensor_copy(rnn[:, :], banks[1][:, 0:R_ROWS]))
            lam = rnn[:, R_LAM:R_LAM + RC]
            v.tensor_scalar(half_b[:, :], rnn[:, R_BRG:R_BRG + 2 * RC], 0.5, None, ALU.mult)
            v.tensor_scalar(sp_t[:, 3, :], lam, -1.0, 0.0, ALU.mult, ALU.max)
            then(v.tensor_scalar(sp_t[:, 2, :], lam, -1.0, None, ALU.mult))
            v.tensor_tensor(sp_t[:, 0, :], sp_t[:, 2, :], lam, ALU.max).then_inc(lam_abs, 1)
            dve.wait_ge(lam_exp, 1)
            then(v.tensor_scalar(sp_t[:, 0, :], sp_t[:, 1, :], 2.0, None, ALU.add))
            then(v.reciprocal(sp_t[:, 0, :], sp_t[:, 0, :]))
            then(v.tensor_tensor(sp_t[:, 1, :], sp_t[:, 1, :], sp_t[:, 0, :], ALU.mult))
            then(v.tensor_tensor(sp_t[:, 2, :], sp_t[:, 1, :], sp_t[:, 1, :], ALU.mult))
            then(v.tensor_scalar(sp_t[:, 0, :], sp_t[:, 2, :], 1.0 / 15, 1.0 / 13, ALU.mult, ALU.add))
            for n in (11, 9, 7, 5, 3, 1):
                then(v.tensor_tensor(sp_t[:, 0, :], sp_t[:, 0, :], sp_t[:, 2, :], ALU.mult))
                then(v.tensor_scalar(sp_t[:, 0, :], sp_t[:, 0, :], 1.0 / n, None, ALU.add))
            then(v.tensor_tensor(sp_t[:, 0, :], sp_t[:, 0, :], sp_t[:, 1, :], ALU.mult))
            then(v.tensor_scalar(sp_t[:, 0, :], sp_t[:, 0, :], 2.0, None, ALU.mult))
            then(v.tensor_tensor(sp_t[:, 0, :], sp_t[:, 0, :], sp_t[:, 3, :], ALU.add))
            v.tensor_scalar(sp2[:, :], sp_t[:, 0, :], 2.0, None, ALU.mult)
            dve.wait_ge(params_landed, 16 * 11)
            for j in range(TC):
                v.tensor_copy(sinks[:, :, j, :], sinks_in[:, :].rearrange("p (g m) -> p m g", g=2))
            dve.wait_ge(consts_ready, 1)
            then(v.tensor_copy(dist[:, :], dist_i[:, :]))
            then(v.tensor_scalar(rstd[:, 0:3 * CHUNK], dist[:, :], -1.0, None, ALU.mult))
            then(v.tensor_tensor(dist[:, :], dist[:, :], rstd[:, 0:3 * CHUNK], ALU.max))
            v.memset(dist[0:CHUNK, 2 * CHUNK:3 * CHUNK], MASKED)
            v.memset(dist[CHUNK:P, 0:CHUNK], MASKED).then_inc(params_ready, 1)
            dve.wait_ge(params_ready, 1)

            for k in range(DC):
                input_lo(k, "mix", G_MIX_PRE, x_hi, x_lo)
                if k == 0:
                    for s in range(3):
                        split_lo(s, s, s, W_COLS)
            reciprocal_of_root("mix")

            def group(g, last=False):
                t = T_IN + 8 * g

                def ahead(p):
                    p += 3
                    if p in (4, 5):
                        split_lo_ri(t + p, p % 4, p - 4)
                    elif p < 8:
                        split_lo(t + p, p % 4, IN_RAW[p], W_COLS)
                    else:
                        split_lo(t + p, p % 4, p - 8, 6 * P if last else W_COLS)

                def xc_low(j):
                    dve.wait_ge(xchi_ready, 3 * g + j + 1)
                    v.tensor_tensor(xc_lo[:, j, :], xc[:, j, :], xc_hi[:, j, :].bitcast(F32), ALU.subtract)\
                        .then_inc(xc_ready, 1)

                for j in range(3):
                    c = 3 * g + j
                    dve.wait_ge(tiles_done, CREDIT + t + j + 1)
                    v.tensor_tensor(xp[:, 4:S + 4], banks[j][:, :], rstd[:, :], ALU.mult).then_inc(xp_ready, 1)
                    ahead(j)
                    dve.wait_ge(tap_ready, c + 1)
                    for k in range(1, 4):
                        ins = v.scalar_tensor_tensor(out=xc[:, j, :], in0=xp[:, 1 + k:S + 1 + k],
                                                     scalar=rnn[:, bass.ds(R_CONV_W + RC * k + c, 1)], in1=xc[:, j, :],
                                                     op0=ALU.mult, op1=ALU.add)
                        if k < 3:
                            then(ins)
                        else:
                            ins.then_inc(conv_ready, 1)
                    xc_low(j)

                def gate_in(j):
                    dve.wait_ge(tiles_done, CREDIT + t + (3, 6, 7)[j] + 1)
                    v.tensor_tensor(gate[:, j, :], banks[j][:, :], rstd[:, :], ALU.mult).then_inc(gate_ready, 1)

                def recurrence(j):
                    c = 3 * g + j
                    then(v.tensor_scalar(decay[:, :], t_u[:, j, :], 1.0, None, ALU.add))
                    then(v.reciprocal(decay[:, :], decay[:, :]))
                    v.tensor_tensor(root[:, j, :], root[:, j, :], decay[:, :], ALU.mult)
                    then(v.scalar_tensor_tensor(out=t_i[:, j, :], in0=t_i[:, j, :], scalar=1.0, in1=xc[:, j, :],
                                                op0=ALU.add, op1=ALU.mult))
                    v.tensor_scalar(decay[:, :], decay[:, :], 2.0, -1.0, ALU.mult, ALU.add)
                    then(v.tensor_tensor(root[:, j, :], root[:, j, :], t_i[:, j, :], ALU.mult))
                    then(v.tensor_tensor_scan(state, decay[:, :], root[:, j, :], 0.0, ALU.mult, ALU.add))
                    dve.wait_ge(gelu_ready, c + 1)
                    v.tensor_tensor(gate[:, j, :], state, gate[:, j, :], ALU.mult).then_inc(y_ready, 1)

                def y_low(j):
                    c = 3 * g + j
                    dve.wait_ge(yhi_ready, c + 1)
                    v.tensor_tensor(y_lo[:, bass.ds(c, 1), :].rearrange("p o n -> p (o n)"), gate[:, j, :],
                                    y_hi[:, bass.ds(c, 1), :].rearrange("p o n -> p (o n)").bitcast(F32),
                                    ALU.subtract).then_inc(ylo_ready, 1)

                ahead(3)
                gate_in(0)
                ahead(4)
                ahead(5)
                dve.wait_ge(roots_ready, g + 1)
                recurrence(0)
                ahead(6)
                gate_in(1)
                y_low(0)
                recurrence(1)
                ahead(7)
                gate_in(2)
                y_low(1)
                recurrence(2)
                y_low(2)

            repeat(dve, 3, steps, 3 * 2 + 3 * 5, group)
            group(3, last=True)

            def sum_squares(stage, m):
                n = DC * OUTS[stage] + m
                dve.wait_ge(mix_free, 2 + n + 1)
                v.tensor_tensor(sq_sum, sq_sum, sq[:, 0, :], ALU.add).then_inc(sum_ready, 1)

            def clear_sum():
                then(v.memset(sq_sum, 0.0))

            clear_sum()

            def w_out(i, last=False):
                for s in range(4):
                    split_lo(T_OUT + 4 * i + 3 + s, (s + 3) % 4, (s + 3) % 4, W_COLS if last and s > 0 else 6 * P)
                    if s % 2:
                        sum_squares("mix0", 2 * i + s // 2)

            repeat(dve, 3, steps, 0, w_out)
            w_out(3, last=True)

            def residual(stage, norm, gain_col=None, hi=None, lo=None):
                reciprocal_of_root(norm)
                for k in range(DC):
                    then(v.tensor_tensor(mix[:, k, :], mix[:, k, :], rstd[:, :], ALU.mult))
                    v.tensor_tensor(h[:, k, :], h[:, k, :], mix[:, k, :], ALU.add).then_inc(h_ready, 1)
                    if hi is not None and k > 0:
                        input_lo(k - 1, stage, gain_col, hi, lo)
                if hi is not None:
                    input_lo(DC - 1, stage, gain_col, hi, lo)

            def ffn(f):
                residual(f"ffn{f}", f"post_mix{f}", G_FFN_PRE + DC * f, x_hi, x_lo)
                reciprocal_of_root(f"ffn{f}")

                def pairs(i, last=False):
                    for a in range(2):
                        n = FC * f + 2 * i + a
                        for s in (2 * a, 2 * a + 1):
                            slot = (s + 3) % 4
                            split_lo(T_GU[f] + 4 * i + s + 3, slot, slot, DN_K[slot] * P if last and s > 0 else W_COLS)
                        dve.wait_ge(tiles_done, CREDIT + T_GU[f] + 4 * i + 2 * a + 1 + 1)
                        v.tensor_tensor(scratch[:, a, :], banks[2 * a][:, :], rstd[:, :], ALU.mult).then_inc(g_ready, 1)
                        v.tensor_tensor(scratch[:, 2 + a, :], banks[2 * a + 1][:, :], rstd[:, :], ALU.mult)\
                            .then_inc(gu_free, 1)
                        dve.wait_ge(gu_free, 2 + n + 1)
                        dve.wait_ge(silu_ready, n + 1)
                        v.tensor_tensor(scratch[:, 2 + a, :], scratch[:, a, :], scratch[:, 2 + a, :], ALU.mult)\
                            .then_inc(hid_ready, 1)
                        dve.wait_ge(hidhi_ready, n + 1)
                        at_m = bass.ds(2 * i + a, 1)
                        v.tensor_tensor(hid_lo[:, at_m, :].rearrange("p o n -> p (o n)"), scratch[:, 2 + a, :],
                                        hid_hi[:, at_m, :].rearrange("p o n -> p (o n)").bitcast(F32),
                                        ALU.subtract).then_inc(hidlo_ready, 1)

                repeat(dve, FC // 2 - 1, steps, 0, pairs)
                pairs(FC // 2 - 1, last=True)
                dve.wait_ge(hidlo_ready, FC * (f + 1))
                clear_sum()

                def down(m, last=False):
                    for s in range(4):
                        slot = (s + 3) % 4
                        cols = DN_K[slot] * P
                        if last and s > 0:
                            cols = 4 * P if f == 0 else 0
                        if cols:
                            split_lo(T_DN[f] + 4 * m + s + 3, slot, slot, cols)
                    sum_squares(f"ffn{f}", m)

                repeat(dve, DC - 1, steps, 0, down)
                down(DC - 1, last=True)

            ffn(0)

            split_lo(T_KV + 3, 3, 3, 4 * P)
            residual("kv", "post_ffn0", G_KV, xkv_hi, xkv_lo)
            reciprocal_of_root("kv")
            split_lo(T_Q, 0, 0, W_COLS)
            split_lo(T_Q + 1, 1, 1, W_COLS)
            for k in range(DC):
                input_lo(k, "q", G_MIX_PRE + DC, x_hi, x_lo)
            dve.wait_ge(tiles_done, CREDIT + T_KV + 3 + 1)
            v.tensor_tensor(kv[:, 1, :], banks[1][:, :], rstd[:, :], ALU.mult)
            v.tensor_tensor(kv[:, 0, :], banks[0][:, :], rstd[:, :], ALU.mult).then_inc(kv_read, 1)
            dve.wait_ge(khi_ready, 1)
            v.tensor_tensor(k_lo[:, :], kv[:, 0, :], k_hi[:, :].bitcast(F32), ALU.subtract)
            dve.wait_ge(vhi_ready, 2)
            v.tensor_tensor(v_lo[:, :, :], banks[3][:, :].rearrange("p (j n) -> p j n", n=P), v_hi[:, :, :].bitcast(F32),
                            ALU.subtract)
            v.tensor_tensor(va_lo[0:HD, 1:TC, :], banks[2][0:HD, P:S].rearrange("p (j n) -> p j n", n=P),
                            va_hi[0:HD, 1:TC, :].bitcast(F32), ALU.subtract).then_inc(v_ready, 1)
            for b in range(2):
                then(v.memset(s_sb[:, b, 0, :, 0:CHUNK], -1e30))

            def q_tiles(i, last=False):
                for s in range(4):
                    slot = (s + 2) % 4
                    split_lo(T_Q + 4 * i + s + 2, slot, slot, W_COLS)
                    m = 4 * i + s
                    dve.wait_ge(tiles_done, CREDIT + T_Q + m + 1)
                    v.scalar_tensor_tensor(out=q[:, bass.ds(m, 1), :].rearrange("p o n -> p (o n)"),
                                           in0=banks[s % 2][:, :], scalar=HD ** -0.5, in1=rstd[:, :], op0=ALU.mult,
                                           op1=ALU.mult).then_inc(q_free, 1)

            repeat(dve, 1, steps, 0, q_tiles)
            q_tiles(1, last=True)

            def q_low(m):
                dve.wait_ge(qhi_ready, m + 1)
                v.tensor_tensor(q_lo[:, :], q[:, bass.ds(m, 1), :].rearrange("p o n -> p (o n)"),
                                q_hi[:, :].bitcast(F32), ALU.subtract).then_inc(qlo_ready, 1)

            def row_max(m, b):
                for j in range(TC):
                    n = TC * m + j
                    dve.wait_ge(s_ready, n + 1)
                    c0 = CHUNK if j == 0 else 0
                    for g in range(2):
                        ins = v.scalar_tensor_tensor(out=s_sb[:, b, j, g, c0:], in0=dist[:, c0:],
                                                     scalar=slopes[:, bass.ds(m + DC * g, 1)],
                                                     in1=banks[2 * g + j % 2][:, c0:3 * CHUNK], op0=ALU.mult, op1=ALU.add)
                    ins.then_inc(s_free, 1)
                dve.wait_ge(s_free, 2 + TC * (m + 1))
                then(v.tensor_reduce(sm[:, b, 0, :], s_sb[:, b, :, :, :].rearrange("p j g w -> p (j g) w"), AX.X, ALU.max))
                sink = sinks[:, bass.ds(m, 1), :, :].rearrange("p o j g -> p (o j g)")
                then(v.tensor_tensor(sm[:, b, 0, :], sm[:, b, 0, :], sink, ALU.max))
                v.tensor_scalar(sm[:, b, 1, :], sm[:, b, 0, :], -1.0, None, ALU.mult)
                v.tensor_tensor(sm[:, b, 2, :], sink, sm[:, b, 0, :], ALU.subtract).then_inc(max_ready, 1)
                dve.wait_ge(max_ready, m + 1)

            def normalise(m, b):
                dve.wait_ge(p_exp, m + 1)
                then(v.tensor_tensor(sm[:, b, 5, :], sm[:, b, 3, :], sm[:, b, 4, :], ALU.add))
                then(v.reciprocal(sm[:, b, 5, :], sm[:, b, 5, :]))
                for j in range(TC):
                    c0 = CHUNK if j == 0 else 0
                    for g in range(2):
                        ins = v.tensor_scalar(s_sb[:, b, j, g, c0:], s_sb[:, b, j, g, c0:],
                                              sm[:, b, 5, 2 * j + g:2 * j + g + 1], None, ALU.mult)
                ins.then_inc(p_ready, 1)

            def turned(m, b):
                for j in range(TC):
                    dve.wait_ge(phi_ready, TC * m + j + 1)
                    if j > 0:
                        v.tensor_tensor(p_lo[0:HD, j % 2, 2 * P:], banks[4 + j % 2][0:HD, 2 * P:],
                                        p_hi[0:HD, j % 2, 2 * P:].bitcast(F32), ALU.subtract)
                    v.tensor_tensor(p_lo[:, j % 2, 0:2 * P], banks[4 + j % 2][:, 0:2 * P],
                                    p_hi[:, j % 2, 0:2 * P].bitcast(F32), ALU.subtract).then_inc(plo_ready, 1)
                dve.wait_ge(ohi_ready, m + 1)
                for g in range(2):
                    lo = o_lo[HD * g:HD * g + HD, bass.ds(m, 1), :].rearrange("p o (j n) -> p (o j) n", n=P)
                    hi = o_hi[HD * g:HD * g + HD, bass.ds(m, 1), :].rearrange("p o (j n) -> p (o j) n", n=P)
                    ins = v.tensor_tensor(lo, o_ps[HD * g:HD * g + HD, :, g, :], hi.bitcast(F32), ALU.subtract)
                ins.then_inc(olo_ready, 1)

            q_low(0)
            row_max(0, 0)
            q_low(1)

            def heads_ahead(i, last=False):
                for b in range(2):
                    m = 2 * i + b
                    normalise(m, b)
                    if not (last and b == 1):
                        row_max(m + 1, 1 - b)
                    turned(m, b)
                    if not last:
                        q_low(m + 2)

            repeat(dve, DC // 2 - 1, steps, 8, heads_ahead)
            heads_ahead(DC // 2 - 1, last=True)
            clear_sum()

            def w_o(i, last=False):
                for s in range(4):
                    slot = (s + 2) % 4
                    split_lo(T_O + 4 * i + s + 2, slot, slot, W_COLS)
                    sum_squares("mix1", 4 * i + s)

            repeat(dve, 1, steps, 0, w_o)
            w_o(1, last=True)
            split_lo(T_GU[1] + 2, 2, 2, W_COLS)
            ffn(1)
            residual("out", "post_ffn1")

        @block.tensor
        def _(pe):
            def products(ps, hi_w, lo_w, hi_x, lo_x, first, final):
                nc.tensor.matmul(ps, hi_w, hi_x, start=first, stop=False)
                nc.tensor.matmul(ps, hi_w, lo_x, start=False, stop=False)
                return nc.tensor.matmul(ps, lo_w, hi_x, start=False, stop=final)

            def tile(ps, slot, at, k, first, final, hi=x_hi, lo=x_lo):
                cols = slice(at * P, at * P + P)
                return products(ps, w_hi[:, slot, cols], w_lo[:, slot, cols], hi[:, k, :], lo[:, k, :], first, final)

            def tile_ready(t):
                pe.wait_ge(w_lo_ready, CREDIT + t + 1)

            def sum_chunk(stage, k):
                pe.wait_ge(sq_ready, DC * SQS[stage] + k + 1)
                ins = nc.tensor.matmul(stat, ones[:, :], sq[:, k % 2, :], start=(k == 0), stop=(k == DC - 1))
                ins.then_inc(sq_used, 1)

            pe.sem_inc(tiles_done, CREDIT)
            pe.wait_ge(consts_ready, 1)
            pe.wait_ge(params_landed, 16 * 11)
            nc.tensor.transpose(banks[0][:, 0:G_ROWS], g_rows[0:G_ROWS, :], ident[0:G_ROWS, 0:G_ROWS]).then_inc(rows_ready, 1)
            nc.tensor.transpose(banks[1][:, 0:R_ROWS], r_rows[0:R_ROWS, :], ident[0:R_ROWS, 0:R_ROWS]).then_inc(rows_ready, 1)
            for c in range(TC):
                pe.wait_ge(x_landed[c], 16)

            def turn_x(k):
                if k >= 2:
                    pe.wait_ge(h_copied, k - 1)
                for c in range(TC):
                    ins = nc.tensor.transpose(banks[4 + k % 2][:, c * P:(c + 1) * P], x_tok[:, c, k * P:(k + 1) * P],
                                              ident[:, :])
                ins.then_inc(xt_ready, 1)

            def block_gates(g):
                for which in range(2):
                    t = T_IN + 8 * g + 4 + which
                    tile_ready(t)
                    if which == 0:
                        pe.wait_ge(xc_ready, 3 * g + 3)
                    for m in range(3):
                        pe.wait_ge(ri_free, 6 * g + 3 * which + m + 1)
                        ks = RI_PAIRS[m]
                        for k in ks:
                            cols = slice(RI_AT[k] + P * m, RI_AT[k] + P * m + P)
                            ins = products(banks[3 + m][:, :], w_hi[:, t_slot(4 + which), cols],
                                           w_lo[:, t_slot(4 + which), cols], xc_hi[:, k, :], xc_lo[:, k, :],
                                           k == ks[0], k == ks[-1])
                    ins.then_inc(tiles_done, 1)

            def t_slot(p):
                return p % 4

            def xg_tile(g, p, n, bank):
                tile_ready(T_IN + 8 * g + p)
                if n < 3:
                    pe.wait_ge(gate_ready, 3 * g + n + 1)
                else:
                    pe.wait_ge(xp_ready, 3 * g + n - 3 + 1)
                for k in range(DC):
                    ins = tile(banks[bank][:, :], t_slot(p), k, k, k == 0, k == DC - 1)
                ins.then_inc(tiles_done, 1)

            def rest_of_group(g):
                xg_tile(g, 3, 3, 0)
                block_gates(g)
                xg_tile(g, 6, 4, 1)
                xg_tile(g, 7, 5, 2)

            turn_x(0)
            turn_x(1)
            for k in range(DC):
                if k + 2 < DC:
                    turn_x(k + 2)
                pe.wait_ge(x_ready, k + 1)
                for p in range(3):
                    if k == 0:
                        tile_ready(p)
                    ins = tile(banks[p][:, :], p, k, k, k == 0, k == DC - 1)
                    if k == DC - 1:
                        ins.then_inc(tiles_done, 1)
                sum_chunk("mix", k)
            rest_of_group(0)

            with pe.Fori(0, 3) as i:
                g = i + 1
                for p in range(3):
                    xg_tile(g, p, p, p)
                rest_of_group(g)

            pe.wait_ge(ri_free, 3 + 24)

            def w_out(i, first=False):
                for s in range(4):
                    m = 2 * i + s // 2
                    tile_ready(T_OUT + 4 * i + s)
                    if s % 2 == 0:
                        pe.wait_ge(mix_free, m + 1)
                    for n in range(6):
                        k = 6 * (s % 2) + n
                        if first:
                            pe.wait_ge(ylo_ready, k + 1)
                        ins = tile(banks[4 + s // 2][:, :], s, n, k, k == 0, k == RC - 1, y_hi, y_lo)
                    ins.then_inc(tiles_done, 1)

            w_out(0, first=True)
            with pe.Fori(0, 3) as i:
                w_out(i + 1)

            def sum_block(norm, stage):
                pe.wait_ge(sum_ready, 1 + DC * (OUTS[stage] + 1))
                nc.tensor.matmul(stat, ones[:, :], sq_sum, start=True, stop=True).then_inc(stat_ready, 1)

            def ffn(f):
                sum_block(f"post_mix{f}", f"mix{f}")

                def pair(n, a, first=False):
                    pe.wait_ge(gu_free, FC * f + n + 1)
                    tile_ready(T_GU[f] + 2 * n)
                    tile_ready(T_GU[f] + 2 * n + 1)
                    for k in range(DC):
                        if first:
                            pe.wait_ge(x_ready, DC * PREP[f"ffn{f}"] + k + 1)
                        for u in range(2):
                            ins = tile(banks[2 * a + u][:, :], 2 * a + u, k, k, k == 0, k == DC - 1)
                            if k == DC - 1:
                                ins.then_inc(tiles_done, 1)
                        if first:
                            sum_chunk(f"ffn{f}", k)

                pair(0, 0, first=True)
                pair(1, 1)
                with pe.Fori(0, FC // 2 - 1) as i:
                    for a in range(2):
                        pair(2 * i + 2 + a, a)

                def down(m, par, first=False):
                    pe.wait_ge(mix_free, DC * OUTS[f"ffn{f}"] + m + 1)
                    for s in range(4):
                        tile_ready(T_DN[f] + 4 * m + s)
                        for n in range(DN_K[s]):
                            k = DN_AT[s] + n
                            if first:
                                pe.wait_ge(hidlo_ready, FC * f + k + 1)
                            ins = tile(banks[4 + par][:, :], s, n, k, k == 0, k == FC - 1, hid_hi, hid_lo)
                        ins.then_inc(tiles_done, 1)

                down(0, 0, first=True)
                down(1, 1)
                with pe.Fori(0, DC // 2 - 1) as i:
                    for a in range(2):
                        down(2 * i + 2 + a, a)

            ffn(0)

            sum_block("post_ffn0", "ffn0")
            for k in range(DC):
                pe.wait_ge(x_ready, DC * PREP["kv"] + k + 1)
                for u in range(2):
                    s = 2 * (k // 4) + u
                    if k % 4 == 0:
                        tile_ready(T_KV + s)
                    ins = tile(banks[u][:, :], s, k % 4, k, k == 0, k == DC - 1, xkv_hi, xkv_lo)
                    if k % 4 == 3:
                        ins.then_inc(tiles_done, 1)
                sum_chunk("kv", k)
            pe.wait_ge(kv_read, 1)
            for j in range(TC):
                ins = nc.tensor.transpose(banks[3][:, j * P:(j + 1) * P], kv[:, 1, j * P:(j + 1) * P], ident[:, :])
            for j in range(1, TC):
                ins = nc.tensor.transpose(banks[2][0:HD, j * P:(j + 1) * P], kv[:, 1, j * P - HD:j * P], ident[:, :])
            ins.then_inc(v_turned, 1)

            def q_chunk(m, s, first=False):
                tile_ready(T_Q + m)
                pe.wait_ge(q_free, m + 1)
                for k in range(DC):
                    if first:
                        pe.wait_ge(x_ready, DC * PREP["q"] + k + 1)
                    ins = tile(banks[s % 2][:, :], s, k, k, k == 0, k == DC - 1)
                ins.then_inc(tiles_done, 1)

            for s in range(4):
                q_chunk(s, s, first=(s == 0))
            with pe.Fori(0, 1) as i:
                for s in range(4):
                    q_chunk(4 * i + 4 + s, s)

            pe.wait_ge(v_ready, 1)
            pe.wait_ge(q_free, 2 + DC)

            def scores(m):
                pe.wait_ge(qlo_ready, m + 1)
                for j in range(TC):
                    pe.wait_ge(s_free, TC * m + j + 1)
                    c0 = CHUNK if j == 0 else 0
                    keys = slice(j * P - CHUNK + c0, j * P + P)
                    for g in range(2):
                        rows = slice(HD * g, HD * g + HD)
                        qs = slice(j * P, (j + 1) * P)
                        ins = products(banks[2 * g + j % 2][:, c0:3 * CHUNK], q_hi[rows, qs], q_lo[rows, qs],
                                       k_hi[rows, keys], k_lo[rows, keys], True, True)
                    ins.then_inc(s_ready, 1)

            def turn(m, b, j):
                n = TC * m + j
                if not isinstance(n, int) or n >= 2:
                    pe.wait_ge(plo_ready, n - 1)
                bank = banks[4 + j % 2]
                for g in range(2):
                    ins = nc.tensor.transpose(bank[:, g * P:(g + 1) * P], s_sb[:, b, j, g, CHUNK:3 * CHUNK], ident[:, :])
                if j > 0:
                    for g in range(2):
                        ins = nc.tensor.transpose(bank[0:HD, (2 + g) * P:(3 + g) * P], s_sb[:, b, j, g, 0:CHUNK],
                                                  ident[:, :])
                ins.then_inc(pt_ready, 1)

            def values(m, j):
                pe.wait_ge(plo_ready, TC * m + j + 1)
                o = o_ps[:, j, :, :].rearrange("p g n -> p (g n)")
                both = slice(0, 2 * P)
                ins = products(o, v_hi[:, j, :], v_lo[:, j, :], p_hi[:, j % 2, both], p_lo[:, j % 2, both], True, j == 0)
                if j > 0:
                    before = slice(2 * P, 4 * P)
                    ins = products(o, va_hi[0:HD, j, :], va_lo[0:HD, j, :], p_hi[0:HD, j % 2, before],
                                   p_lo[0:HD, j % 2, before], False, True)
                return ins

            scores(0)

            def heads(i, last=False):
                for b in range(2):
                    m = 2 * i + b
                    if not (last and b == 1):
                        scores(m + 1)
                    pe.wait_ge(p_ready, m + 1)
                    turn(m, b, 0)
                    turn(m, b, 1)
                    if not isinstance(m, int) or m > 0:
                        pe.wait_ge(olo_ready, m)
                    for j in range(TC):
                        ins = values(m, j)
                        if j + 2 < TC:
                            turn(m, b, j + 2)
                    ins.then_inc(o_ready, 1)

            heads(0)
            with pe.Fori(0, DC // 2 - 2) as i:
                heads(i + 1)
            heads(DC // 2 - 1, last=True)

            pe.wait_ge(olo_ready, DC)

            def w_o(m, s):
                tile_ready(T_O + m)
                pe.wait_ge(mix_free, DC * OUTS["mix1"] + m + 1)
                for k in range(DC):
                    ins = tile(banks[4 + s % 2][:, :], s, k, k, k == 0, k == DC - 1, o_hi, o_lo)
                ins.then_inc(tiles_done, 1)

            with pe.Fori(0, 2) as i:
                for s in range(4):
                    w_o(4 * i + s, s)
            ffn(1)

            sum_block("post_ffn1", "ffn1")
            for k in range(DC):
                pe.wait_ge(h_ready, DC * RES["out"] + k + 1)
                if k >= 2:
                    pe.wait_ge(otok_ready, k - 1)
                for c in range(TC):
                    ins = nc.tensor.transpose(banks[4 + k % 2][:, c * P:(c + 1) * P], h[:, k, c * P:(c + 1) * P],
                                              ident[:, :])
                ins.then_inc(ot_ready, 1)


_INS = ["x", "a_w_in", "a_conv_w", "a_conv_b", "a_w_rg", "a_b_rg", "a_w_ig", "a_b_ig", "a_lam", "a_w_out", "kv_norm",
        "w_kv", "b_w_q", "b_sinks", "b_w_o", "ffn_w_gu", "ffn_w_down", "mix_pre", "mix_post", "ffn_pre", "ffn_post"]


def kernel(**inputs):
    import numpy as np
    import concourse.bacc as bacc
    from concourse.bass_utils import run_bass_kernel_spmd

    nc = bacc.Bacc("TRN2", target_bir_lowering=False, num_devices=1)
    arrays, args = {}, []
    for name in _INS:
        a = np.ascontiguousarray(inputs[name])
        arrays[f"in_{name}"] = a
        args.append(nc.dram_tensor(f"in_{name}", a.shape, mybir.dt.from_np(a.dtype), kind="ExternalInput").ap())
    args.append(nc.dram_tensor("result", (1, S, D), F32, kind="ExternalOutput").ap())
    trunk(nc, *args)
    r = run_bass_kernel_spmd(nc, [arrays], core_ids=[0])
    return r.results[0]["result"]
```

```python
import concourse.bass as bass
from concourse import mybir
from contextlib import ExitStack

F32 = mybir.dt.float32
F32R = mybir.dt.float32r
I32 = mybir.dt.int32
ALU = mybir.AluOpType
ACT = mybir.ActivationFunctionType
AX = mybir.AxisListType

P = 128
D, S, R, FF = 1024, 512, 1536, 2816
DC, RC, FC = D // P, R // P, FF // P
TC = S // P
BW = 96
HD, HEADS, CHUNK = 64, 16, 64
EPS = 1e-6
MASKED = 1e33
W_COLS = 1024
CREDIT = 8

T_IN = 0
T_OUT = T_IN + 32
T_GU = [T_OUT + 16, 0]
T_DN = [T_GU[0] + 44, 0]
T_KV = T_DN[0] + 32
T_Q = T_KV + 4
T_O = T_Q + 8
T_GU[1] = T_O + 8
T_DN[1] = T_GU[1] + 44
DN_K = [6, 5, 6, 5]
DN_AT = [0, 6, 11, 17]
RI_AT = [0, 256, 640 - 128]
RI_PAIRS = [[0, 1], [0, 1, 2], [1, 2]]
RI_COLS = 896
IN_RAW = [0, 1, 2, 3, None, None, 0, 1]

PREP = {"mix": 0, "ffn0": 1, "kv": 2, "q": 3, "ffn1": 4}
SQS = {"mix": 0, "ffn0": 1, "kv": 2, "ffn1": 3}
RES = {"ffn0": 0, "kv": 1, "ffn1": 2, "out": 3}
BLOCK_NORM = {"post_mix0": 0, "post_ffn0": 1, "post_mix1": 2, "post_ffn1": 3}
NORM = {"mix": 0, "post_mix0": 1, "ffn0": 2, "post_ffn0": 3, "kv": 4, "post_mix1": 5, "ffn1": 6, "post_ffn1": 7}
OUTS = {"mix0": 0, "ffn0": 1, "mix1": 2, "ffn1": 3}

G_MIX_PRE, G_MIX_POST, G_FFN_PRE, G_FFN_POST, G_KV, G_ROWS = 0, 16, 32, 48, 64, 72
R_CONV_W, R_CONV_B, R_BRG, R_BIG, R_LAM, R_ROWS = 0, 48, 60, 72, 84, 96


PAIRS_H = HEADS // 2
STEPS = range(-1, PAIRS_H + 2)
Q_BANK = [4, 1] + [5] * 6
Q_PARTS = [range(0, 2), range(2, 4), range(4, 6), range(6, 8)]


def o_half(m, j):
    pair, half = (m - 2, 1) if j == 1 else (m - 1, 0) if j == 3 else (-1, 0)
    return (pair, half) if 0 <= pair < PAIRS_H else None


class Count:

    def __init__(self, sem):
        self.sem, self.n, self.shift = sem, 0, 0

    def inc(self, ins):
        ins.then_inc(self.sem, 1)
        self.n += 1
        return self.n + self.shift


def repeat(eng, times, count, per_turn, body):
    if times <= 0:
        return
    start = count.n
    with eng.Fori(0, times) as i:
        count.shift = i * per_turn
        body(i)
        assert count.n - start == per_turn, (count.n - start, per_turn)
    count.n, count.shift = start + times * per_turn, 0


def trunk(nc, x, a_w_in, a_conv_w, a_conv_b, a_w_rg, a_b_rg, a_w_ig, a_b_ig, a_lam, a_w_out,
          kv_norm, w_kv, b_w_q, b_sinks, b_w_o, ffn_w_gu, ffn_w_down,
          mix_pre, mix_post, ffn_pre, ffn_post, out):
    at = {"top": (nc.sbuf_base + 63) // 64 * 64}

    def sb(name, shape, dt=F32, offset=None):
        n = 4
        for d in shape[1:]:
            n *= d
        if offset is None:
            offset = at["top"]
            at["top"] += (n + 31) // 32 * 32
        at[name] = offset
        return nc.alloc_sbuf_tensor_at(name, shape, dt, offset=offset)

    h = sb("h", [P, DC, S])
    x_hi = sb("x_hi", [P, DC, S], F32R)
    x_lo = sb("x_lo", [P, DC, S], F32R)
    mix = sb("mix", [P, DC, S], F32, at["x_hi"])
    raw = sb("raw", [P, 4, W_COLS])
    w_hi = sb("w_hi", [P, 4, W_COLS], F32R)
    w_lo = sb("w_lo", [P, 4, W_COLS], F32R)
    ident = sb("ident", [P, P])
    ones = sb("ones", [P, P])
    eps = sb("eps", [P, 1])
    g_rows = sb("g_rows", [P, P])
    r_rows = sb("r_rows", [P, P])
    gains = sb("gains", [P, G_ROWS])
    rnn = sb("rnn", [P, R_ROWS])
    half_b = sb("half_b", [P, 2 * RC])
    sp2 = sb("sp2", [P, RC])
    sp_t = sb("sp_t", [P, 4, RC])
    dist_i = sb("dist_i", [P, 3 * CHUNK], I32)
    dist = sb("dist", [P, 3 * CHUNK])
    slopes = sb("slopes", [P, HEADS])
    sinks_in = sb("sinks_in", [P, HEADS])
    sinks = sb("sinks", [P, DC, TC, 2])
    rstd = sb("rstd", [P, S])
    scratch = sb("scratch", [P, 4, S])
    std, sq, sq_sum = scratch[:, 0, :], scratch[:, 1:3, :], scratch[:, 3, :]
    U = at["top"]

    y_hi = sb("y_hi", [P, RC, S], F32R)
    y_lo = sb("y_lo", [P, RC, S], F32R)
    x_tok = sb("x_tok", [P, TC, D], F32, at["y_lo"])
    ri_raw = sb("ri_raw", [P, 2, RI_COLS])
    xp = sb("xp", [P, S + 4])
    xc = sb("xc", [P, 3, S])
    xc_hi = sb("xc_hi", [P, 3, S], F32R)
    xc_lo = sb("xc_lo", [P, 3, S], F32R)
    gate = sb("gate", [P, 3, S])
    t_i = sb("t_i", [P, 3, S])
    t_u = sb("t_u", [P, 3, S])
    root = scratch[:, 0:3, :]
    decay = sb("decay", [P, S])
    state = scratch[:, 3, :]
    end_a = at["top"]

    at["top"] = U
    hid_hi = sb("hid_hi", [P, FC, S], F32R)
    hid_lo = sb("hid_lo", [P, FC, S], F32R)
    end_f = at["top"]

    at["top"] = U
    o_hi = sb("o_hi", [P, DC, S], F32R)
    o_lo = sb("o_lo", [P, DC, S], F32R)
    xkv_hi = sb("xkv_hi", [P, DC, S], F32R, at["o_hi"])
    xkv_lo = sb("xkv_lo", [P, DC, S], F32R, at["o_lo"])
    q = sb("q", [P, 2, S])
    q_hi = sb("q_hi", [P, 2, S], F32R)
    q_lo = sb("q_lo", [P, 2, S], F32R)
    kv = sb("kv", [P, 2, S])
    k_hi = sb("k_hi", [P, S], F32R)
    k_lo = sb("k_lo", [P, S], F32R)
    v_hi = sb("v_hi", [P, TC, P], F32R)
    v_lo = sb("v_lo", [P, TC, P], F32R)
    va_hi = sb("va_hi", [P, TC, P], F32R)
    va_lo = sb("va_lo", [P, TC, P], F32R)
    s_sb = sb("s_sb", [P, 2, TC, 2, 3 * CHUNK])
    p_hi = sb("p_hi", [P, 2, 4 * P], F32R)
    p_lo = sb("p_lo", [P, 2, 4 * P], F32R)
    sm = sb("sm", [P, 2, 6, 2 * TC])
    end_b = at["top"]
    o_tok = sb("o_tok", [P, DC, S], F32, U)
    assert max(end_a, end_f, end_b) <= nc.sbuf_usable_end, (end_a, end_f, end_b, nc.sbuf_usable_end)

    win_v = a_w_in[0].rearrange("(k p) (g m c) -> p k g m c", p=P, g=2, c=P)
    wout_v = a_w_out[0].rearrange("(k p) n -> p k n", p=P)
    gu_v = [ffn_w_gu[f].rearrange("(k p) (u n) -> p k u n", p=P, u=2) for f in range(2)]
    dn_v = [ffn_w_down[f].rearrange("(k p) n -> p k n", p=P) for f in range(2)]
    kv_v = w_kv.rearrange("(k p) (u n) -> p k u n", p=P, u=2)
    q_v = b_w_q[0].rearrange("(k p) (g n) -> p k g n", p=P, g=2)
    o_v = b_w_o[0].rearrange("(g c d) n -> g d c n", g=2, d=HD)
    rg_v = [w[0].rearrange("(g b) c d -> c b g d", b=4) for w in (a_w_rg, a_w_ig)]
    ri_parts = [(0, 0, 96, 0, 0), (1, 0, 32, 0, 96), (1, 32, 64, 1, 0), (2, 0, 64, 1, 64), (2, 64, 32, 2, 0),
                (3, 0, 96, 2, 32)]

    with ExitStack() as ctx:
        banks = [ctx.enter_context(nc.psum_tensor(f"bank{b}", [P, S], F32)) for b in range(6)]
        o_ps = ctx.enter_context(nc.psum_tensor("o_ps", [P, TC, 2, P], F32))
        stat = o_ps[:, 2:4, :, :].rearrange("p j g n -> p (j g n)")

        def sem(name):
            return ctx.enter_context(nc.semaphore(name))

        x_landed = [sem(f"x_landed{c}") for c in range(TC)]
        params_landed = sem("params_landed")
        raw_landed = [sem(f"raw_landed{s}") for s in range(4)]
        ri_landed = [sem(f"ri_landed{s}") for s in range(2)]
        out_stored = sem("out_stored")
        consts_ready = sem("consts_ready")
        zero_ready = sem("zero_ready")
        pool_steps = sem("pool_steps")
        params_ready = sem("params_ready")
        rows_ready = sem("rows_ready")
        lam_exp = sem("lam_exp")
        lam_abs = sem("lam_abs")
        w_hi_ready = sem("w_hi_ready")
        w_lo_ready = sem("w_lo_ready")
        tiles_done = sem("tiles_done")
        xt_ready = sem("xt_ready")
        h_copied = sem("h_copied")
        sq_ready = sem("sq_ready")
        sq_used = sem("sq_used")
        stat_ready = sem("stat_ready")
        std_ready = sem("std_ready")
        rstd_ready = sem("rstd_ready")
        h_ready = sem("h_ready")
        xhi_ready = sem("xhi_ready")
        x_ready = sem("x_ready")
        xp_ready = sem("xp_ready")
        tap_ready = sem("tap_ready")
        conv_ready = sem("conv_ready")
        xchi_ready = sem("xchi_ready")
        xc_ready = sem("xc_ready")
        ri_free = sem("ri_free")
        act_steps = sem("act_steps")
        roots_ready = sem("roots_ready")
        gate_ready = sem("gate_ready")
        gelu_ready = sem("gelu_ready")
        y_ready = sem("y_ready")
        yhi_ready = sem("yhi_ready")
        ylo_ready = sem("ylo_ready")
        gu_free = sem("gu_free")
        g_ready = sem("g_ready")
        silu_ready = sem("silu_ready")
        hid_ready = sem("hid_ready")
        hidhi_ready = sem("hidhi_ready")
        hidlo_ready = sem("hidlo_ready")
        mix_free = sem("mix_free")
        sum_ready = sem("sum_ready")
        dve_steps = sem("dve_steps")
        kv_read = sem("kv_read")
        khi_ready = sem("khi_ready")
        v_turned = sem("v_turned")
        vhi_ready = sem("vhi_ready")
        v_ready = sem("v_ready")
        q_read = sem("q_read")
        qhi_ready = sem("qhi_ready")
        qlo_ready = sem("qlo_ready")
        s_ready = sem("s_ready")
        s_read = sem("s_read")
        max_ready = sem("max_ready")
        p_exp = sem("p_exp")
        den_ready = sem("den_ready")
        p0_ready = sem("p0_ready")
        p1_ready = sem("p1_ready")
        pt_ready = sem("pt_ready")
        phi_ready = sem("phi_ready")
        plo_ready = sem("plo_ready")
        o_ready = sem("o_ready")
        ohi_ready = sem("ohi_ready")
        olo_ready = sem("olo_ready")
        ot_ready = sem("ot_ready")
        otok_ready = sem("otok_ready")

        block = ctx.enter_context(nc.Block())

        @block.sync
        def _(sp):
            uses = [0, 0, 0, 0]

            def load(t, slot, lag, src, cols, part=(0, P)):
                sp.lower_ap_dma(src)
                sp.wait_ge(w_lo_ready, CREDIT + t - lag + 1)
                dst = raw[part[0]:part[1], slot, 0:cols]
                return sp.dma_start(dst.rearrange("p (k n) -> p k n", n=P), src)

            for c in range(TC):
                sp.dma_start(x_tok[:, c, :], x[0, c * P:(c + 1) * P, :]).then_inc(x_landed[c], 16)
            for row, v in ((G_MIX_PRE, mix_pre), (G_MIX_POST, mix_post), (G_FFN_PRE, ffn_pre), (G_FFN_POST, ffn_post)):
                sp.dma_start(g_rows[row:row + 16, :], v.rearrange("l (c p) -> (l c) p", p=P)).then_inc(params_landed, 16)
            sp.dma_start(g_rows[G_KV:G_ROWS, :], kv_norm.rearrange("(c p) -> c p", p=P)).then_inc(params_landed, 16)
            sp.dma_start(r_rows[0:48, :], a_conv_w[0].rearrange("w (c p) -> (w c) p", p=P)).then_inc(params_landed, 16)
            for row, v in ((R_CONV_B, a_conv_b[0]), (R_BRG, a_b_rg[0].rearrange("n c -> (n c)")),
                           (R_BIG, a_b_ig[0].rearrange("n c -> (n c)")), (R_LAM, a_lam[0])):
                sp.dma_start(r_rows[row:row + 12, :], v.rearrange("(c p) -> c p", p=P)).then_inc(params_landed, 16)
            sp.dma_start(sinks_in[:, :], b_sinks[0:1, :].broadcast_to([P, HEADS])).then_inc(params_landed, 16)
            sp.wait_ge(zero_ready, 1)

            def group(g):
                t = T_IN + 8 * g
                lags = [2, 2, 6, 8 - 0, None, None, 6, 6]
                for p in range(8):
                    if IN_RAW[p] is None:
                        blocks = [rg_v[p - 4][r0:r0 + n, b, bass.ds(g, 1), :].rearrange("c o d -> c (o d)")
                                  for b, r0, n, k, p0 in ri_parts]
                        sp.lower_ap_dma(blocks[0])
                        sp.wait_ge(w_lo_ready, CREDIT + t + p - 8 + 1)
                        for (b, r0, n, k, p0), src in zip(ri_parts, blocks):
                            lo = RI_AT[k] + BW * b
                            sp.dma_start(ri_raw[p0:p0 + n, p - 4, lo:lo + BW], src).then_inc(ri_landed[p - 4], 16)
                    else:
                        half, m = (1, 3 * g + p) if p < 3 else (0, 3 * g + (0, 0, 0, 0, 0, 0, 1, 2)[p])
                        src = win_v[:, :, half, bass.ds(m, 1), :].rearrange("p k o c -> p k (o c)")
                        load(t + p, IN_RAW[p], lags[p], src, W_COLS).then_inc(raw_landed[IN_RAW[p]], 16)

            with sp.Fori(0, 4) as g:
                group(g)

            with sp.Fori(0, 4) as i:
                for s in range(4):
                    m, half = 2 * i + s // 2, s % 2
                    load(T_OUT + 4 * i + s, s, 2 if s < 2 else 4, wout_v[:, 6 * half:6 * half + 6, bass.ds(P * m, P)],
                         6 * P).then_inc(raw_landed[s], 16)

            def ffn(f):
                with sp.Fori(0, FC // 2) as i:
                    for s in range(4):
                        m, up = 2 * i + s // 2, s % 2
                        load(T_GU[f] + 4 * i + s, s, 4, gu_v[f][:, :, up, bass.ds(P * m, P)],
                             W_COLS).then_inc(raw_landed[s], 16)
                with sp.Fori(0, DC) as m:
                    for s in range(4):
                        load(T_DN[f] + 4 * m + s, s, 4, dn_v[f][:, DN_AT[s]:DN_AT[s] + DN_K[s], bass.ds(P * m, P)],
                             DN_K[s] * P).then_inc(raw_landed[s], 16)

            ffn(0)
            for s in range(4):
                load(T_KV + s, s, 4, kv_v[:, 4 * (s // 2):4 * (s // 2) + 4, s % 2, :], 4 * P).then_inc(raw_landed[s], 16)
            with sp.Fori(0, 2) as i:
                for s in range(4):
                    m = 4 * i + s
                    halves = [q_v[:, :, g, bass.ds(HD * m, HD)] for g in range(2)]
                    sp.lower_ap_dma(halves[0])
                    sp.wait_ge(w_lo_ready, CREDIT + T_Q + m - 4 + 1)
                    for g in range(2):
                        sp.dma_start(raw[:, s, :].rearrange("p (k n) -> p k n", n=P)[:, :, HD * g:HD * g + HD],
                                     halves[g]).then_inc(raw_landed[s], 16)
            with sp.Fori(0, 2) as i:
                for s in range(4):
                    m = 4 * i + s
                    halves = [o_v[g, :, :, bass.ds(P * m, P)] for g in range(2)]
                    sp.lower_ap_dma(halves[0])
                    sp.wait_ge(w_lo_ready, CREDIT + T_O + m - 4 + 1)
                    for g in range(2):
                        sp.dma_start(raw[HD * g:HD * g + HD, s, :].rearrange("p (k n) -> p k n", n=P),
                                     halves[g]).then_inc(raw_landed[s], 16)
            ffn(1)
            for k in range(DC):
                sp.wait_ge(otok_ready, k + 1)
                sp.dma_start(out[0].rearrange("(c p) n -> p c n", p=P)[:, :, k * P:(k + 1) * P],
                             o_tok[:, k, :].rearrange("p (c n) -> p c n", n=P)).then_inc(out_stored, 16)
            sp.wait_ge(out_stored, 16 * DC)

        @block.gpsimd
        def _(pool):
            steps = Count(pool_steps)

            def then(ins):
                pool.wait_ge(pool_steps, steps.inc(ins))

            nc.gpsimd.memset(ri_raw[:, :, :], 0.0).then_inc(zero_ready, 1)
            then(nc.gpsimd.memset(ident[:, :], 0.0))
            then(nc.gpsimd.affine_select(out=ident[:, :], in_=ident[:, :], compare_op=ALU.not_equal, fill=1.0, base=0,
                                         pattern=[[-1, P]], channel_multiplier=1))
            nc.gpsimd.memset(ones[:, :], 1.0)
            nc.gpsimd.memset(eps[:, :], EPS)
            for n in range(HEADS):
                nc.gpsimd.memset(slopes[:, n:n + 1], -(2.0 ** (-8.0 * (n + 1) / HEADS)))
            nc.gpsimd.memset(xp[:, 0:4], 0.0)
            nc.gpsimd.iota(dist_i[:, :], pattern=[[-1, 3 * CHUNK]], base=CHUNK, channel_multiplier=1)\
                .then_inc(consts_ready, 1)

        @block.scalar
        def _(act):
            steps = Count(act_steps)
            landed = [0, 0, 0, 0]

            def split_hi(t, slot, raw_slot, count, cols):
                act.wait_ge(raw_landed[raw_slot], 16 * count)
                act.wait_ge(tiles_done, CREDIT + t - 4 + 1)
                nc.scalar.copy(w_hi[:, slot, 0:cols], raw[:, raw_slot, 0:cols]).then_inc(w_hi_ready, 1)

            def split_ri(t, g, slot, which):
                act.wait_ge(ri_landed[which], 96 * (g + 1))
                act.wait_ge(tiles_done, CREDIT + t - 4 + 1)
                nc.scalar.copy(w_hi[:, slot, 0:RI_COLS], ri_raw[:, which, :]).then_inc(w_hi_ready, 1)

            def prep(k, stage, gain_col, dst_hi, squares=True):
                nc.scalar.mul(dst_hi[:, k, :], h[:, k, :], gains[:, gain_col + k:gain_col + k + 1]).then_inc(xhi_ready, 1)
                if squares:
                    n = DC * SQS[stage] + k
                    if n >= 2:
                        act.wait_ge(sq_used, n - 1)
                    nc.scalar.activation(sq[:, k % 2, :], h[:, k, :], ACT.Square).then_inc(sq_ready, 1)

            def root_of_mean(norm):
                if norm in SQS:
                    act.wait_ge(sq_used, DC * (SQS[norm] + 1))
                else:
                    act.wait_ge(stat_ready, BLOCK_NORM[norm] + 1)
                nc.scalar.activation(std, stat, ACT.Sqrt, bias=eps[:, 0:1], scale=1.0 / D).then_inc(std_ready, 1)

            act.sem_inc(ri_free, 3)
            act.sem_inc(mix_free, 2)

            act.wait_ge(lam_abs, 1)
            nc.scalar.activation(sp_t[:, 1, :], sp_t[:, 0, :], ACT.Exp, scale=-1.0).then_inc(lam_exp, 1)

            act.wait_ge(params_ready, 1)
            for k in range(DC):
                act.wait_ge(xt_ready, k + 1)
                nc.scalar.copy(h[:, k, :], banks[4 + k % 2][:, :]).then_inc(h_copied, 1)
                act.wait_ge(h_copied, k + 1)
                nc.scalar.mul(x_hi[:, k, :], h[:, k, :], gains[:, G_MIX_PRE + k:G_MIX_PRE + k + 1]).then_inc(xhi_ready, 1)
                if k >= 2:
                    act.wait_ge(sq_used, k - 1)
                nc.scalar.activation(sq[:, k % 2, :], h[:, k, :], ACT.Square).then_inc(sq_ready, 1)
                if k == 0:
                    for s in range(3):
                        split_hi(s, s, s, 1, W_COLS)
            root_of_mean("mix")

            def group(g, last=False):
                t = T_IN + 8 * g
                fills = [(0, 2 * g + 1), (1, 2 * g + 1), (2, g + 1), (3, g + 1), None, None, (0, 2 * g + 2), (1, 2 * g + 2)]

                def ahead(p):
                    p += 3
                    if p in (4, 5):
                        split_ri(t + p, g, p % 4, p - 4)
                    elif p < 8:
                        split_hi(t + p, p % 4, *fills[p], W_COLS)
                    elif not last:
                        split_hi(t + p, p % 4, p - 8, (2 * g + 3) if p < 10 else g + 2, W_COLS)
                    else:
                        split_hi(t + p, p % 4, p - 8, 9 if p < 10 else 5, 6 * P)

                for p in range(3):
                    ahead(p)
                    c = 3 * g + p
                    act.wait_ge(xp_ready, c + 1)
                    nc.scalar.activation(xc[:, p, :], xp[:, 1:S + 1], ACT.Identity, bias=rnn[:, bass.ds(R_CONV_B + c, 1)],
                                         scale=rnn[:, bass.ds(R_CONV_W + c, 1)]).then_inc(tap_ready, 1)
                    act.wait_ge(conv_ready, c + 1)
                    nc.scalar.copy(xc_hi[:, p, :], xc[:, p, :]).then_inc(xchi_ready, 1)

                def gelu(j):
                    act.wait_ge(gate_ready, 3 + 3 * g + j + 1)
                    nc.scalar.activation(gate[:, j, :], gate[:, j, :], ACT.Gelu_apprx_tanh).then_inc(gelu_ready, 1)

                ahead(3)
                gelu(0)
                ahead(4)
                act.wait_ge(tiles_done, CREDIT + t + 4 + 1)
                for j in range(3):
                    ins = nc.scalar.activation(t_u[:, j, :], banks[3 + j][:, :], ACT.Tanh,
                                               bias=half_b[:, bass.ds(3 * g + j, 1)], scale=0.5)
                    ins.then_inc(ri_free, 1)
                ahead(5)
                act.wait_ge(tiles_done, CREDIT + t + 5 + 1)
                for j in range(3):
                    nc.scalar.activation(t_i[:, j, :], banks[3 + j][:, :], ACT.Tanh,
                                         bias=half_b[:, bass.ds(RC + 3 * g + j, 1)], scale=0.5).then_inc(ri_free, 1)
                act.wait_ge(ri_free, 3 + 6 * g + 6)
                for j in range(3):
                    steps_at = steps.inc(nc.scalar.activation(
                        t_u[:, j, :], t_u[:, j, :], ACT.Tanh, bias=sp2[:, bass.ds(3 * g + j, 1)],
                        scale=sp2[:, bass.ds(3 * g + j, 1)]))
                act.wait_ge(act_steps, steps_at)
                nc.scalar.activation(root, t_u[:, :, :], ACT.Sqrt).then_inc(roots_ready, 1)
                ahead(6)
                gelu(1)

                def y_high(j):
                    c = 3 * g + j
                    act.wait_ge(y_ready, c + 1)
                    nc.scalar.copy(y_hi[:, bass.ds(c, 1), :].rearrange("p o n -> p (o n)"), gate[:, j, :])\
                        .then_inc(yhi_ready, 1)

                y_high(0)
                ahead(7)
                gelu(2)
                y_high(1)
                y_high(2)

            repeat(act, 3, steps, 3, group)
            group(3, last=True)

            def out_chunk(stage, m, par, gain_col, t):
                n = DC * OUTS[stage] + m
                act.wait_ge(tiles_done, CREDIT + t + 1)
                nc.scalar.mul(mix[:, bass.ds(m, 1), :].rearrange("p o n -> p (o n)"), banks[4 + par][:, :],
                              gains[:, bass.ds(gain_col + m, 1)])
                act.wait_ge(sum_ready, n + 1)
                nc.scalar.activation(sq[:, 0, :], banks[4 + par][:, :], ACT.Square).then_inc(mix_free, 1)

            def w_out(i, last=False):
                for s in range(4):
                    if s == 0:
                        split_hi(T_OUT + 4 * i + 3, 3, 3, 5 + i, 6 * P)
                    elif not last:
                        split_hi(T_OUT + 4 * i + 3 + s, s - 1, s - 1, (9 if s < 3 else 5) + i + 1, 6 * P)
                    else:
                        split_hi(T_OUT + 4 * i + 3 + s, s - 1, s - 1, (9 if s < 3 else 5) + i + 1, W_COLS)
                    if s % 2:
                        out_chunk("mix0", 2 * i + s // 2, s // 2, G_MIX_POST, T_OUT + 4 * i + s)

            repeat(act, 3, steps, 0, w_out)
            w_out(3, last=True)
            base = [8 + 4, 8 + 4, 4 + 4, 4 + 4]

            def residual(stage, norm, gain_col, dst_hi=None):
                root_of_mean(norm)
                for k in range(DC):
                    if stage == "out":
                        continue
                    act.wait_ge(h_ready, DC * RES[stage] + k + 1)
                    prep(k, stage, gain_col, dst_hi)

            def ffn(f, base):
                residual(f"ffn{f}", f"post_mix{f}", G_FFN_PRE + DC * f, x_hi)
                root_of_mean(f"ffn{f}")

                def pairs(i, last=False):
                    for a in range(2):
                        n = FC * f + 2 * i + a
                        for s in (2 * a, 2 * a + 1):
                            slot = (s + 3) % 4
                            cols = DN_K[slot] * P if last and s > 0 else W_COLS
                            split_hi(T_GU[f] + 4 * i + s + 3, slot, slot, base[slot] + i + (2 if s > 0 else 1), cols)
                        act.wait_ge(g_ready, n + 1)
                        nc.scalar.activation(scratch[:, a, :], scratch[:, a, :], ACT.Silu).then_inc(silu_ready, 1)
                        act.wait_ge(hid_ready, n + 1)
                        nc.scalar.copy(hid_hi[:, bass.ds(2 * i + a, 1), :].rearrange("p o n -> p (o n)"),
                                       scratch[:, 2 + a, :]).then_inc(hidhi_ready, 1)

                repeat(act, FC // 2 - 1, steps, 0, pairs)
                pairs(FC // 2 - 1, last=True)
                b2 = [n + FC // 2 for n in base]

                def down(m, par, last=False):
                    for s in range(4):
                        slot = (s + 3) % 4
                        cols = DN_K[slot] * P
                        if last and s > 0:
                            cols = 4 * P if f == 0 else 0
                        if cols:
                            split_hi(T_DN[f] + 4 * m + s + 3, slot, slot, b2[slot] + m + (2 if s > 0 else 1), cols)
                    out_chunk(f"ffn{f}", m, par, G_FFN_POST + DC * f, T_DN[f] + 4 * m + 3)

                def two(i, last=False):
                    down(2 * i, 0)
                    down(2 * i + 1, 1, last)

                repeat(act, DC // 2 - 1, steps, 0, two)
                two(DC // 2 - 1, last=True)
                return [n + DC for n in b2]

            base = ffn(0, base)

            split_hi(T_KV + 3, 3, 3, base[3] + 1, 4 * P)
            residual("kv", "post_ffn0", G_KV, xkv_hi)
            root_of_mean("kv")
            base = [n + 1 for n in base]
            for s in range(3):
                split_hi(T_Q + s, s, s, base[s] + 2, W_COLS)
            for k in range(DC):
                nc.scalar.mul(x_hi[:, k, :], h[:, k, :], gains[:, G_MIX_PRE + DC + k:G_MIX_PRE + DC + k + 1])\
                    .then_inc(xhi_ready, 1)
            act.wait_ge(kv_read, 1)
            nc.scalar.copy(k_hi[:, :], kv[:, 0, :]).then_inc(khi_ready, 1)
            act.wait_ge(v_turned, 1)
            nc.scalar.copy(v_hi[:, :, :], banks[3][:, :].rearrange("p (j n) -> p j n", n=P)).then_inc(vhi_ready, 1)
            nc.scalar.copy(va_hi[0:HD, 1:TC, :], banks[2][0:HD, P:S].rearrange("p (j n) -> p j n", n=P))\
                .then_inc(vhi_ready, 1)

            def q_high(m):
                act.wait_ge(q_read, m + 1)
                nc.scalar.copy(q_hi[:, m % 2, :], q[:, m % 2, :]).then_inc(qhi_ready, 1)

            def exponentials(m, js):
                if js[0] == 0:
                    act.wait_ge(max_ready, m + 1)
                for j in js:
                    c0 = CHUNK if j == 0 else 0
                    for g in range(2):
                        n = 2 * j + g
                        nc.scalar.activation(s_sb[:, m % 2, j, g, c0:], s_sb[:, m % 2, j, g, c0:], ACT.Exp,
                                             bias=sm[:, m % 2, 1, n:n + 1], accum_out=sm[:, m % 2, 3, n:n + 1])
                if js[-1] == TC - 1:
                    nc.scalar.activation(sm[:, m % 2, 4, :], sm[:, m % 2, 2, :], ACT.Exp).then_inc(p_exp, 1)

            def p_high(n):
                act.wait_ge(pt_ready, n + 1)
                if n % TC > 0:
                    nc.scalar.copy(p_hi[0:HD, n % 2, 2 * P:], banks[2 + n % 2][0:HD, 2 * P:])
                nc.scalar.copy(p_hi[:, n % 2, 0:2 * P], banks[2 + n % 2][:, 0:2 * P]).then_inc(phi_ready, 1)

            def o_high(m, half):
                act.wait_ge(o_ready, 2 * m + half + 1)
                js = slice(2 * half, 2 * half + 2)
                for g in range(2):
                    rows = slice(HD * g, HD * g + HD)
                    ins = nc.scalar.copy(o_hi[rows, m, :].rearrange("p (j n) -> p j n", n=P)[:, js, :],
                                         o_ps[rows, js, g, :])
                ins.then_inc(ohi_ready, 1)

            q_high(0)
            q_high(1)
            for m in STEPS:
                for j in range(TC):
                    if 0 <= TC * m + j - 4 < TC * PAIRS_H:
                        p_high(TC * m + j - 4)
                    if j == 0 and 2 <= m + 2 < PAIRS_H:
                        q_high(m + 2)
                    if j == 0 and m + 4 < PAIRS_H + 3:
                        t = m + 4
                        split_hi(T_Q + t, t % 4, t % 4, base[t % 4] + 2 * (t // 4 + 1), W_COLS)
                    if j in (1, 2) and 0 <= m < PAIRS_H:
                        exponentials(m, range(2 * j - 2, 2 * j))
                    if j == 3 and 0 <= m < PAIRS_H:
                        act.wait_ge(den_ready, m + 1)
                        for n in range(TC):
                            c0 = CHUNK if n == 0 else 0
                            ins = nc.scalar.mul(s_sb[:, m % 2, n, 1, c0:], s_sb[:, m % 2, n, 1, c0:],
                                                sm[:, m % 2, 5, 2 * n + 1:2 * n + 2])
                        ins.then_inc(p1_ready, 1)
                    if o_half(m, j):
                        o_high(*o_half(m, j))
            base = [n + 4 for n in base]

            def w_o(i, last=False):
                for s in range(4):
                    slot = (s + 3) % 4
                    t = T_O + 4 * i + s + 3
                    if last and s >= 1:
                        split_hi(t, slot, slot, base[slot] + 4 + 1, W_COLS)
                    else:
                        split_hi(t, slot, slot, base[slot] + 2 * i + (4 if s >= 1 else 2), W_COLS)
                    out_chunk("mix1", 4 * i + s, s % 2, G_MIX_POST + DC, T_O + 4 * i + s)

            repeat(act, 1, steps, 0, w_o)
            w_o(1, last=True)
            base = [n + 4 for n in base]
            base = ffn(1, base)
            residual("out", "post_ffn1", None)
            for k in range(DC):
                act.wait_ge(ot_ready, k + 1)
                nc.scalar.copy(o_tok[:, k, :], banks[4 + k % 2][:, :]).then_inc(otok_ready, 1)

        @block.vector
        def _(dve):
            v = nc.vector
            steps = Count(dve_steps)

            def then(ins):
                dve.wait_ge(dve_steps, steps.inc(ins))

            def split_lo(t, slot, raw_slot, cols):
                dve.wait_ge(w_hi_ready, t + 1)
                v.tensor_tensor(w_lo[:, slot, 0:cols], raw[:, raw_slot, 0:cols], w_hi[:, slot, 0:cols].bitcast(F32),
                                ALU.subtract).then_inc(w_lo_ready, 1)

            def split_lo_ri(t, slot, which):
                dve.wait_ge(w_hi_ready, t + 1)
                v.tensor_tensor(w_lo[:, slot, 0:RI_COLS], ri_raw[:, which, :], w_hi[:, slot, 0:RI_COLS].bitcast(F32),
                                ALU.subtract).then_inc(w_lo_ready, 1)

            def input_lo(k, stage, gain_col, hi, lo):
                dve.wait_ge(xhi_ready, DC * PREP[stage] + k + 1)
                v.scalar_tensor_tensor(out=lo[:, k, :], in0=h[:, k, :], scalar=gains[:, gain_col + k:gain_col + k + 1],
                                       in1=hi[:, k, :].bitcast(F32), op0=ALU.mult, op1=ALU.subtract).then_inc(x_ready, 1)

            def reciprocal_of_root(norm):
                dve.wait_ge(std_ready, NORM[norm] + 1)
                v.reciprocal(rstd[:, :], std).then_inc(rstd_ready, 1)
                dve.wait_ge(rstd_ready, NORM[norm] + 1)

            dve.sem_inc(w_lo_ready, CREDIT)
            dve.sem_inc(gate_ready, 3)
            dve.sem_inc(gu_free, 2)
            dve.sem_inc(sum_ready, 1)

            dve.wait_ge(rows_ready, 2)
            v.tensor_copy(gains[:, :], banks[0][:, 0:G_ROWS])
            then(v.tensor_copy(rnn[:, :], banks[1][:, 0:R_ROWS]))
            lam = rnn[:, R_LAM:R_LAM + RC]
            v.tensor_scalar(half_b[:, :], rnn[:, R_BRG:R_BRG + 2 * RC], 0.5, None, ALU.mult)
            v.tensor_scalar(sp_t[:, 3, :], lam, -1.0, 0.0, ALU.mult, ALU.max)
            then(v.tensor_scalar(sp_t[:, 2, :], lam, -1.0, None, ALU.mult))
            v.tensor_tensor(sp_t[:, 0, :], sp_t[:, 2, :], lam, ALU.max).then_inc(lam_abs, 1)
            dve.wait_ge(lam_exp, 1)
            then(v.tensor_scalar(sp_t[:, 0, :], sp_t[:, 1, :], 2.0, None, ALU.add))
            then(v.reciprocal(sp_t[:, 0, :], sp_t[:, 0, :]))
            then(v.tensor_tensor(sp_t[:, 1, :], sp_t[:, 1, :], sp_t[:, 0, :], ALU.mult))
            then(v.tensor_tensor(sp_t[:, 2, :], sp_t[:, 1, :], sp_t[:, 1, :], ALU.mult))
            then(v.tensor_scalar(sp_t[:, 0, :], sp_t[:, 2, :], 1.0 / 15, 1.0 / 13, ALU.mult, ALU.add))
            for n in (11, 9, 7, 5, 3, 1):
                then(v.tensor_tensor(sp_t[:, 0, :], sp_t[:, 0, :], sp_t[:, 2, :], ALU.mult))
                then(v.tensor_scalar(sp_t[:, 0, :], sp_t[:, 0, :], 1.0 / n, None, ALU.add))
            then(v.tensor_tensor(sp_t[:, 0, :], sp_t[:, 0, :], sp_t[:, 1, :], ALU.mult))
            then(v.tensor_scalar(sp_t[:, 0, :], sp_t[:, 0, :], 2.0, None, ALU.mult))
            then(v.tensor_tensor(sp_t[:, 0, :], sp_t[:, 0, :], sp_t[:, 3, :], ALU.add))
            v.tensor_scalar(sp2[:, :], sp_t[:, 0, :], 2.0, None, ALU.mult)
            dve.wait_ge(params_landed, 16 * 11)
            for j in range(TC):
                v.tensor_copy(sinks[:, :, j, :], sinks_in[:, :].rearrange("p (g m) -> p m g", g=2))
            dve.wait_ge(consts_ready, 1)
            then(v.tensor_copy(dist[:, :], dist_i[:, :]))
            then(v.tensor_scalar(rstd[:, 0:3 * CHUNK], dist[:, :], -1.0, None, ALU.mult))
            then(v.tensor_tensor(dist[:, :], dist[:, :], rstd[:, 0:3 * CHUNK], ALU.max))
            v.memset(dist[0:CHUNK, 2 * CHUNK:3 * CHUNK], MASKED)
            v.memset(dist[CHUNK:P, 0:CHUNK], MASKED).then_inc(params_ready, 1)
            dve.wait_ge(params_ready, 1)

            for k in range(DC):
                input_lo(k, "mix", G_MIX_PRE, x_hi, x_lo)
                if k == 0:
                    for s in range(3):
                        split_lo(s, s, s, W_COLS)
            reciprocal_of_root("mix")

            def group(g, last=False):
                t = T_IN + 8 * g

                def ahead(p):
                    p += 3
                    if p in (4, 5):
                        split_lo_ri(t + p, p % 4, p - 4)
                    elif p < 8:
                        split_lo(t + p, p % 4, IN_RAW[p], W_COLS)
                    else:
                        split_lo(t + p, p % 4, p - 8, 6 * P if last else W_COLS)

                def xc_low(j):
                    dve.wait_ge(xchi_ready, 3 * g + j + 1)
                    v.tensor_tensor(xc_lo[:, j, :], xc[:, j, :], xc_hi[:, j, :].bitcast(F32), ALU.subtract)\
                        .then_inc(xc_ready, 1)

                for j in range(3):
                    c = 3 * g + j
                    dve.wait_ge(tiles_done, CREDIT + t + j + 1)
                    v.tensor_tensor(xp[:, 4:S + 4], banks[j][:, :], rstd[:, :], ALU.mult).then_inc(xp_ready, 1)
                    ahead(j)
                    dve.wait_ge(tap_ready, c + 1)
                    for k in range(1, 4):
                        ins = v.scalar_tensor_tensor(out=xc[:, j, :], in0=xp[:, 1 + k:S + 1 + k],
                                                     scalar=rnn[:, bass.ds(R_CONV_W + RC * k + c, 1)], in1=xc[:, j, :],
                                                     op0=ALU.mult, op1=ALU.add)
                        if k < 3:
                            then(ins)
                        else:
                            ins.then_inc(conv_ready, 1)
                    xc_low(j)

                def gate_in(j):
                    dve.wait_ge(tiles_done, CREDIT + t + (3, 6, 7)[j] + 1)
                    v.tensor_tensor(gate[:, j, :], banks[j][:, :], rstd[:, :], ALU.mult).then_inc(gate_ready, 1)

                def recurrence(j):
                    c = 3 * g + j
                    then(v.tensor_scalar(decay[:, :], t_u[:, j, :], 1.0, None, ALU.add))
                    then(v.reciprocal(decay[:, :], decay[:, :]))
                    v.tensor_tensor(root[:, j, :], root[:, j, :], decay[:, :], ALU.mult)
                    then(v.scalar_tensor_tensor(out=t_i[:, j, :], in0=t_i[:, j, :], scalar=1.0, in1=xc[:, j, :],
                                                op0=ALU.add, op1=ALU.mult))
                    v.tensor_scalar(decay[:, :], decay[:, :], 2.0, -1.0, ALU.mult, ALU.add)
                    then(v.tensor_tensor(root[:, j, :], root[:, j, :], t_i[:, j, :], ALU.mult))
                    then(v.tensor_tensor_scan(state, decay[:, :], root[:, j, :], 0.0, ALU.mult, ALU.add))
                    dve.wait_ge(gelu_ready, c + 1)
                    v.tensor_tensor(gate[:, j, :], state, gate[:, j, :], ALU.mult).then_inc(y_ready, 1)

                def y_low(j):
                    c = 3 * g + j
                    dve.wait_ge(yhi_ready, c + 1)
                    v.tensor_tensor(y_lo[:, bass.ds(c, 1), :].rearrange("p o n -> p (o n)"), gate[:, j, :],
                                    y_hi[:, bass.ds(c, 1), :].rearrange("p o n -> p (o n)").bitcast(F32),
                                    ALU.subtract).then_inc(ylo_ready, 1)

                ahead(3)
                gate_in(0)
                ahead(4)
                ahead(5)
                dve.wait_ge(roots_ready, g + 1)
                recurrence(0)
                ahead(6)
                gate_in(1)
                y_low(0)
                recurrence(1)
                ahead(7)
                gate_in(2)
                y_low(1)
                recurrence(2)
                y_low(2)

            repeat(dve, 3, steps, 3 * 2 + 3 * 5, group)
            group(3, last=True)

            def sum_squares(stage, m):
                n = DC * OUTS[stage] + m
                dve.wait_ge(mix_free, 2 + n + 1)
                v.tensor_tensor(sq_sum, sq_sum, sq[:, 0, :], ALU.add).then_inc(sum_ready, 1)

            def clear_sum():
                then(v.memset(sq_sum, 0.0))

            clear_sum()

            def w_out(i, last=False):
                for s in range(4):
                    split_lo(T_OUT + 4 * i + 3 + s, (s + 3) % 4, (s + 3) % 4, W_COLS if last and s > 0 else 6 * P)
                    if s % 2:
                        sum_squares("mix0", 2 * i + s // 2)

            repeat(dve, 3, steps, 0, w_out)
            w_out(3, last=True)

            def residual(stage, norm, gain_col=None, hi=None, lo=None):
                reciprocal_of_root(norm)
                for k in range(DC):
                    then(v.tensor_tensor(mix[:, k, :], mix[:, k, :], rstd[:, :], ALU.mult))
                    v.tensor_tensor(h[:, k, :], h[:, k, :], mix[:, k, :], ALU.add).then_inc(h_ready, 1)
                    if hi is not None and k > 0:
                        input_lo(k - 1, stage, gain_col, hi, lo)
                if hi is not None:
                    input_lo(DC - 1, stage, gain_col, hi, lo)

            def ffn(f):
                residual(f"ffn{f}", f"post_mix{f}", G_FFN_PRE + DC * f, x_hi, x_lo)
                reciprocal_of_root(f"ffn{f}")

                def pairs(i, last=False):
                    for a in range(2):
                        n = FC * f + 2 * i + a
                        for s in (2 * a, 2 * a + 1):
                            slot = (s + 3) % 4
                            split_lo(T_GU[f] + 4 * i + s + 3, slot, slot, DN_K[slot] * P if last and s > 0 else W_COLS)
                        dve.wait_ge(tiles_done, CREDIT + T_GU[f] + 4 * i + 2 * a + 1 + 1)
                        v.tensor_tensor(scratch[:, a, :], banks[2 * a][:, :], rstd[:, :], ALU.mult).then_inc(g_ready, 1)
                        v.tensor_tensor(scratch[:, 2 + a, :], banks[2 * a + 1][:, :], rstd[:, :], ALU.mult)\
                            .then_inc(gu_free, 1)
                        dve.wait_ge(gu_free, 2 + n + 1)
                        dve.wait_ge(silu_ready, n + 1)
                        v.tensor_tensor(scratch[:, 2 + a, :], scratch[:, a, :], scratch[:, 2 + a, :], ALU.mult)\
                            .then_inc(hid_ready, 1)
                        dve.wait_ge(hidhi_ready, n + 1)
                        at_m = bass.ds(2 * i + a, 1)
                        v.tensor_tensor(hid_lo[:, at_m, :].rearrange("p o n -> p (o n)"), scratch[:, 2 + a, :],
                                        hid_hi[:, at_m, :].rearrange("p o n -> p (o n)").bitcast(F32),
                                        ALU.subtract).then_inc(hidlo_ready, 1)

                repeat(dve, FC // 2 - 1, steps, 0, pairs)
                pairs(FC // 2 - 1, last=True)
                dve.wait_ge(hidlo_ready, FC * (f + 1))
                clear_sum()

                def down(m, last=False):
                    for s in range(4):
                        slot = (s + 3) % 4
                        cols = DN_K[slot] * P
                        if last and s > 0:
                            cols = 4 * P if f == 0 else 0
                        if cols:
                            split_lo(T_DN[f] + 4 * m + s + 3, slot, slot, cols)
                    sum_squares(f"ffn{f}", m)

                repeat(dve, DC - 1, steps, 0, down)
                down(DC - 1, last=True)

            ffn(0)

            split_lo(T_KV + 3, 3, 3, 4 * P)
            residual("kv", "post_ffn0", G_KV, xkv_hi, xkv_lo)
            reciprocal_of_root("kv")
            for s in range(3):
                split_lo(T_Q + s, s, s, W_COLS)
            for k in range(DC):
                input_lo(k, "q", G_MIX_PRE + DC, x_hi, x_lo)
            dve.wait_ge(tiles_done, CREDIT + T_KV + 3 + 1)
            v.tensor_tensor(kv[:, 1, :], banks[1][:, :], rstd[:, :], ALU.mult)
            v.tensor_tensor(kv[:, 0, :], banks[0][:, :], rstd[:, :], ALU.mult).then_inc(kv_read, 1)
            dve.wait_ge(khi_ready, 1)
            v.tensor_tensor(k_lo[:, :], kv[:, 0, :], k_hi[:, :].bitcast(F32), ALU.subtract)
            dve.wait_ge(vhi_ready, 2)
            v.tensor_tensor(v_lo[:, :, :], banks[3][:, :].rearrange("p (j n) -> p j n", n=P), v_hi[:, :, :].bitcast(F32),
                            ALU.subtract)
            v.tensor_tensor(va_lo[0:HD, 1:TC, :], banks[2][0:HD, P:S].rearrange("p (j n) -> p j n", n=P),
                            va_hi[0:HD, 1:TC, :].bitcast(F32), ALU.subtract).then_inc(v_ready, 1)
            for b in range(2):
                then(v.memset(s_sb[:, b, 0, :, 0:CHUNK], -1e30))

            def q_in(m):
                dve.wait_ge(tiles_done, CREDIT + T_Q + m + 1)
                v.scalar_tensor_tensor(out=q[:, m % 2, :], in0=banks[Q_BANK[m]][:, :], scalar=HD ** -0.5, in1=rstd[:, :],
                                       op0=ALU.mult, op1=ALU.mult).then_inc(q_read, 1)

            def q_low(m):
                dve.wait_ge(qhi_ready, m + 1)
                v.tensor_tensor(q_lo[:, m % 2, :], q[:, m % 2, :], q_hi[:, m % 2, :].bitcast(F32), ALU.subtract)\
                    .then_inc(qlo_ready, 1)

            def biased(m, j):
                dve.wait_ge(s_ready, TC * m + j + 1)
                c0 = CHUNK if j == 0 else 0
                for g in range(2):
                    head = m + PAIRS_H * g
                    ins = v.scalar_tensor_tensor(out=s_sb[:, m % 2, j, g, c0:], in0=dist[:, c0:],
                                                 scalar=slopes[:, head:head + 1], in1=banks[g][:, c0:3 * CHUNK],
                                                 op0=ALU.mult, op1=ALU.add)
                ins.then_inc(s_read, 1)

            def row_max(m):
                b = m % 2
                dve.wait_ge(s_read, TC * (m + 1))
                then(v.tensor_reduce(sm[:, b, 0, :], s_sb[:, b, :, :, :].rearrange("p j g w -> p (j g) w"), AX.X, ALU.max))
                sink = sinks[:, m, :, :].rearrange("p j g -> p (j g)")
                then(v.tensor_tensor(sm[:, b, 0, :], sm[:, b, 0, :], sink, ALU.max))
                v.tensor_scalar(sm[:, b, 1, :], sm[:, b, 0, :], -1.0, None, ALU.mult)
                v.tensor_tensor(sm[:, b, 2, :], sink, sm[:, b, 0, :], ALU.subtract).then_inc(max_ready, 1)

            def normalise(m):
                b = m % 2
                dve.wait_ge(p_exp, m + 1)
                then(v.tensor_tensor(sm[:, b, 5, :], sm[:, b, 3, :], sm[:, b, 4, :], ALU.add))
                v.reciprocal(sm[:, b, 5, :], sm[:, b, 5, :]).then_inc(den_ready, 1)
                dve.wait_ge(den_ready, m + 1)
                for n in range(TC):
                    c0 = CHUNK if n == 0 else 0
                    ins = v.tensor_scalar(s_sb[:, b, n, 0, c0:], s_sb[:, b, n, 0, c0:], sm[:, b, 5, 2 * n:2 * n + 1],
                                          None, ALU.mult)
                ins.then_inc(p0_ready, 1)

            def p_low(n):
                dve.wait_ge(phi_ready, n + 1)
                bank = banks[2 + n % 2]
                if n % TC > 0:
                    v.tensor_tensor(p_lo[0:HD, n % 2, 2 * P:], bank[0:HD, 2 * P:], p_hi[0:HD, n % 2, 2 * P:].bitcast(F32),
                                    ALU.subtract)
                v.tensor_tensor(p_lo[:, n % 2, 0:2 * P], bank[:, 0:2 * P], p_hi[:, n % 2, 0:2 * P].bitcast(F32),
                                ALU.subtract).then_inc(plo_ready, 1)

            def o_low(m, half):
                dve.wait_ge(ohi_ready, 2 * m + half + 1)
                js = slice(2 * half, 2 * half + 2)
                for g in range(2):
                    rows = slice(HD * g, HD * g + HD)
                    lo = o_lo[rows, m, :].rearrange("p (j n) -> p j n", n=P)[:, js, :]
                    hi = o_hi[rows, m, :].rearrange("p (j n) -> p j n", n=P)[:, js, :]
                    ins = v.tensor_tensor(lo, o_ps[rows, js, g, :], hi.bitcast(F32), ALU.subtract)
                ins.then_inc(olo_ready, 1)

            q_in(0)
            q_in(1)
            q_low(0)
            q_low(1)
            for m in STEPS:
                for j in range(TC):
                    if j == 0 and 2 <= m + 2 < PAIRS_H:
                        q_in(m + 2)
                    if j == 3 and 0 <= m < PAIRS_H:
                        normalise(m)
                    if m + 1 < PAIRS_H:
                        biased(m + 1, j)
                    if 0 <= TC * m + j - 4 < TC * PAIRS_H:
                        p_low(TC * m + j - 4)
                    if j == 0 and 0 <= m < PAIRS_H:
                        row_max(m)
                    if j == 1 and 2 <= m + 2 < PAIRS_H:
                        q_low(m + 2)
                    if j == 1 and m + 4 < PAIRS_H + 3:
                        split_lo(T_Q + m + 4, m % 4, m % 4, W_COLS)
                    if o_half(m, j):
                        o_low(*o_half(m, j))
            clear_sum()

            def w_o(i, last=False):
                for s in range(4):
                    slot = (s + 3) % 4
                    split_lo(T_O + 4 * i + s + 3, slot, slot, W_COLS)
                    sum_squares("mix1", 4 * i + s)

            repeat(dve, 1, steps, 0, w_o)
            w_o(1, last=True)
            ffn(1)
            residual("out", "post_ffn1")

        @block.tensor
        def _(pe):
            def products(ps, hi_w, lo_w, hi_x, lo_x, first, final):
                nc.tensor.matmul(ps, hi_w, hi_x, start=first, stop=False)
                nc.tensor.matmul(ps, hi_w, lo_x, start=False, stop=False)
                return nc.tensor.matmul(ps, lo_w, hi_x, start=False, stop=final)

            def tile(ps, slot, at, k, first, final, hi=x_hi, lo=x_lo):
                cols = slice(at * P, at * P + P)
                return products(ps, w_hi[:, slot, cols], w_lo[:, slot, cols], hi[:, k, :], lo[:, k, :], first, final)

            def tile_ready(t):
                pe.wait_ge(w_lo_ready, CREDIT + t + 1)

            def sum_chunk(stage, k):
                pe.wait_ge(sq_ready, DC * SQS[stage] + k + 1)
                ins = nc.tensor.matmul(stat, ones[:, :], sq[:, k % 2, :], start=(k == 0), stop=(k == DC - 1))
                ins.then_inc(sq_used, 1)

            pe.sem_inc(tiles_done, CREDIT)
            pe.wait_ge(consts_ready, 1)
            pe.wait_ge(params_landed, 16 * 11)
            nc.tensor.transpose(banks[0][:, 0:G_ROWS], g_rows[0:G_ROWS, :], ident[0:G_ROWS, 0:G_ROWS]).then_inc(rows_ready, 1)
            nc.tensor.transpose(banks[1][:, 0:R_ROWS], r_rows[0:R_ROWS, :], ident[0:R_ROWS, 0:R_ROWS]).then_inc(rows_ready, 1)
            for c in range(TC):
                pe.wait_ge(x_landed[c], 16)

            def turn_x(k):
                if k >= 2:
                    pe.wait_ge(h_copied, k - 1)
                for c in range(TC):
                    ins = nc.tensor.transpose(banks[4 + k % 2][:, c * P:(c + 1) * P], x_tok[:, c, k * P:(k + 1) * P],
                                              ident[:, :])
                ins.then_inc(xt_ready, 1)

            def block_gates(g):
                for which in range(2):
                    t = T_IN + 8 * g + 4 + which
                    tile_ready(t)
                    if which == 0:
                        pe.wait_ge(xc_ready, 3 * g + 3)
                    for m in range(3):
                        pe.wait_ge(ri_free, 6 * g + 3 * which + m + 1)
                        ks = RI_PAIRS[m]
                        for k in ks:
                            cols = slice(RI_AT[k] + P * m, RI_AT[k] + P * m + P)
                            ins = products(banks[3 + m][:, :], w_hi[:, t_slot(4 + which), cols],
                                           w_lo[:, t_slot(4 + which), cols], xc_hi[:, k, :], xc_lo[:, k, :],
                                           k == ks[0], k == ks[-1])
                    ins.then_inc(tiles_done, 1)

            def t_slot(p):
                return p % 4

            def xg_tile(g, p, n, bank):
                tile_ready(T_IN + 8 * g + p)
                if n < 3:
                    pe.wait_ge(gate_ready, 3 * g + n + 1)
                else:
                    pe.wait_ge(xp_ready, 3 * g + n - 3 + 1)
                for k in range(DC):
                    ins = tile(banks[bank][:, :], t_slot(p), k, k, k == 0, k == DC - 1)
                ins.then_inc(tiles_done, 1)

            def rest_of_group(g):
                xg_tile(g, 3, 3, 0)
                block_gates(g)
                xg_tile(g, 6, 4, 1)
                xg_tile(g, 7, 5, 2)

            turn_x(0)
            turn_x(1)
            for k in range(DC):
                if k + 2 < DC:
                    turn_x(k + 2)
                pe.wait_ge(x_ready, k + 1)
                for p in range(3):
                    if k == 0:
                        tile_ready(p)
                    ins = tile(banks[p][:, :], p, k, k, k == 0, k == DC - 1)
                    if k == DC - 1:
                        ins.then_inc(tiles_done, 1)
                sum_chunk("mix", k)
            rest_of_group(0)

            with pe.Fori(0, 3) as i:
                g = i + 1
                for p in range(3):
                    xg_tile(g, p, p, p)
                rest_of_group(g)

            pe.wait_ge(ri_free, 3 + 24)

            def w_out(i, first=False):
                for s in range(4):
                    m = 2 * i + s // 2
                    tile_ready(T_OUT + 4 * i + s)
                    if s % 2 == 0:
                        pe.wait_ge(mix_free, m + 1)
                    for n in range(6):
                        k = 6 * (s % 2) + n
                        if first:
                            pe.wait_ge(ylo_ready, k + 1)
                        ins = tile(banks[4 + s // 2][:, :], s, n, k, k == 0, k == RC - 1, y_hi, y_lo)
                    ins.then_inc(tiles_done, 1)

            w_out(0, first=True)
            with pe.Fori(0, 3) as i:
                w_out(i + 1)

            def sum_block(norm, stage):
                pe.wait_ge(sum_ready, 1 + DC * (OUTS[stage] + 1))
                nc.tensor.matmul(stat, ones[:, :], sq_sum, start=True, stop=True).then_inc(stat_ready, 1)

            def ffn(f):
                sum_block(f"post_mix{f}", f"mix{f}")

                def pair(n, a, first=False):
                    pe.wait_ge(gu_free, FC * f + n + 1)
                    tile_ready(T_GU[f] + 2 * n)
                    tile_ready(T_GU[f] + 2 * n + 1)
                    for k in range(DC):
                        if first:
                            pe.wait_ge(x_ready, DC * PREP[f"ffn{f}"] + k + 1)
                        for u in range(2):
                            ins = tile(banks[2 * a + u][:, :], 2 * a + u, k, k, k == 0, k == DC - 1)
                            if k == DC - 1:
                                ins.then_inc(tiles_done, 1)
                        if first:
                            sum_chunk(f"ffn{f}", k)

                pair(0, 0, first=True)
                pair(1, 1)
                with pe.Fori(0, FC // 2 - 1) as i:
                    for a in range(2):
                        pair(2 * i + 2 + a, a)

                def down(m, par, first=False):
                    pe.wait_ge(mix_free, DC * OUTS[f"ffn{f}"] + m + 1)
                    for s in range(4):
                        tile_ready(T_DN[f] + 4 * m + s)
                        for n in range(DN_K[s]):
                            k = DN_AT[s] + n
                            if first:
                                pe.wait_ge(hidlo_ready, FC * f + k + 1)
                            ins = tile(banks[4 + par][:, :], s, n, k, k == 0, k == FC - 1, hid_hi, hid_lo)
                        ins.then_inc(tiles_done, 1)

                down(0, 0, first=True)
                down(1, 1)
                with pe.Fori(0, DC // 2 - 1) as i:
                    for a in range(2):
                        down(2 * i + 2 + a, a)

            ffn(0)

            sum_block("post_ffn0", "ffn0")
            for k in range(DC):
                pe.wait_ge(x_ready, DC * PREP["kv"] + k + 1)
                for u in range(2):
                    s = 2 * (k // 4) + u
                    if k % 4 == 0:
                        tile_ready(T_KV + s)
                    ins = tile(banks[u][:, :], s, k % 4, k, k == 0, k == DC - 1, xkv_hi, xkv_lo)
                    if k % 4 == 3:
                        ins.then_inc(tiles_done, 1)
                sum_chunk("kv", k)
            pe.wait_ge(kv_read, 1)
            for j in range(TC):
                ins = nc.tensor.transpose(banks[3][:, j * P:(j + 1) * P], kv[:, 1, j * P:(j + 1) * P], ident[:, :])
            for j in range(1, TC):
                ins = nc.tensor.transpose(banks[2][0:HD, j * P:(j + 1) * P], kv[:, 1, j * P - HD:j * P], ident[:, :])
            ins.then_inc(v_turned, 1)

            def q_chunk(m, ks):
                if ks[0] == 0:
                    tile_ready(T_Q + m)
                    if m >= 3:
                        pe.wait_ge(q_read, m)
                for k in ks:
                    if m == 0:
                        pe.wait_ge(x_ready, DC * PREP["q"] + k + 1)
                    ins = tile(banks[Q_BANK[m]][:, :], m % 4, k, k, k == 0, k == DC - 1)
                if ks[-1] == DC - 1:
                    ins.then_inc(tiles_done, 1)

            def scores(m, j):
                if j == 0:
                    pe.wait_ge(qlo_ready, m + 1)
                if m > 0 or j > 0:
                    pe.wait_ge(s_read, TC * m + j)
                else:
                    pe.wait_ge(q_read, 2)
                c0 = CHUNK if j == 0 else 0
                keys = slice(j * P - CHUNK + c0, j * P + P)
                for g in range(2):
                    rows = slice(HD * g, HD * g + HD)
                    qs = slice(j * P, (j + 1) * P)
                    ins = products(banks[g][:, c0:3 * CHUNK], q_hi[rows, m % 2, qs], q_lo[rows, m % 2, qs],
                                   k_hi[rows, keys], k_lo[rows, keys], True, True)
                ins.then_inc(s_ready, 1)

            def turn(n):
                m, j, b = n // TC, n % TC, n // TC % 2
                if j == 0:
                    pe.wait_ge(p0_ready, m + 1)
                    pe.wait_ge(p1_ready, m + 1)
                if n >= 2:
                    pe.wait_ge(plo_ready, n - 1)
                bank = banks[2 + n % 2]
                for g in range(2):
                    ins = nc.tensor.transpose(bank[:, g * P:(g + 1) * P], s_sb[:, b, j, g, CHUNK:3 * CHUNK], ident[:, :])
                if j > 0:
                    for g in range(2):
                        ins = nc.tensor.transpose(bank[0:HD, (2 + g) * P:(3 + g) * P], s_sb[:, b, j, g, 0:CHUNK],
                                                  ident[:, :])
                ins.then_inc(pt_ready, 1)

            def values(n):
                m, j = n // TC, n % TC
                pe.wait_ge(plo_ready, n + 1)
                if m > 0 and j % 2 == 0:
                    pe.wait_ge(olo_ready, 2 * m - 1 + j // 2)
                o = o_ps[:, j, :, :].rearrange("p g n -> p (g n)")
                both, before = slice(0, 2 * P), slice(2 * P, 4 * P)
                ins = products(o, v_hi[:, j, :], v_lo[:, j, :], p_hi[:, n % 2, both], p_lo[:, n % 2, both], True, j == 0)
                if j > 0:
                    ins = products(o, va_hi[0:HD, j, :], va_lo[0:HD, j, :], p_hi[0:HD, n % 2, before],
                                   p_lo[0:HD, n % 2, before], False, True)
                if j % 2:
                    ins.then_inc(o_ready, 1)

            pe.wait_ge(kv_read, 1)
            q_chunk(0, range(DC))
            q_chunk(1, range(DC))
            q_chunk(2, range(DC))
            pe.wait_ge(v_ready, 1)
            for m in STEPS:
                for j in range(TC):
                    if 0 <= TC * m + j - 4 < TC * PAIRS_H:
                        turn(TC * m + j - 4)
                    if m + 1 < PAIRS_H:
                        scores(m + 1, j)
                    if 3 <= m + 3 < PAIRS_H:
                        q_chunk(m + 3, Q_PARTS[j])
                    if 0 <= TC * m + j - 5 < TC * PAIRS_H:
                        values(TC * m + j - 5)

            pe.wait_ge(olo_ready, 2 * PAIRS_H)

            def w_o(m, s):
                tile_ready(T_O + m)
                pe.wait_ge(mix_free, DC * OUTS["mix1"] + m + 1)
                for k in range(DC):
                    ins = tile(banks[4 + s % 2][:, :], s, k, k, k == 0, k == DC - 1, o_hi, o_lo)
                ins.then_inc(tiles_done, 1)

            with pe.Fori(0, 2) as i:
                for s in range(4):
                    w_o(4 * i + s, s)
            ffn(1)

            sum_block("post_ffn1", "ffn1")
            for k in range(DC):
                pe.wait_ge(h_ready, DC * RES["out"] + k + 1)
                if k >= 2:
                    pe.wait_ge(otok_ready, k - 1)
                for c in range(TC):
                    ins = nc.tensor.transpose(banks[4 + k % 2][:, c * P:(c + 1) * P], h[:, k, c * P:(c + 1) * P],
                                              ident[:, :])
                ins.then_inc(ot_ready, 1)


_INS = ["x", "a_w_in", "a_conv_w", "a_conv_b", "a_w_rg", "a_b_rg", "a_w_ig", "a_b_ig", "a_lam", "a_w_out", "kv_norm",
        "w_kv", "b_w_q", "b_sinks", "b_w_o", "ffn_w_gu", "ffn_w_down", "mix_pre", "mix_post", "ffn_pre", "ffn_post"]


def kernel(**inputs):
    import numpy as np
    import concourse.bacc as bacc
    from concourse.bass_utils import run_bass_kernel_spmd

    nc = bacc.Bacc("TRN2", target_bir_lowering=False, num_devices=1)
    arrays, args = {}, []
    for name in _INS:
        a = np.ascontiguousarray(inputs[name])
        arrays[f"in_{name}"] = a
        args.append(nc.dram_tensor(f"in_{name}", a.shape, mybir.dt.from_np(a.dtype), kind="ExternalInput").ap())
    args.append(nc.dram_tensor("result", (1, S, D), F32, kind="ExternalOutput").ap())
    trunk(nc, *args)
    r = run_bass_kernel_spmd(nc, [arrays], core_ids=[0])
    return r.results[0]["result"]
```

```python
import concourse.bass as bass
from concourse import mybir
from contextlib import ExitStack

F32 = mybir.dt.float32
F32R = mybir.dt.float32r
I32 = mybir.dt.int32
ALU = mybir.AluOpType
ACT = mybir.ActivationFunctionType
AX = mybir.AxisListType

P = 128
D, S, R, FF = 1024, 512, 1536, 2816
DC, RC, FC = D // P, R // P, FF // P
TC = S // P
BW = 96
HD, HEADS, CHUNK = 64, 16, 64
EPS = 1e-6
MASKED = 1e33
W_COLS = 1024
CREDIT = 8

T_IN = 0
T_OUT = T_IN + 32
T_GU = [T_OUT + 16, 0]
T_DN = [T_GU[0] + 44, 0]
T_KV = T_DN[0] + 32
T_Q = T_KV + 4
T_O = T_Q + 8
T_GU[1] = T_O + 8
T_DN[1] = T_GU[1] + 44
DN_K = [6, 5, 6, 5]
DN_AT = [0, 6, 11, 17]
RI_AT = [0, 256, 640 - 128]
RI_PAIRS = [[0, 1], [0, 1, 2], [1, 2]]
RI_COLS = 896
R_TILE, I_TILE = 6, 7

PREP = {"mix": 0, "ffn0": 1, "kv": 2, "q": 3, "ffn1": 4}
SQS = {"mix": 0, "ffn0": 1, "kv": 2, "ffn1": 3}
RES = {"ffn0": 0, "kv": 1, "ffn1": 2, "out": 3}
NORM = {"post_mix0": 0, "post_ffn0": 1, "post_mix1": 2, "post_ffn1": 3}
NORM = {"mix": 0, "post_mix0": 1, "ffn0": 2, "post_ffn0": 3, "kv": 4, "post_mix1": 5, "ffn1": 6, "post_ffn1": 7}
OUTS = {"mix0": 0, "ffn0": 1, "mix1": 2, "ffn1": 3}

G_MIX_PRE, G_MIX_POST, G_FFN_PRE, G_FFN_POST, G_KV, G_ROWS = 0, 16, 32, 48, 64, 72
R_CONV_W, R_CONV_B, R_BRG, R_BIG, R_LAM, R_ROWS = 0, 48, 60, 72, 84, 96


PAIRS_H = HEADS // 2
STEPS = range(-1, PAIRS_H + 2)
Q_BANK = [4, 5, 6] + [5] * 5
Q_PARTS = [range(0, 2), range(2, 4), range(4, 6), range(6, 8)]


def o_half(m, j):
    pair, half = (m - 2, 1) if j == 1 else (m - 1, 0) if j == 3 else (-1, 0)
    return (pair, half) if 0 <= pair < PAIRS_H else None


class Count:

    def __init__(self, sem):
        self.sem, self.n, self.shift = sem, 0, 0

    def inc(self, ins):
        ins.then_inc(self.sem, 1)
        self.n += 1
        return self.n + self.shift


def repeat(eng, times, count, per_turn, body):
    start = count.n
    with eng.Fori(0, times) as i:
        count.shift = i * per_turn
        body(i)
        assert count.n - start == per_turn, (count.n - start, per_turn)
    count.n, count.shift = start + times * per_turn, 0


def trunk(nc, x, a_w_in, a_conv_w, a_conv_b, a_w_rg, a_b_rg, a_w_ig, a_b_ig, a_lam, a_w_out,
          kv_norm, w_kv, b_w_q, b_sinks, b_w_o, ffn_w_gu, ffn_w_down,
          mix_pre, mix_post, ffn_pre, ffn_post, out):
    at = {"top": (nc.sbuf_base + 63) // 64 * 64}

    def sb(name, shape, dt=F32, offset=None):
        n = 4
        for d in shape[1:]:
            n *= d
        if offset is None:
            offset = at["top"]
            at["top"] += (n + 31) // 32 * 32
        at[name] = offset
        return nc.alloc_sbuf_tensor_at(name, shape, dt, offset=offset)

    h = sb("h", [P, DC, S])
    x_hi = sb("x_hi", [P, DC, S], F32R)
    x_lo = sb("x_lo", [P, DC, S], F32R)
    mix = sb("mix", [P, DC, S], F32, at["x_hi"])
    raw = sb("raw", [P, 4, W_COLS])
    w_hi = sb("w_hi", [P, 4, W_COLS], F32R)
    w_lo = sb("w_lo", [P, 4, W_COLS], F32R)
    ident = sb("ident", [P, P])
    ones = sb("ones", [P, P])
    eps = sb("eps", [P, 1])
    gains = sb("gains", [P, G_ROWS])
    rnn = sb("rnn", [P, R_ROWS])
    half_b = sb("half_b", [P, 2 * RC])
    sp2 = sb("sp2", [P, RC])
    sp4 = sb("sp4", [P, RC])
    sp_t = sb("sp_t", [P, 4, RC])
    dist = sb("dist", [P, 3 * CHUNK])
    slopes = sb("slopes", [P, HEADS])
    sinks_in = sb("sinks_in", [P, HEADS])
    sinks = sb("sinks", [P, DC, TC, 2])
    rstd = sb("rstd", [P, S])
    scratch = sb("scratch", [P, 4, S])
    diag, sq, sq_sum = scratch[:, 0, :], scratch[:, 1:3, :], scratch[:, 3, :]
    root_t = sb("root_t", [P, TC])
    rstd_t = sb("rstd_t", [P, TC])
    U = at["top"]

    y_hi = sb("y_hi", [P, RC, S], F32R)
    y_lo = sb("y_lo", [P, RC, S], F32R)
    x_tok = sb("x_tok", [P, TC, D], F32, at["y_lo"])
    ri_raw = sb("ri_raw", [P, 2, RI_COLS])
    xp = sb("xp", [P, S + 4])
    xc = sb("xc", [P, 3, S])
    xc_hi = sb("xc_hi", [P, 3, S], F32R)
    xc_lo = sb("xc_lo", [P, 3, S], F32R)
    gate = sb("gate", [P, 3, S])
    t_i = sb("t_i", [P, 3, S])
    t_u = sb("t_u", [P, 3, S])
    root = scratch[:, 0:3, :]
    e_tail = sb("e_tail", [P, 2, S])
    e_u = [scratch[:, 3, :], e_tail[:, 0, :], e_tail[:, 1, :]]
    g_rows = sb("g_rows", [P, P], F32, at["gate"])
    r_rows = sb("r_rows", [P, P], F32, at["gate"] + 4 * P)
    dist_i = sb("dist_i", [P, 3 * CHUNK], I32, at["gate"] + 8 * P)
    end_a = at["top"]

    at["top"] = U
    hid_hi = sb("hid_hi", [P, FC, S], F32R)
    hid_lo = sb("hid_lo", [P, FC, S], F32R)
    end_f = at["top"]

    at["top"] = U
    o_hi = sb("o_hi", [P, DC, S], F32R)
    o_lo = sb("o_lo", [P, DC, S], F32R)
    xkv_hi = sb("xkv_hi", [P, DC, S], F32R, at["o_hi"])
    xkv_lo = sb("xkv_lo", [P, DC, S], F32R, at["o_lo"])
    q = sb("q", [P, 2, S])
    q_hi = sb("q_hi", [P, 2, S], F32R)
    q_lo = sb("q_lo", [P, 2, S], F32R)
    kv = sb("kv", [P, 2, S])
    k_hi = sb("k_hi", [P, S], F32R)
    k_lo = sb("k_lo", [P, S], F32R)
    v_hi = sb("v_hi", [P, TC, P], F32R)
    v_lo = sb("v_lo", [P, TC, P], F32R)
    va_hi = sb("va_hi", [P, TC, P], F32R)
    va_lo = sb("va_lo", [P, TC, P], F32R)
    s_sb = sb("s_sb", [P, 2, TC, 2, 3 * CHUNK])
    p_hi = sb("p_hi", [P, 2, 4 * P], F32R)
    p_lo = sb("p_lo", [P, 2, 4 * P], F32R)
    sm = sb("sm", [P, 2, 6, 2 * TC])
    end_b = at["top"]
    o_tok = sb("o_tok", [P, DC, S], F32, U)
    assert max(end_a, end_f, end_b) <= nc.sbuf_usable_end, (end_a, end_f, end_b, nc.sbuf_usable_end)

    win_v = a_w_in[0].rearrange("(k p) (g m c) -> p k g m c", p=P, g=2, c=P)
    wout_v = a_w_out[0].rearrange("(k p) n -> p k n", p=P)
    gu_v = [ffn_w_gu[f].rearrange("(k p) (u n) -> p k u n", p=P, u=2) for f in range(2)]
    dn_v = [ffn_w_down[f].rearrange("(k p) n -> p k n", p=P) for f in range(2)]
    kv_v = w_kv.rearrange("(k p) (u n) -> p k u n", p=P, u=2)
    q_v = b_w_q[0].rearrange("(k p) (g n) -> p k g n", p=P, g=2)
    o_v = b_w_o[0].rearrange("(g c d) n -> g d c n", g=2, d=HD)
    rg_v = [w[0].rearrange("(g b) c d -> c b g d", b=4) for w in (a_w_rg, a_w_ig)]
    ri_parts = [(0, 0, 96, 0, 0), (1, 0, 32, 0, 96), (1, 32, 64, 1, 0), (2, 0, 64, 1, 64), (2, 64, 32, 2, 0),
                (3, 0, 96, 2, 32)]

    with ExitStack() as ctx:
        banks = [ctx.enter_context(nc.psum_tensor(f"bank{b}", [P, S], F32)) for b in range(6)]
        o_ps = ctx.enter_context(nc.psum_tensor("o_ps", [P, TC, 2, P], F32))
        q_ps = {4: banks[4][:, :], 5: banks[5][:, :], 6: o_ps[:, 0:2, :, :].rearrange("p j g n -> p (j g n)")}
        stat = o_ps[:, 2:4, :, :].rearrange("p j g n -> p (j g n)")

        def sem(name):
            return ctx.enter_context(nc.semaphore(name))

        stat_t = stat[:, 0:TC]
        x_landed = [sem(f"x_landed{c}") for c in range(TC)]
        params_landed = sem("params_landed")
        raw_landed = [sem(f"raw_landed{s}") for s in range(4)]
        ri_landed = [sem(f"ri_landed{s}") for s in range(2)]
        out_stored = sem("out_stored")
        consts_ready = sem("consts_ready")
        zero_ready = sem("zero_ready")
        pool_steps = sem("pool_steps")
        params_ready = sem("params_ready")
        rows_ready = sem("rows_ready")
        lam_exp = sem("lam_exp")
        lam_abs = sem("lam_abs")
        w_hi_ready = sem("w_hi_ready")
        w_lo_ready = sem("w_lo_ready")
        tiles_done = sem("tiles_done")
        xt_ready = sem("xt_ready")
        h_copied = sem("h_copied")
        sq_ready = sem("sq_ready")
        sq_used = sem("sq_used")
        total_ready = sem("total_ready")
        stat_ready = sem("stat_ready")
        std_ready = sem("std_ready")
        diag_ready = sem("diag_ready")
        spread_ready = sem("spread_ready")
        rstd_ready = sem("rstd_ready")
        gains_ready = sem("gains_ready")
        h_ready = sem("h_ready")
        xhi_ready = sem("xhi_ready")
        x_ready = sem("x_ready")
        conv_ready = sem("conv_ready")
        xchi_ready = sem("xchi_ready")
        xc_ready = sem("xc_ready")
        ri_free = sem("ri_free")
        te_ready = sem("te_ready")
        roots_ready = sem("roots_ready")
        gate_ready = sem("gate_ready")
        gelu_ready = sem("gelu_ready")
        state_ready = sem("state_ready")
        y_ready = sem("y_ready")
        yhi_ready = sem("yhi_ready")
        ylo_ready = sem("ylo_ready")
        gu_free = sem("gu_free")
        g_ready = sem("g_ready")
        silu_ready = sem("silu_ready")
        hid_ready = sem("hid_ready")
        hidhi_ready = sem("hidhi_ready")
        hidlo_ready = sem("hidlo_ready")
        mix_free = sem("mix_free")
        out_squared = sem("out_squared")
        sum_ready = sem("sum_ready")
        dve_steps = sem("dve_steps")
        kv_read = sem("kv_read")
        khi_ready = sem("khi_ready")
        v_turned = sem("v_turned")
        vhi_ready = sem("vhi_ready")
        v_ready = sem("v_ready")
        q_read = sem("q_read")
        qhi_ready = sem("qhi_ready")
        qlo_ready = sem("qlo_ready")
        s_ready = sem("s_ready")
        s_read = sem("s_read")
        max_ready = sem("max_ready")
        p_exp = sem("p_exp")
        den_ready = sem("den_ready")
        p0_ready = sem("p0_ready")
        p1_ready = sem("p1_ready")
        pt_ready = sem("pt_ready")
        phi_ready = sem("phi_ready")
        plo_ready = sem("plo_ready")
        o_ready = sem("o_ready")
        ohi_ready = sem("ohi_ready")
        olo_ready = sem("olo_ready")
        ot_ready = sem("ot_ready")
        otok_ready = sem("otok_ready")

        block = ctx.enter_context(nc.Block())

        @block.sync
        def _(sp):
            def load(t, slot, lag, src, cols, part=(0, P)):
                sp.lower_ap_dma(src)
                sp.wait_ge(w_lo_ready, CREDIT + t - lag + 1)
                dst = raw[part[0]:part[1], slot, 0:cols]
                return sp.dma_start(dst.rearrange("p (k n) -> p k n", n=P), src)

            for c in range(TC):
                sp.dma_start(x_tok[:, c, :], x[0, c * P:(c + 1) * P, :]).then_inc(x_landed[c], 16)
            for row, v in ((G_MIX_PRE, mix_pre), (G_MIX_POST, mix_post), (G_FFN_PRE, ffn_pre), (G_FFN_POST, ffn_post)):
                sp.dma_start(g_rows[row:row + 16, :], v.rearrange("l (c p) -> (l c) p", p=P)).then_inc(params_landed, 16)
            sp.dma_start(g_rows[G_KV:G_ROWS, :], kv_norm.rearrange("(c p) -> c p", p=P)).then_inc(params_landed, 16)
            sp.dma_start(r_rows[0:48, :], a_conv_w[0].rearrange("w (c p) -> (w c) p", p=P)).then_inc(params_landed, 16)
            for row, v in ((R_CONV_B, a_conv_b[0]), (R_BRG, a_b_rg[0].rearrange("n c -> (n c)")),
                           (R_BIG, a_b_ig[0].rearrange("n c -> (n c)")), (R_LAM, a_lam[0])):
                sp.dma_start(r_rows[row:row + 12, :], v.rearrange("(c p) -> c p", p=P)).then_inc(params_landed, 16)
            sp.dma_start(sinks_in[:, :], b_sinks[0:1, :].broadcast_to([P, HEADS])).then_inc(params_landed, 16)
            sp.wait_ge(zero_ready, 1)

            def group(g):
                t = T_IN + 8 * g
                lags = [4, 4, 8, 8, 4, 4]
                for p in range(6):
                    half, m = (1, 3 * g + p) if p < 3 else (0, 3 * g + p - 3)
                    src = win_v[:, :, half, bass.ds(m, 1), :].rearrange("p k o c -> p k (o c)")
                    load(t + p, p % 4, lags[p], src, W_COLS).then_inc(raw_landed[p % 4], 16)
                for which in range(2):
                    blocks = [rg_v[which][r0:r0 + n, b, bass.ds(g, 1), :].rearrange("c o d -> c (o d)")
                              for b, r0, n, k, p0 in ri_parts]
                    sp.lower_ap_dma(blocks[0])
                    sp.wait_ge(w_lo_ready, CREDIT + t + R_TILE + which - 8 + 1)
                    for (b, r0, n, k, p0), src in zip(ri_parts, blocks):
                        lo = RI_AT[k] + BW * b
                        sp.dma_start(ri_raw[p0:p0 + n, which, lo:lo + BW], src).then_inc(ri_landed[which], 16)

            with sp.Fori(0, 4) as g:
                group(g)

            with sp.Fori(0, 2) as i:
                for s in range(8):
                    m, half = 4 * i + s % 4, s // 4
                    load(T_OUT + 8 * i + s, s % 4, 4, wout_v[:, 6 * half:6 * half + 6, bass.ds(P * m, P)],
                         6 * P).then_inc(raw_landed[s % 4], 16)

            def ffn(f):
                with sp.Fori(0, FC // 2) as i:
                    for s in range(4):
                        m, up = 2 * i + s // 2, s % 2
                        load(T_GU[f] + 4 * i + s, s, 4, gu_v[f][:, :, up, bass.ds(P * m, P)],
                             W_COLS).then_inc(raw_landed[s], 16)
                with sp.Fori(0, DC) as m:
                    for s in range(4):
                        load(T_DN[f] + 4 * m + s, s, 4, dn_v[f][:, DN_AT[s]:DN_AT[s] + DN_K[s], bass.ds(P * m, P)],
                             DN_K[s] * P).then_inc(raw_landed[s], 16)

            ffn(0)
            for s in range(4):
                load(T_KV + s, s, 4, kv_v[:, 4 * (s // 2):4 * (s // 2) + 4, s % 2, :], 4 * P).then_inc(raw_landed[s], 16)
            with sp.Fori(0, 2) as i:
                for s in range(4):
                    m = 4 * i + s
                    halves = [q_v[:, :, g, bass.ds(HD * m, HD)] for g in range(2)]
                    sp.lower_ap_dma(halves[0])
                    sp.wait_ge(w_lo_ready, CREDIT + T_Q + m - 4 + 1)
                    for g in range(2):
                        sp.dma_start(raw[:, s, :].rearrange("p (k n) -> p k n", n=P)[:, :, HD * g:HD * g + HD],
                                     halves[g]).then_inc(raw_landed[s], 16)
            with sp.Fori(0, 2) as i:
                for s in range(4):
                    m = 4 * i + s
                    halves = [o_v[g, :, :, bass.ds(P * m, P)] for g in range(2)]
                    sp.lower_ap_dma(halves[0])
                    sp.wait_ge(w_lo_ready, CREDIT + T_O + m - 4 + 1)
                    for g in range(2):
                        sp.dma_start(raw[HD * g:HD * g + HD, s, :].rearrange("p (k n) -> p k n", n=P),
                                     halves[g]).then_inc(raw_landed[s], 16)
            ffn(1)
            for k in range(DC):
                sp.wait_ge(otok_ready, k + 1)
                sp.dma_start(out[0].rearrange("(c p) n -> p c n", p=P)[:, :, k * P:(k + 1) * P],
                             o_tok[:, k, :].rearrange("p (c n) -> p c n", n=P)).then_inc(out_stored, 16)
            sp.wait_ge(out_stored, 16 * DC)

        @block.gpsimd
        def _(pool):
            steps = Count(pool_steps)

            def then(ins):
                pool.wait_ge(pool_steps, steps.inc(ins))

            nc.gpsimd.memset(ri_raw[:, :, :], 0.0).then_inc(zero_ready, 1)
            then(nc.gpsimd.memset(ident[:, :], 0.0))
            then(nc.gpsimd.affine_select(out=ident[:, :], in_=ident[:, :], compare_op=ALU.not_equal, fill=1.0, base=0,
                                         pattern=[[-1, P]], channel_multiplier=1))
            nc.gpsimd.memset(ones[:, :], 1.0)
            nc.gpsimd.memset(eps[:, :], EPS)
            for n in range(HEADS):
                nc.gpsimd.memset(slopes[:, n:n + 1], -(2.0 ** (-8.0 * (n + 1) / HEADS)))
            nc.gpsimd.memset(xp[:, 0:4], 0.0)
            nc.gpsimd.iota(dist_i[:, :], pattern=[[-1, 3 * CHUNK]], base=CHUNK, channel_multiplier=1)\
                .then_inc(consts_ready, 1)
            def add_squares(stage):
                for k in range(1, DC):
                    n = DC * SQS[stage] + k
                    pool.wait_ge(sq_ready, n + 1)
                    if k == 1:
                        ins = nc.gpsimd.tensor_tensor(sq_sum, sq[:, 0, :], sq[:, 1, :], ALU.add)
                    else:
                        pool.wait_ge(sq_used, n)
                        ins = nc.gpsimd.tensor_tensor(sq_sum, sq_sum, sq[:, k % 2, :], ALU.add)
                    ins.then_inc(sq_used, 2 if k == 1 else 1)
                pool.wait_ge(sq_used, DC * (SQS[stage] + 1))
                pool.sem_inc(total_ready, 1)

            add_squares("mix")

            def xc_low(g, j):
                pool.wait_ge(xchi_ready, 3 * g + j + 1)
                nc.gpsimd.tensor_tensor(xc_lo[:, j, :], xc[:, j, :], xc_hi[:, j, :].bitcast(F32), ALU.subtract)\
                    .then_inc(xc_ready, 1)

            def y_out(g, j):
                c = 3 * g + j
                pool.wait_ge(gelu_ready, c + 1)
                pool.wait_ge(state_ready, c + 1)
                nc.gpsimd.tensor_tensor(gate[:, j, :], t_i[:, j, :], gate[:, j, :], ALU.mult).then_inc(y_ready, 1)
                pool.wait_ge(yhi_ready, c + 1)
                nc.gpsimd.tensor_tensor(y_lo[:, bass.ds(c, 1), :].rearrange("p o n -> p (o n)"), gate[:, j, :],
                                        y_hi[:, bass.ds(c, 1), :].rearrange("p o n -> p (o n)").bitcast(F32),
                                        ALU.subtract).then_inc(ylo_ready, 1)

            for j in range(3):
                xc_low(0, j)
            with pool.Fori(0, 3) as i:
                g = i + 1
                xc_low(g, 0)
                y_out(g - 1, 0)
                xc_low(g, 1)
                xc_low(g, 2)
                y_out(g - 1, 1)
                y_out(g - 1, 2)
            for j in range(3):
                y_out(3, j)
            add_squares("ffn0")
            add_squares("kv")

            for m in STEPS:
                if 2 <= m + 2 < PAIRS_H:
                    pool.wait_ge(qhi_ready, m + 3)
                    nc.gpsimd.tensor_tensor(q_lo[:, m % 2, :], q[:, m % 2, :], q_hi[:, m % 2, :].bitcast(F32),
                                            ALU.subtract).then_inc(qlo_ready, 1)
                if m + 4 < PAIRS_H + 3:
                    t = T_Q + m + 4
                    pool.wait_ge(w_lo_ready, CREDIT + t)
                    pool.wait_ge(w_hi_ready, t + 1)
                    nc.gpsimd.tensor_tensor(w_lo[:, t % 4, :], raw[:, t % 4, :], w_hi[:, t % 4, :].bitcast(F32),
                                            ALU.subtract).then_inc(w_lo_ready, 1)

            add_squares("ffn1")

        @block.scalar
        def _(act):
            landed = [0, 0, 0, 0]

            def split_hi(t, slot, raw_slot, count, cols):
                act.wait_ge(raw_landed[raw_slot], 16 * count)
                act.wait_ge(tiles_done, CREDIT + t - 4 + 1)
                nc.scalar.copy(w_hi[:, slot, 0:cols], raw[:, raw_slot, 0:cols]).then_inc(w_hi_ready, 1)

            def split_ri(t, g, slot, which):
                act.wait_ge(ri_landed[which], 96 * (g + 1))
                act.wait_ge(tiles_done, CREDIT + t - 4 + 1)
                nc.scalar.copy(w_hi[:, slot, 0:RI_COLS], ri_raw[:, which, :]).then_inc(w_hi_ready, 1)

            def prep(k, stage, gain_col, dst_hi, squares=True):
                nc.scalar.mul(dst_hi[:, k, :], h[:, k, :], gains[:, gain_col + k:gain_col + k + 1]).then_inc(xhi_ready, 1)
                if squares:
                    n = DC * SQS[stage] + k
                    if n >= 2:
                        act.wait_ge(sq_used, n - 1)
                    nc.scalar.activation(sq[:, k % 2, :], h[:, k, :], ACT.Square).then_inc(sq_ready, 1)

            def root_of_mean(norm):
                act.wait_ge(stat_ready, NORM[norm] + 1)
                nc.scalar.activation(root_t[:, :], stat_t, ACT.Sqrt, bias=eps[:, 0:1], scale=1.0 / D)\
                    .then_inc(std_ready, 1)

            def keep_rstd(norm):
                act.wait_ge(spread_ready, NORM[norm] + 1)
                nc.scalar.copy(rstd[:, :], stat).then_inc(rstd_ready, 1)

            act.sem_inc(ri_free, 6)
            act.sem_inc(mix_free, 2)

            act.wait_ge(lam_abs, 1)
            nc.scalar.activation(sp_t[:, 1, :], sp_t[:, 0, :], ACT.Exp, scale=-1.0).then_inc(lam_exp, 1)

            act.wait_ge(gains_ready, 1)
            for k in range(DC):
                act.wait_ge(xt_ready, k + 1)
                nc.scalar.copy(h[:, k, :], banks[4 + k % 2][:, :]).then_inc(h_copied, 1)
                act.wait_ge(h_copied, k + 1)
                nc.scalar.mul(x_hi[:, k, :], h[:, k, :], gains[:, G_MIX_PRE + k:G_MIX_PRE + k + 1]).then_inc(xhi_ready, 1)
                if k >= 2:
                    act.wait_ge(sq_used, k - 1)
                nc.scalar.activation(sq[:, k % 2, :], h[:, k, :], ACT.Square).then_inc(sq_ready, 1)
                if k == 0:
                    for s in range(3):
                        split_hi(s, s, s, 1, W_COLS)
                if k == 3:
                    split_hi(3, 3, 3, 1, W_COLS)
            act.wait_ge(params_ready, 1)
            root_of_mean("mix")
            keep_rstd("mix")

            def roots(g):
                act.wait_ge(ri_free, 6 + 6 * g + 3)
                for j in range(3):
                    c = 3 * g + j
                    nc.scalar.activation(e_u[j], t_u[:, j, :], ACT.Exp, bias=sp4[:, bass.ds(c, 1)],
                                         scale=sp4[:, bass.ds(c, 1)])
                    nc.scalar.activation(t_u[:, j, :], t_u[:, j, :], ACT.Tanh, bias=sp2[:, bass.ds(c, 1)],
                                         scale=sp2[:, bass.ds(c, 1)]).then_inc(te_ready, 1)
                act.wait_ge(te_ready, 3 * g + 3)
                for j in range(3):
                    nc.scalar.activation(root[:, j, :], t_u[:, j, :], ACT.Sqrt, scale=0.25).then_inc(roots_ready, 1)

            def y_high(g, j):
                c = 3 * g + j
                act.wait_ge(y_ready, c + 1)
                nc.scalar.copy(y_hi[:, bass.ds(c, 1), :].rearrange("p o n -> p (o n)"), gate[:, j, :])\
                    .then_inc(yhi_ready, 1)

            def group(g, first=False):
                t = T_IN + 8 * g
                fills = [2 * g + 1, 2 * g + 1, g + 1, g + 1, 2 * g + 2, 2 * g + 2, None, None, 2 * g + 3, 2 * g + 3, g + 2]

                def ahead(p):
                    p += 3
                    if p in (R_TILE, I_TILE):
                        split_ri(t + p, g, p % 4, p - R_TILE)
                    else:
                        split_hi(t + p, p % 4, p % 4, fills[p], W_COLS)

                def xc_high(j):
                    act.wait_ge(conv_ready, 3 * g + j + 1)
                    nc.scalar.copy(xc_hi[:, j, :], xc[:, j, :]).then_inc(xchi_ready, 1)

                if not first:
                    ahead(0)
                    roots(g - 1)
                ahead(1)
                xc_high(0)
                if not first:
                    y_high(g - 1, 0)
                ahead(2)
                xc_high(1)
                ahead(3)
                xc_high(2)
                if not first:
                    y_high(g - 1, 1)
                    y_high(g - 1, 2)
                for p in range(4, 7):
                    ahead(p)
                act.wait_ge(gate_ready, 3 * g + 3)
                for j in range(3):
                    nc.scalar.activation(gate[:, j, :], gate[:, j, :], ACT.Gelu_apprx_tanh).then_inc(gelu_ready, 1)
                act.wait_ge(tiles_done, CREDIT + t + R_TILE + 1)
                for j in range(3):
                    nc.scalar.activation(t_u[:, j, :], banks[j][:, :], ACT.Tanh,
                                         bias=half_b[:, bass.ds(3 * g + j, 1)], scale=0.5).then_inc(ri_free, 1)
                ahead(7)
                act.wait_ge(tiles_done, CREDIT + t + I_TILE + 1)
                for j in range(3):
                    nc.scalar.activation(t_i[:, j, :], banks[3 + j][:, :], ACT.Tanh,
                                         bias=half_b[:, bass.ds(RC + 3 * g + j, 1)], scale=0.5).then_inc(ri_free, 1)

            group(0, first=True)
            with act.Fori(0, 3) as i:
                group(i + 1)

            def out_chunk(stage, m, bank, gain_col, t):
                n = DC * OUTS[stage] + m
                act.wait_ge(tiles_done, CREDIT + t + 1)
                act.wait_ge(sum_ready, n + 1)
                nc.scalar.activation(sq[:, 0, :], banks[bank][:, :], ACT.Square).then_inc(out_squared, 1)
                nc.scalar.mul(mix[:, bass.ds(m, 1), :].rearrange("p o n -> p (o n)"), banks[bank][:, :],
                              gains[:, bass.ds(gain_col + m, 1)]).then_inc(mix_free, 1)

            def w_out(i, last=False):
                for s in range(8):
                    slot = (s + 3) % 4
                    split_hi(T_OUT + 8 * i + s + 3, slot, slot, (8 if slot < 2 else 4) + 2 * i + (s + 3) // 4 + 1,
                             W_COLS if last and s >= 5 else 6 * P)
                    if not last and s == 0:
                        roots(3)
                    if not last and 1 <= s < 4:
                        y_high(3, s - 1)
                    if s >= 4:
                        out_chunk("mix0", 4 * i + s - 4, s - 4, G_MIX_POST, T_OUT + 8 * i + s)

            w_out(0)
            w_out(1, last=True)
            base = [8 + 4, 8 + 4, 4 + 4, 4 + 4]

            def residual(stage, norm, gain_col, dst_hi=None, after=lambda k: None):
                root_of_mean(norm)
                for k in range(DC):
                    if stage == "out":
                        continue
                    act.wait_ge(h_ready, DC * RES[stage] + k + 1)
                    prep(k, stage, gain_col, dst_hi)
                    after(k)

            def ffn(f, base):
                def fourth(k):
                    if k == 3:
                        split_hi(T_GU[f] + 3, 3, 3, base[3] + 1, W_COLS)

                residual(f"ffn{f}", f"post_mix{f}", G_FFN_PRE + DC * f, x_hi, fourth)
                split_hi(T_GU[f] + 4, 0, 0, base[0] + 2, W_COLS)
                root_of_mean(f"ffn{f}")
                keep_rstd(f"ffn{f}")

                def pairs(i, first=False, last=False):
                    for a in range(2):
                        n = FC * f + 2 * i + a
                        for s in (2 * a, 2 * a + 1):
                            if first and s < 2:
                                continue
                            slot = (s + 3) % 4
                            cols = DN_K[slot] * P if last and s > 0 else W_COLS
                            split_hi(T_GU[f] + 4 * i + s + 3, slot, slot, base[slot] + i + (2 if s > 0 else 1), cols)
                        act.wait_ge(g_ready, n + 1)
                        nc.scalar.activation(scratch[:, a, :], scratch[:, a, :], ACT.Silu).then_inc(silu_ready, 1)
                        act.wait_ge(hid_ready, n + 1)
                        nc.scalar.copy(hid_hi[:, bass.ds(2 * i + a, 1), :].rearrange("p o n -> p (o n)"),
                                       scratch[:, 2 + a, :]).then_inc(hidhi_ready, 1)

                pairs(0, first=True)
                with act.Fori(0, FC // 2 - 2) as i:
                    pairs(i + 1)
                pairs(FC // 2 - 1, last=True)
                b2 = [n + FC // 2 for n in base]

                def down(m, par, last=False):
                    for s in range(4):
                        slot = (s + 3) % 4
                        cols = DN_K[slot] * P
                        if last and s > 0:
                            cols = 4 * P if f == 0 else 0
                        if cols:
                            split_hi(T_DN[f] + 4 * m + s + 3, slot, slot, b2[slot] + m + (2 if s > 0 else 1), cols)
                    out_chunk(f"ffn{f}", m, 4 + par, G_FFN_POST + DC * f, T_DN[f] + 4 * m + 3)

                def two(i, last=False):
                    down(2 * i, 0)
                    down(2 * i + 1, 1, last)

                with act.Fori(0, DC // 2 - 1) as i:
                    two(i)
                two(DC // 2 - 1, last=True)
                return [n + DC for n in b2]

            base = ffn(0, base)

            split_hi(T_KV + 3, 3, 3, base[3] + 1, 4 * P)

            def first_queries(k):
                if k >= 6:
                    split_hi(T_Q + k - 6, k - 6, k - 6, base[k - 6] + 3, W_COLS)

            residual("kv", "post_ffn0", G_KV, xkv_hi, first_queries)
            base = [n + 1 for n in base]
            for k in range(DC):
                nc.scalar.mul(x_hi[:, k, :], h[:, k, :], gains[:, G_MIX_PRE + DC + k:G_MIX_PRE + DC + k + 1])\
                    .then_inc(xhi_ready, 1)
            root_of_mean("kv")
            split_hi(T_Q + 2, 2, 2, base[2] + 2, W_COLS)
            keep_rstd("kv")
            act.wait_ge(kv_read, 1)
            nc.scalar.copy(k_hi[:, :], kv[:, 0, :]).then_inc(khi_ready, 1)
            act.wait_ge(v_turned, 1)
            nc.scalar.copy(v_hi[:, :, :], banks[3][:, :].rearrange("p (j n) -> p j n", n=P)).then_inc(vhi_ready, 1)
            nc.scalar.copy(va_hi[0:HD, 1:TC, :], banks[2][0:HD, P:S].rearrange("p (j n) -> p j n", n=P))\
                .then_inc(vhi_ready, 1)

            def q_high(m):
                act.wait_ge(q_read, m + 1)
                nc.scalar.copy(q_hi[:, m % 2, :], q[:, m % 2, :]).then_inc(qhi_ready, 1)

            def exponentials(m, js):
                if js[0] == 0:
                    act.wait_ge(max_ready, m + 1)
                for j in js:
                    c0 = CHUNK if j == 0 else 0
                    for g in range(2):
                        n = 2 * j + g
                        nc.scalar.activation(s_sb[:, m % 2, j, g, c0:], s_sb[:, m % 2, j, g, c0:], ACT.Exp,
                                             bias=sm[:, m % 2, 1, n:n + 1], accum_out=sm[:, m % 2, 3, n:n + 1])
                if js[-1] == TC - 1:
                    nc.scalar.activation(sm[:, m % 2, 4, :], sm[:, m % 2, 2, :], ACT.Exp).then_inc(p_exp, 1)

            def p_high(n):
                act.wait_ge(pt_ready, n + 1)
                if n % TC > 0:
                    nc.scalar.copy(p_hi[0:HD, n % 2, 2 * P:], banks[2 + n % 2][0:HD, 2 * P:])
                nc.scalar.copy(p_hi[:, n % 2, 0:2 * P], banks[2 + n % 2][:, 0:2 * P]).then_inc(phi_ready, 1)

            def o_high(m, half):
                act.wait_ge(o_ready, 2 * m + half + 1)
                js = slice(2 * half, 2 * half + 2)
                for g in range(2):
                    rows = slice(HD * g, HD * g + HD)
                    ins = nc.scalar.copy(o_hi[rows, m, :].rearrange("p (j n) -> p j n", n=P)[:, js, :],
                                         o_ps[rows, js, g, :])
                ins.then_inc(ohi_ready, 1)

            q_high(0)
            q_high(1)
            for m in STEPS:
                for j in range(TC):
                    if 0 <= TC * m + j - 4 < TC * PAIRS_H:
                        p_high(TC * m + j - 4)
                    if j == 0 and 2 <= m + 2 < PAIRS_H:
                        q_high(m + 2)
                    if j == 0 and m + 4 < PAIRS_H + 3:
                        t = m + 4
                        split_hi(T_Q + t, t % 4, t % 4, base[t % 4] + 2 * (t // 4 + 1), W_COLS)
                    if j in (1, 2) and 0 <= m < PAIRS_H:
                        exponentials(m, range(2 * j - 2, 2 * j))
                    if j == 3 and 0 <= m < PAIRS_H:
                        act.wait_ge(den_ready, m + 1)
                        for n in range(TC):
                            c0 = CHUNK if n == 0 else 0
                            ins = nc.scalar.mul(s_sb[:, m % 2, n, 1, c0:], s_sb[:, m % 2, n, 1, c0:],
                                                sm[:, m % 2, 5, 2 * n + 1:2 * n + 2])
                        ins.then_inc(p1_ready, 1)
                    if o_half(m, j):
                        o_high(*o_half(m, j))
            base = [n + 4 for n in base]

            def w_o(i, last=False):
                for s in range(4):
                    slot = (s + 3) % 4
                    t = T_O + 4 * i + s + 3
                    if last and s >= 1:
                        split_hi(t, slot, slot, base[slot] + 4 + 1, W_COLS)
                    else:
                        split_hi(t, slot, slot, base[slot] + 2 * i + (4 if s >= 1 else 2), W_COLS)
                    out_chunk("mix1", 4 * i + s, 4 + s % 2, G_MIX_POST + DC, T_O + 4 * i + s)

            w_o(0)
            w_o(1, last=True)
            base = [n + 4 for n in base]
            base = ffn(1, base)
            residual("out", "post_ffn1", None)
            for k in range(DC):
                act.wait_ge(ot_ready, k + 1)
                nc.scalar.copy(o_tok[:, k, :], banks[4 + k % 2][:, :]).then_inc(otok_ready, 1)

        @block.vector
        def _(dve):
            v = nc.vector
            steps = Count(dve_steps)

            def then(ins):
                dve.wait_ge(dve_steps, steps.inc(ins))

            def split_lo(t, slot, raw_slot, cols):
                dve.wait_ge(w_hi_ready, t + 1)
                v.tensor_tensor(w_lo[:, slot, 0:cols], raw[:, raw_slot, 0:cols], w_hi[:, slot, 0:cols].bitcast(F32),
                                ALU.subtract).then_inc(w_lo_ready, 1)

            def split_lo_ri(t, slot, which):
                dve.wait_ge(w_hi_ready, t + 1)
                v.tensor_tensor(w_lo[:, slot, 0:RI_COLS], ri_raw[:, which, :], w_hi[:, slot, 0:RI_COLS].bitcast(F32),
                                ALU.subtract).then_inc(w_lo_ready, 1)

            def input_lo(k, stage, gain_col, hi, lo):
                dve.wait_ge(xhi_ready, DC * PREP[stage] + k + 1)
                v.scalar_tensor_tensor(out=lo[:, k, :], in0=h[:, k, :], scalar=gains[:, gain_col + k:gain_col + k + 1],
                                       in1=hi[:, k, :].bitcast(F32), op0=ALU.mult, op1=ALU.subtract).then_inc(x_ready, 1)

            def reciprocal_of_root(norm):
                dve.wait_ge(std_ready, NORM[norm] + 1)
                then(v.reciprocal(rstd_t[:, :], root_t[:, :]))
                for c in range(TC):
                    ins = v.tensor_scalar(diag[:, c * P:(c + 1) * P], ident[:, :], rstd_t[:, c:c + 1], None, ALU.mult)
                ins.then_inc(diag_ready, 1)

            def rstd_kept(norm):
                dve.wait_ge(rstd_ready, SQS[norm] + 1)

            dve.sem_inc(w_lo_ready, CREDIT)
            dve.sem_inc(gu_free, 2)
            dve.sem_inc(sum_ready, 1)

            dve.wait_ge(rows_ready, 2)
            v.tensor_copy(gains[:, :], banks[0][:, 0:G_ROWS])
            v.tensor_copy(rnn[:, :], banks[1][:, 0:R_ROWS]).then_inc(gains_ready, 1)
            dve.wait_ge(gains_ready, 1)
            lam = rnn[:, R_LAM:R_LAM + RC]
            v.tensor_scalar(sp_t[:, 3, :], lam, -1.0, 0.0, ALU.mult, ALU.max)
            then(v.tensor_scalar(sp_t[:, 2, :], lam, -1.0, None, ALU.mult))
            v.tensor_tensor(sp_t[:, 0, :], sp_t[:, 2, :], lam, ALU.max).then_inc(lam_abs, 1)

            def parameters():
                v.tensor_scalar(half_b[:, :], rnn[:, R_BRG:R_BRG + 2 * RC], 0.5, None, ALU.mult)
                dve.wait_ge(lam_exp, 1)
                then(v.tensor_scalar(sp_t[:, 0, :], sp_t[:, 1, :], 2.0, None, ALU.add))
                then(v.reciprocal(sp_t[:, 0, :], sp_t[:, 0, :]))
                then(v.tensor_tensor(sp_t[:, 1, :], sp_t[:, 1, :], sp_t[:, 0, :], ALU.mult))
                then(v.tensor_tensor(sp_t[:, 2, :], sp_t[:, 1, :], sp_t[:, 1, :], ALU.mult))
                then(v.tensor_scalar(sp_t[:, 0, :], sp_t[:, 2, :], 1.0 / 15, 1.0 / 13, ALU.mult, ALU.add))
                for n in (11, 9, 7, 5, 3, 1):
                    then(v.tensor_tensor(sp_t[:, 0, :], sp_t[:, 0, :], sp_t[:, 2, :], ALU.mult))
                    then(v.tensor_scalar(sp_t[:, 0, :], sp_t[:, 0, :], 1.0 / n, None, ALU.add))
                then(v.tensor_tensor(sp_t[:, 0, :], sp_t[:, 0, :], sp_t[:, 1, :], ALU.mult))
                then(v.tensor_scalar(sp_t[:, 0, :], sp_t[:, 0, :], 2.0, None, ALU.mult))
                then(v.tensor_tensor(sp_t[:, 0, :], sp_t[:, 0, :], sp_t[:, 3, :], ALU.add))
                v.tensor_scalar(sp2[:, :], sp_t[:, 0, :], 2.0, None, ALU.mult)
                v.tensor_scalar(sp4[:, :], sp_t[:, 0, :], -4.0, None, ALU.mult)
                dve.wait_ge(params_landed, 16 * 11)
                for j in range(TC):
                    v.tensor_copy(sinks[:, :, j, :], sinks_in[:, :].rearrange("p (g m) -> p m g", g=2))
                dve.wait_ge(consts_ready, 1)
                then(v.tensor_copy(dist[:, :], dist_i[:, :]))
                then(v.tensor_scalar(rstd[:, 0:3 * CHUNK], dist[:, :], -1.0, None, ALU.mult))
                then(v.tensor_tensor(dist[:, :], dist[:, :], rstd[:, 0:3 * CHUNK], ALU.max))
                v.memset(dist[0:CHUNK, 2 * CHUNK:3 * CHUNK], MASKED)
                v.memset(dist[CHUNK:P, 0:CHUNK], MASKED).then_inc(params_ready, 1)

            for k in range(DC):
                input_lo(k, "mix", G_MIX_PRE, x_hi, x_lo)
                if k == 0:
                    for s in range(3):
                        split_lo(s, s, s, W_COLS)
                if k == 3:
                    split_lo(3, 3, 3, W_COLS)
                if k == DC - 1:
                    parameters()
            reciprocal_of_root("mix")
            rstd_kept("mix")

            def with_gate(g):
                for j in range(3):
                    dve.wait_ge(ri_free, 6 + 6 * g + 3 + j + 1)
                    v.scalar_tensor_tensor(out=t_i[:, j, :], in0=t_i[:, j, :], scalar=1.0, in1=xc[:, j, :],
                                           op0=ALU.add, op1=ALU.mult)

            def recurrence(g, j):
                c = 3 * g + j
                dve.wait_ge(roots_ready, c + 1)
                v.scalar_tensor_tensor(out=t_u[:, j, :], in0=e_u[j], scalar=1.0, in1=t_u[:, j, :],
                                       op0=ALU.add, op1=ALU.mult)
                then(v.scalar_tensor_tensor(out=root[:, j, :], in0=e_u[j], scalar=1.0, in1=root[:, j, :],
                                            op0=ALU.add, op1=ALU.mult))
                v.tensor_scalar(t_u[:, j, :], t_u[:, j, :], -1.0, 1.0, ALU.mult, ALU.add)
                then(v.tensor_tensor(root[:, j, :], root[:, j, :], t_i[:, j, :], ALU.mult))
                v.tensor_tensor_scan(t_i[:, j, :], t_u[:, j, :], root[:, j, :], 0.0, ALU.mult, ALU.add)\
                    .then_inc(state_ready, 1)

            def group(g, first=False):
                t = T_IN + 8 * g

                def ahead(p):
                    p += 3
                    if p in (R_TILE, I_TILE):
                        split_lo_ri(t + p, p % 4, p - R_TILE)
                    else:
                        split_lo(t + p, p % 4, p % 4, W_COLS)

                def conv(j):
                    c = 3 * g + j
                    dve.wait_ge(tiles_done, CREDIT + t + j + 1)
                    if j > 0:
                        dve.wait_ge(conv_ready, c)
                    then(v.tensor_tensor(xp[:, 4:S + 4], banks[j][:, :], rstd[:, :], ALU.mult))
                    then(v.tensor_scalar(xc[:, j, :], xp[:, 1:S + 1], rnn[:, bass.ds(R_CONV_W + c, 1)],
                                         rnn[:, bass.ds(R_CONV_B + c, 1)], ALU.mult, ALU.add))
                    for k in range(1, 4):
                        ins = v.scalar_tensor_tensor(out=xc[:, j, :], in0=xp[:, 1 + k:S + 1 + k],
                                                     scalar=rnn[:, bass.ds(R_CONV_W + RC * k + c, 1)], in1=xc[:, j, :],
                                                     op0=ALU.mult, op1=ALU.add)
                        if k < 3:
                            then(ins)
                        else:
                            ins.then_inc(conv_ready, 1)

                def gate_in(j):
                    dve.wait_ge(tiles_done, CREDIT + t + 3 + j + 1)
                    v.tensor_tensor(gate[:, j, :], banks[3 + j][:, :], rstd[:, :], ALU.mult).then_inc(gate_ready, 1)

                if not first:
                    with_gate(g - 1)
                    ahead(0)
                for j in range(3):
                    conv(j)
                    if j == 0 and not first:
                        recurrence(g - 1, 0)
                    ahead(j + 1)
                if not first:
                    recurrence(g - 1, 1)
                    recurrence(g - 1, 2)
                for j in range(3):
                    ahead(4 + j)
                    if j == 0 and not first:
                        dve.wait_ge(ylo_ready, 3 * g)
                    gate_in(j)
                ahead(7)

            group(0, first=True)
            repeat(dve, 3, steps, 3 * 4 + 3 * 2, lambda i: group(i + 1))
            with_gate(3)

            def sum_squares(stage, m):
                n = DC * OUTS[stage] + m
                dve.wait_ge(out_squared, n + 1)
                v.tensor_tensor(sq_sum, sq_sum, sq[:, 0, :], ALU.add).then_inc(sum_ready, 1)

            def clear_sum():
                then(v.memset(sq_sum, 0.0))

            def w_out(i, last=False):
                for s in range(8):
                    slot = (s + 3) % 4
                    split_lo(T_OUT + 8 * i + s + 3, slot, slot, W_COLS if last and s >= 5 else 6 * P)
                    if not last and s < 3:
                        recurrence(3, s)
                    if not last and s == 3:
                        clear_sum()
                    if s >= 4:
                        sum_squares("mix0", 4 * i + s - 4)

            w_out(0)
            w_out(1, last=True)

            def residual(stage, norm, gain_col=None, hi=None, lo=None, after=lambda k: None):
                reciprocal_of_root(norm)

                def scaled(k):
                    return steps.inc(v.tensor_tensor(mix[:, k, :], mix[:, k, :], stat, ALU.mult))

                dve.wait_ge(spread_ready, NORM[norm] + 1)
                dve.wait_ge(mix_free, 2 + DC * (NORM[norm] // 2 + 1))
                done = scaled(0)
                for k in range(DC):
                    mine, done = done, scaled(k + 1) if k + 1 < DC else 0
                    dve.wait_ge(dve_steps, mine)
                    v.tensor_tensor(h[:, k, :], h[:, k, :], mix[:, k, :], ALU.add).then_inc(h_ready, 1)
                    if hi is not None and k > 0:
                        input_lo(k - 1, stage, gain_col, hi, lo)
                        after(k - 1)
                if hi is not None:
                    input_lo(DC - 1, stage, gain_col, hi, lo)
                    after(DC - 1)

            def ffn(f):
                def fourth(k):
                    if k == 3:
                        split_lo(T_GU[f] + 3, 3, 3, W_COLS)

                residual(f"ffn{f}", f"post_mix{f}", G_FFN_PRE + DC * f, x_hi, x_lo, fourth)
                split_lo(T_GU[f] + 4, 0, 0, W_COLS)
                reciprocal_of_root(f"ffn{f}")
                rstd_kept(f"ffn{f}")

                def pairs(i, first=False, last=False):
                    for a in range(2):
                        n = FC * f + 2 * i + a
                        for s in (2 * a, 2 * a + 1):
                            if first and s < 2:
                                continue
                            slot = (s + 3) % 4
                            split_lo(T_GU[f] + 4 * i + s + 3, slot, slot, DN_K[slot] * P if last and s > 0 else W_COLS)
                        dve.wait_ge(tiles_done, CREDIT + T_GU[f] + 4 * i + 2 * a + 1 + 1)
                        v.tensor_tensor(scratch[:, a, :], banks[2 * a][:, :], rstd[:, :], ALU.mult).then_inc(g_ready, 1)
                        v.tensor_tensor(scratch[:, 2 + a, :], banks[2 * a + 1][:, :], rstd[:, :], ALU.mult)\
                            .then_inc(gu_free, 1)
                        dve.wait_ge(gu_free, 2 + n + 1)
                        dve.wait_ge(silu_ready, n + 1)
                        v.tensor_tensor(scratch[:, 2 + a, :], scratch[:, a, :], scratch[:, 2 + a, :], ALU.mult)\
                            .then_inc(hid_ready, 1)
                        dve.wait_ge(hidhi_ready, n + 1)
                        at_m = bass.ds(2 * i + a, 1)
                        v.tensor_tensor(hid_lo[:, at_m, :].rearrange("p o n -> p (o n)"), scratch[:, 2 + a, :],
                                        hid_hi[:, at_m, :].rearrange("p o n -> p (o n)").bitcast(F32),
                                        ALU.subtract).then_inc(hidlo_ready, 1)

                pairs(0, first=True)
                with dve.Fori(0, FC // 2 - 2) as i:
                    pairs(i + 1)
                pairs(FC // 2 - 1, last=True)
                dve.wait_ge(hidlo_ready, FC * (f + 1))
                clear_sum()

                def down(m, last=False):
                    for s in range(4):
                        slot = (s + 3) % 4
                        cols = DN_K[slot] * P
                        if last and s > 0:
                            cols = 4 * P if f == 0 else 0
                        if cols:
                            split_lo(T_DN[f] + 4 * m + s + 3, slot, slot, cols)
                    sum_squares(f"ffn{f}", m)

                with dve.Fori(0, DC - 1) as m:
                    down(m)
                down(DC - 1, last=True)

            ffn(0)

            split_lo(T_KV + 3, 3, 3, 4 * P)

            def first_queries(k):
                if k >= 6:
                    split_lo(T_Q + k - 6, k - 6, k - 6, W_COLS)

            residual("kv", "post_ffn0", G_KV, xkv_hi, xkv_lo, first_queries)
            for k in range(DC):
                input_lo(k, "q", G_MIX_PRE + DC, x_hi, x_lo)
            reciprocal_of_root("kv")
            split_lo(T_Q + 2, 2, 2, W_COLS)
            rstd_kept("kv")
            dve.wait_ge(tiles_done, CREDIT + T_KV + 3 + 1)
            v.tensor_tensor(kv[:, 1, :], banks[1][:, :], rstd[:, :], ALU.mult)
            v.tensor_tensor(kv[:, 0, :], banks[0][:, :], rstd[:, :], ALU.mult).then_inc(kv_read, 1)
            dve.wait_ge(khi_ready, 1)
            v.tensor_tensor(k_lo[:, :], kv[:, 0, :], k_hi[:, :].bitcast(F32), ALU.subtract)
            dve.wait_ge(vhi_ready, 2)
            v.tensor_tensor(v_lo[:, :, :], banks[3][:, :].rearrange("p (j n) -> p j n", n=P), v_hi[:, :, :].bitcast(F32),
                            ALU.subtract)
            v.tensor_tensor(va_lo[0:HD, 1:TC, :], banks[2][0:HD, P:S].rearrange("p (j n) -> p j n", n=P),
                            va_hi[0:HD, 1:TC, :].bitcast(F32), ALU.subtract).then_inc(v_ready, 1)
            for b in range(2):
                then(v.memset(s_sb[:, b, 0, :, 0:CHUNK], -1e30))

            def q_in(m):
                dve.wait_ge(tiles_done, CREDIT + T_Q + m + 1)
                v.scalar_tensor_tensor(out=q[:, m % 2, :], in0=q_ps[Q_BANK[m]], scalar=HD ** -0.5, in1=rstd[:, :],
                                       op0=ALU.mult, op1=ALU.mult).then_inc(q_read, 1)

            def q_low(m):
                dve.wait_ge(qhi_ready, m + 1)
                v.tensor_tensor(q_lo[:, m % 2, :], q[:, m % 2, :], q_hi[:, m % 2, :].bitcast(F32), ALU.subtract)\
                    .then_inc(qlo_ready, 1)

            def biased(m, j):
                dve.wait_ge(s_ready, TC * m + j + 1)
                c0 = CHUNK if j == 0 else 0
                for g in range(2):
                    head = m + PAIRS_H * g
                    ins = v.scalar_tensor_tensor(out=s_sb[:, m % 2, j, g, c0:], in0=dist[:, c0:],
                                                 scalar=slopes[:, head:head + 1], in1=banks[g][:, c0:3 * CHUNK],
                                                 op0=ALU.mult, op1=ALU.add)
                ins.then_inc(s_read, 1)

            def row_max(m):
                b = m % 2
                dve.wait_ge(s_read, TC * (m + 1))
                then(v.tensor_reduce(sm[:, b, 0, :], s_sb[:, b, :, :, :].rearrange("p j g w -> p (j g) w"), AX.X, ALU.max))
                sink = sinks[:, m, :, :].rearrange("p j g -> p (j g)")
                then(v.tensor_tensor(sm[:, b, 0, :], sm[:, b, 0, :], sink, ALU.max))
                v.tensor_scalar(sm[:, b, 1, :], sm[:, b, 0, :], -1.0, None, ALU.mult)
                v.tensor_tensor(sm[:, b, 2, :], sink, sm[:, b, 0, :], ALU.subtract).then_inc(max_ready, 1)

            def normalise(m):
                b = m % 2
                dve.wait_ge(p_exp, m + 1)
                then(v.tensor_tensor(sm[:, b, 5, :], sm[:, b, 3, :], sm[:, b, 4, :], ALU.add))
                v.reciprocal(sm[:, b, 5, :], sm[:, b, 5, :]).then_inc(den_ready, 1)
                dve.wait_ge(den_ready, m + 1)
                for n in range(TC):
                    c0 = CHUNK if n == 0 else 0
                    ins = v.tensor_scalar(s_sb[:, b, n, 0, c0:], s_sb[:, b, n, 0, c0:], sm[:, b, 5, 2 * n:2 * n + 1],
                                          None, ALU.mult)
                ins.then_inc(p0_ready, 1)

            def p_low(n):
                dve.wait_ge(phi_ready, n + 1)
                bank = banks[2 + n % 2]
                if n % TC > 0:
                    v.tensor_tensor(p_lo[0:HD, n % 2, 2 * P:], bank[0:HD, 2 * P:], p_hi[0:HD, n % 2, 2 * P:].bitcast(F32),
                                    ALU.subtract)
                v.tensor_tensor(p_lo[:, n % 2, 0:2 * P], bank[:, 0:2 * P], p_hi[:, n % 2, 0:2 * P].bitcast(F32),
                                ALU.subtract).then_inc(plo_ready, 1)

            def o_low(m, half):
                dve.wait_ge(ohi_ready, 2 * m + half + 1)
                js = slice(2 * half, 2 * half + 2)
                for g in range(2):
                    rows = slice(HD * g, HD * g + HD)
                    lo = o_lo[rows, m, :].rearrange("p (j n) -> p j n", n=P)[:, js, :]
                    hi = o_hi[rows, m, :].rearrange("p (j n) -> p j n", n=P)[:, js, :]
                    ins = v.tensor_tensor(lo, o_ps[rows, js, g, :], hi.bitcast(F32), ALU.subtract)
                ins.then_inc(olo_ready, 1)

            q_in(0)
            q_in(1)
            q_low(0)
            q_low(1)
            for m in STEPS:
                for j in range(TC):
                    if j == 0 and 2 <= m + 2 < PAIRS_H:
                        q_in(m + 2)
                    if j == 3 and 0 <= m < PAIRS_H:
                        normalise(m)
                    if m + 1 < PAIRS_H:
                        biased(m + 1, j)
                    if 0 <= TC * m + j - 4 < TC * PAIRS_H:
                        p_low(TC * m + j - 4)
                    if j == 0 and 0 <= m < PAIRS_H:
                        row_max(m)
                    if o_half(m, j):
                        o_low(*o_half(m, j))
            clear_sum()
            dve.wait_ge(w_lo_ready, CREDIT + T_O + 3)

            def w_o(i, last=False):
                for s in range(4):
                    slot = (s + 3) % 4
                    split_lo(T_O + 4 * i + s + 3, slot, slot, W_COLS)
                    sum_squares("mix1", 4 * i + s)

            w_o(0)
            w_o(1, last=True)
            ffn(1)
            residual("out", "post_ffn1")

        @block.tensor
        def _(pe):
            def products(ps, hi_w, lo_w, hi_x, lo_x, first, final):
                nc.tensor.matmul(ps, hi_w, hi_x, start=first, stop=False)
                nc.tensor.matmul(ps, hi_w, lo_x, start=False, stop=False)
                return nc.tensor.matmul(ps, lo_w, hi_x, start=False, stop=final)

            def tile(ps, slot, at, k, first, final, hi=x_hi, lo=x_lo):
                cols = slice(at * P, at * P + P)
                return products(ps, w_hi[:, slot, cols], w_lo[:, slot, cols], hi[:, k, :], lo[:, k, :], first, final)

            def tile_ready(t):
                pe.wait_ge(w_lo_ready, CREDIT + t + 1)

            def sum_over_features():
                for c in range(TC):
                    ins = nc.tensor.matmul(stat[:, c:c + 1], sq_sum[:, c * P:(c + 1) * P], ones[:, 0:1], start=c == 0,
                                           stop=c == TC - 1, skip_group_check=True)
                ins.then_inc(stat_ready, 1)

            def sum_input(norm):
                pe.wait_ge(total_ready, SQS[norm] + 1)
                sum_over_features()

            def spread(norm):
                pe.wait_ge(diag_ready, NORM[norm] + 1)
                nc.tensor.matmul(stat, ones[:, :], diag, start=True, stop=True).then_inc(spread_ready, 1)

            pe.sem_inc(tiles_done, CREDIT)
            pe.wait_ge(consts_ready, 1)
            pe.wait_ge(params_landed, 16 * 11)
            nc.tensor.transpose(banks[0][:, 0:G_ROWS], g_rows[0:G_ROWS, :], ident[0:G_ROWS, 0:G_ROWS]).then_inc(rows_ready, 1)
            nc.tensor.transpose(banks[1][:, 0:R_ROWS], r_rows[0:R_ROWS, :], ident[0:R_ROWS, 0:R_ROWS]).then_inc(rows_ready, 1)
            for c in range(TC):
                pe.wait_ge(x_landed[c], 16)

            def turn_x(k):
                if k >= 2:
                    pe.wait_ge(h_copied, k - 1)
                for c in range(TC):
                    ins = nc.tensor.transpose(banks[4 + k % 2][:, c * P:(c + 1) * P], x_tok[:, c, k * P:(k + 1) * P],
                                              ident[:, :])
                ins.then_inc(xt_ready, 1)

            def block_gates(g):
                for which in range(2):
                    p = R_TILE + which
                    tile_ready(T_IN + 8 * g + p)
                    if which == 0:
                        pe.wait_ge(xc_ready, 3 * g + 3)
                    for m in range(3):
                        if which == 1:
                            pe.wait_ge(gate_ready, 3 * g + m + 1)
                        ks = RI_PAIRS[m]
                        for k in ks:
                            cols = slice(RI_AT[k] + P * m, RI_AT[k] + P * m + P)
                            ins = products(banks[3 * which + m][:, :], w_hi[:, p % 4, cols], w_lo[:, p % 4, cols],
                                           xc_hi[:, k, :], xc_lo[:, k, :], k == ks[0], k == ks[-1])
                    ins.then_inc(tiles_done, 1)

            def xg_tile(g, p, norm=None):
                tile_ready(T_IN + 8 * g + p)
                pe.wait_ge(ri_free, 6 * g + p + 1)
                if norm:
                    sum_input(norm)
                for k in range(DC):
                    ins = tile(banks[p][:, :], p % 4, k, k, k == 0, k == DC - 1)
                    if norm and k == 4:
                        spread(norm)
                ins.then_inc(tiles_done, 1)

            turn_x(0)
            turn_x(1)
            for k in range(DC):
                if k + 2 < DC:
                    turn_x(k + 2)
                pe.wait_ge(x_ready, k + 1)
                for p in range(3):
                    if k == 0:
                        tile_ready(p)
                    ins = tile(banks[p][:, :], p, k, k, k == 0, k == DC - 1)
                    if k == DC - 1:
                        ins.then_inc(tiles_done, 1)
            for p in range(3, 6):
                xg_tile(0, p, "mix" if p == 3 else None)
            block_gates(0)

            with pe.Fori(0, 3) as i:
                g = i + 1
                for p in range(6):
                    xg_tile(g, p)
                block_gates(g)

            def out_part(s, ks, i, first=False):
                for k in ks:
                    if first:
                        pe.wait_ge(ylo_ready, k + 1)
                    ins = tile(banks[s % 4][:, :], s % 4, k % 6, k, k == 0, k == RC - 1, y_hi, y_lo)
                if ks[-1] % 6 == 5:
                    ins.then_inc(tiles_done, 1)

            def w_out(i, first=False):
                for s in range(4):
                    m = 4 * i + s
                    tile_ready(T_OUT + 8 * i + s)
                    if first:
                        pe.wait_ge(ri_free, 6 + 6 * 3 + s + 1)
                    else:
                        pe.wait_ge(mix_free, 2 + m - 4 + 1)
                    out_part(s, range(6), i, first and s == 0)
                if first:
                    tile_ready(T_OUT + 4)
                    out_part(4, range(6, 9), i, True)
                    tile_ready(T_OUT + 5)
                    out_part(5, range(6, 9), i)
                    out_part(4, range(9, 12), i, True)
                    out_part(5, range(9, 12), i)
                for s in range(6 if first else 4, 8):
                    tile_ready(T_OUT + 8 * i + s)
                    out_part(s, range(6, 12), i)

            w_out(0, first=True)
            w_out(1)

            def sum_block(norm, stage):
                pe.wait_ge(sum_ready, 1 + DC * (OUTS[stage] + 1))
                sum_over_features()
                spread(norm)

            def ffn(f):
                sum_block(f"post_mix{f}", f"mix{f}")

                for k in range(DC):
                    pe.wait_ge(x_ready, DC * PREP[f"ffn{f}"] + k + 1)
                    for s in range(3):
                        if k == 0:
                            tile_ready(T_GU[f] + s)
                        ins = tile(banks[s][:, :], s, k, k, k == 0, k == DC - 1)
                        if k == DC - 1:
                            ins.then_inc(tiles_done, 1)
                sum_input(f"ffn{f}")
                tile_ready(T_GU[f] + 3)
                for k in range(DC):
                    ins = tile(banks[3][:, :], 3, k, k, k == 0, k == DC - 1)
                    if k == 4:
                        spread(f"ffn{f}")
                ins.then_inc(tiles_done, 1)

                def pair(n, a):
                    pe.wait_ge(gu_free, FC * f + n + 1)
                    for u in range(2):
                        tile_ready(T_GU[f] + 2 * n + u)
                        for k in range(DC):
                            ins = tile(banks[2 * a + u][:, :], 2 * a + u, k, k, k == 0, k == DC - 1)
                        ins.then_inc(tiles_done, 1)

                with pe.Fori(0, FC // 2 - 1) as i:
                    for a in range(2):
                        pair(2 * i + 2 + a, a)

                def down(m, par, first=False):
                    pe.wait_ge(mix_free, DC * OUTS[f"ffn{f}"] + m + 1)
                    for s in range(4):
                        tile_ready(T_DN[f] + 4 * m + s)
                        for n in range(DN_K[s]):
                            k = DN_AT[s] + n
                            if first:
                                pe.wait_ge(hidlo_ready, FC * f + k + 1)
                            ins = tile(banks[4 + par][:, :], s, n, k, k == 0, k == FC - 1, hid_hi, hid_lo)
                        ins.then_inc(tiles_done, 1)

                down(0, 0, first=True)
                down(1, 1)
                with pe.Fori(0, DC // 2 - 1) as i:
                    for a in range(2):
                        down(2 * i + 2 + a, a)

            ffn(0)

            sum_block("post_ffn0", "ffn0")
            for k in range(DC):
                pe.wait_ge(x_ready, DC * PREP["kv"] + k + 1)
                for u in range(2):
                    s = 2 * (k // 4) + u
                    if k % 4 == 0:
                        tile_ready(T_KV + s)
                    ins = tile(banks[u][:, :], s, k % 4, k, k == 0, k == DC - 1, xkv_hi, xkv_lo)
                    if k % 4 == 3:
                        ins.then_inc(tiles_done, 1)

            def turn_v():
                pe.wait_ge(kv_read, 1)
                for j in range(TC):
                    ins = nc.tensor.transpose(banks[3][:, j * P:(j + 1) * P], kv[:, 1, j * P:(j + 1) * P], ident[:, :])
                for j in range(1, TC):
                    ins = nc.tensor.transpose(banks[2][0:HD, j * P:(j + 1) * P], kv[:, 1, j * P - HD:j * P],
                                              ident[:, :])
                ins.then_inc(v_turned, 1)

            def q_chunk(m, ks):
                if ks[0] == 0:
                    tile_ready(T_Q + m)
                    if m >= 3:
                        pe.wait_ge(q_read, m)
                for k in ks:
                    if m == 0:
                        pe.wait_ge(x_ready, DC * PREP["q"] + k + 1)
                    ins = tile(q_ps[Q_BANK[m]], m % 4, k, k, k == 0, k == DC - 1)
                if ks[-1] == DC - 1:
                    ins.then_inc(tiles_done, 1)

            def scores(m, j):
                if j == 0:
                    pe.wait_ge(qlo_ready, m + 1)
                if m > 0 or j > 0:
                    pe.wait_ge(s_read, TC * m + j)
                c0 = CHUNK if j == 0 else 0
                keys = slice(j * P - CHUNK + c0, j * P + P)
                for g in range(2):
                    rows = slice(HD * g, HD * g + HD)
                    qs = slice(j * P, (j + 1) * P)
                    ins = products(banks[g][:, c0:3 * CHUNK], q_hi[rows, m % 2, qs], q_lo[rows, m % 2, qs],
                                   k_hi[rows, keys], k_lo[rows, keys], True, True)
                ins.then_inc(s_ready, 1)

            def turn(n):
                m, j, b = n // TC, n % TC, n // TC % 2
                if j == 0:
                    pe.wait_ge(p0_ready, m + 1)
                    pe.wait_ge(p1_ready, m + 1)
                if n >= 2:
                    pe.wait_ge(plo_ready, n - 1)
                bank = banks[2 + n % 2]
                for g in range(2):
                    ins = nc.tensor.transpose(bank[:, g * P:(g + 1) * P], s_sb[:, b, j, g, CHUNK:3 * CHUNK], ident[:, :])
                if j > 0:
                    for g in range(2):
                        ins = nc.tensor.transpose(bank[0:HD, (2 + g) * P:(3 + g) * P], s_sb[:, b, j, g, 0:CHUNK],
                                                  ident[:, :])
                ins.then_inc(pt_ready, 1)

            def values(n):
                m, j = n // TC, n % TC
                pe.wait_ge(plo_ready, n + 1)
                if m > 0 and j % 2 == 0:
                    pe.wait_ge(olo_ready, 2 * m - 1 + j // 2)
                o = o_ps[:, j, :, :].rearrange("p g n -> p (g n)")
                both, before = slice(0, 2 * P), slice(2 * P, 4 * P)
                ins = products(o, v_hi[:, j, :], v_lo[:, j, :], p_hi[:, n % 2, both], p_lo[:, n % 2, both], True, j == 0)
                if j > 0:
                    ins = products(o, va_hi[0:HD, j, :], va_lo[0:HD, j, :], p_hi[0:HD, n % 2, before],
                                   p_lo[0:HD, n % 2, before], False, True)
                if j % 2:
                    ins.then_inc(o_ready, 1)

            q_chunk(0, range(0, 3))
            sum_input("kv")
            q_chunk(0, range(3, 8))
            spread("kv")
            q_chunk(1, range(DC))
            turn_v()
            q_chunk(2, range(DC))
            pe.wait_ge(v_ready, 1)
            for m in STEPS:
                for j in range(TC):
                    if 0 <= TC * m + j - 4 < TC * PAIRS_H:
                        turn(TC * m + j - 4)
                    if m + 1 < PAIRS_H:
                        scores(m + 1, j)
                    if 3 <= m + 3 < PAIRS_H:
                        q_chunk(m + 3, Q_PARTS[j])
                    if 0 <= TC * m + j - 5 < TC * PAIRS_H:
                        values(TC * m + j - 5)

            pe.wait_ge(olo_ready, 2 * PAIRS_H)

            def w_o(m, s):
                tile_ready(T_O + m)
                pe.wait_ge(mix_free, DC * OUTS["mix1"] + m + 1)
                for k in range(DC):
                    ins = tile(banks[4 + s % 2][:, :], s, k, k, k == 0, k == DC - 1, o_hi, o_lo)
                ins.then_inc(tiles_done, 1)

            with pe.Fori(0, 2) as i:
                for s in range(4):
                    w_o(4 * i + s, s)
            ffn(1)

            sum_block("post_ffn1", "ffn1")
            for k in range(DC):
                pe.wait_ge(h_ready, DC * RES["out"] + k + 1)
                if k >= 2:
                    pe.wait_ge(otok_ready, k - 1)
                for c in range(TC):
                    ins = nc.tensor.transpose(banks[4 + k % 2][:, c * P:(c + 1) * P], h[:, k, c * P:(c + 1) * P],
                                              ident[:, :])
                ins.then_inc(ot_ready, 1)


_INS = ["x", "a_w_in", "a_conv_w", "a_conv_b", "a_w_rg", "a_b_rg", "a_w_ig", "a_b_ig", "a_lam", "a_w_out", "kv_norm",
        "w_kv", "b_w_q", "b_sinks", "b_w_o", "ffn_w_gu", "ffn_w_down", "mix_pre", "mix_post", "ffn_pre", "ffn_post"]


def kernel(**inputs):
    import numpy as np
    import concourse.bacc as bacc
    from concourse.bass_utils import run_bass_kernel_spmd

    nc = bacc.Bacc("TRN2", target_bir_lowering=False, num_devices=1)
    arrays, args = {}, []
    for name in _INS:
        a = np.ascontiguousarray(inputs[name])
        arrays[f"in_{name}"] = a
        args.append(nc.dram_tensor(f"in_{name}", a.shape, mybir.dt.from_np(a.dtype), kind="ExternalInput").ap())
    args.append(nc.dram_tensor("result", (1, S, D), F32, kind="ExternalOutput").ap())
    trunk(nc, *args)
    r = run_bass_kernel_spmd(nc, [arrays], core_ids=[0])
    return r.results[0]["result"]
```
